# Optimizing a Trainium2 kernel written in Bass

```python
import jax, jax.numpy as jnp
from jax import lax
import numpy as np
import math

D_MODEL = 1024
BATCH = 1
SEQ = 512
DEPTH = 2

HEAD_DIM = 64
MLA_HEADS = 6
MLA_NOPE = 64
MLA_ROPE = 32
MLA_V = 64
MLA_Q_LORA = 256
MLA_KV_LORA = 128
NSA_HEADS = 6
NSA_KV_HEADS = 2
NSA_GROUP = NSA_HEADS // NSA_KV_HEADS
NSA_BRANCHES = 3
CMP_LEN = 32
CMP_STRIDE = 16
CMP_HIDDEN = 128
SEL_LEN = 64
SEL_TOPK = 16
WINDOW = 512
SB_HEADS = 4
D_MIX = MLA_HEADS * MLA_V + NSA_HEADS * HEAD_DIM + SB_HEADS * HEAD_DIM
D_FF = 2816
ROPE_THETA = 500000.0
PARTIAL_ROT = HEAD_DIM // 4
Q_BLOCK = 128
EPS = 1e-6
NEG_INF = -1e30
FORCE_SCORE = 1e4
NSA_KV_W = NSA_KV_HEADS * HEAD_DIM
IN_WIDTHS = (MLA_Q_LORA, MLA_KV_LORA, MLA_ROPE,
             NSA_HEADS * HEAD_DIM,
             NSA_KV_W, NSA_KV_W, NSA_KV_W, NSA_KV_W, NSA_KV_W, NSA_KV_W,
             NSA_HEADS * NSA_BRANCHES,
             SB_HEADS * HEAD_DIM, SB_HEADS * HEAD_DIM, SB_HEADS * HEAD_DIM)
D_IN = sum(IN_WIDTHS)


def rmsnorm(x, g):
    xf = x.astype(jnp.float32)
    y = xf * lax.rsqrt(jnp.mean(xf * xf, axis=-1, keepdims=True) + EPS)
    return (y * g.astype(jnp.float32)).astype(x.dtype)

def rope(x, pos, rot_dim):
    half = rot_dim // 2
    inv_freq = ROPE_THETA ** (-jnp.arange(half, dtype=jnp.float32) / half)
    ang = pos.astype(jnp.float32)[:, None] * inv_freq[None, :]
    cos = jnp.cos(ang)[:, None, :]
    sin = jnp.sin(ang)[:, None, :]
    xr = x[..., :rot_dim].astype(jnp.float32)
    x1, x2 = xr[..., :half], xr[..., half:]
    rot = jnp.concatenate([x1 * cos - x2 * sin, x2 * cos + x1 * sin], axis=-1)
    return jnp.concatenate([rot.astype(x.dtype), x[..., rot_dim:]], axis=-1)

def masked_softmax(s, mask):
    return jax.nn.softmax(jnp.where(mask, s.astype(jnp.float32), NEG_INF), axis=-1)

def swiglu(h, w_gate, w_up, w_down):
    return (jax.nn.silu(h @ w_gate) * (h @ w_up)) @ w_down

def split_heads(t, n_heads):
    b, s, _ = t.shape
    return t.reshape(b, s, n_heads, -1)

def sweep_query_blocks(block_fn, n_blocks):
    out = lax.map(block_fn, jnp.arange(n_blocks, dtype=jnp.int32))
    nb, b, q, h, d = out.shape
    return out.transpose(1, 0, 2, 3, 4).reshape(b, nb * q, h, d)

def mla_attention(c_q, c_kv, k_rope, q_norm, w_uq, kv_norm, w_ukv, pos):
    b, s, _ = c_q.shape
    q = (rmsnorm(c_q, q_norm) @ w_uq).reshape(b, s, MLA_HEADS, MLA_NOPE + MLA_ROPE)
    q_nope = q[..., :MLA_NOPE]
    q_pe = rope(q[..., MLA_NOPE:], pos, MLA_ROPE)
    kv = (rmsnorm(c_kv, kv_norm) @ w_ukv).reshape(b, s, MLA_HEADS, MLA_NOPE + MLA_V)
    k_nope, v = kv[..., :MLA_NOPE], kv[..., MLA_NOPE:]
    k_pe = rope(k_rope[:, :, None, :], pos, MLA_ROPE)[:, :, 0]
    scale = (MLA_NOPE + MLA_ROPE) ** -0.5

    def block(i):
        q0 = i * Q_BLOCK
        qn = lax.dynamic_slice_in_dim(q_nope, q0, Q_BLOCK, axis=1)
        qp = lax.dynamic_slice_in_dim(q_pe, q0, Q_BLOCK, axis=1)
        sc = (jnp.einsum('bqhd,bkhd->bhqk', qn, k_nope)
              + jnp.einsum('bqhr,bkr->bhqk', qp, k_pe)).astype(jnp.float32) * scale
        qpos = q0 + jnp.arange(Q_BLOCK)
        p = masked_softmax(sc, pos[None, :] <= qpos[:, None]).astype(v.dtype)
        return jnp.einsum('bhqk,bkhd->bqhd', p, v)

    return sweep_query_blocks(block, s // Q_BLOCK)

def compress_blocks(x, pos_emb, w1, w2):
    b, s, g, d = x.shape
    chunks = x.reshape(b, s // CMP_STRIDE, CMP_STRIDE, g, d)
    blocks = jnp.concatenate([chunks[:, :-1], chunks[:, 1:]], axis=2)
    blocks = blocks + pos_emb[None, None, :, None, :]
    flat = blocks.transpose(0, 1, 3, 2, 4).reshape(b, s // CMP_STRIDE - 1, g, CMP_LEN * d)
    return jax.nn.gelu(flat @ w1) @ w2

def nsa_attention(q, k_cmp, v_cmp, k_sel, v_sel, k_win, v_win, gates,
                  cmp_pos_k, cmp_w1_k, cmp_w2_k, cmp_pos_v, cmp_w1_v, cmp_w2_v, pos):
    b, s, h, d = q.shape
    q = rope(q, pos, PARTIAL_ROT)
    k_cmp = rope(k_cmp, pos, PARTIAL_ROT)
    k_sel = rope(k_sel, pos, PARTIAL_ROT)
    k_win = rope(k_win, pos, PARTIAL_ROT)
    scale = d ** -0.5
    kc = compress_blocks(k_cmp, cmp_pos_k, cmp_w1_k, cmp_w2_k)
    vc = compress_blocks(v_cmp, cmp_pos_v, cmp_w1_v, cmp_w2_v)
    n_cmp = s // CMP_STRIDE - 1
    cmp_start = jnp.arange(n_cmp) * CMP_STRIDE
    cmp_end = cmp_start + CMP_LEN - 1
    n_slc = s // SEL_LEN
    n_top = min(SEL_TOPK, n_slc)
    slc_start = jnp.arange(n_slc) * SEL_LEN
    overlap = ((cmp_start[:, None] < slc_start[None, :] + SEL_LEN)
               & (cmp_start[:, None] + CMP_LEN > slc_start[None, :])).astype(jnp.float32)
    ksb = k_sel.reshape(b, n_slc, SEL_LEN, NSA_KV_HEADS, d).transpose(0, 3, 1, 2, 4)
    vsb = v_sel.reshape(b, n_slc, SEL_LEN, NSA_KV_HEADS, d).transpose(0, 3, 1, 2, 4)
    b_ix = jnp.arange(b)[:, None, None, None]
    g_ix = jnp.arange(NSA_KV_HEADS)[None, :, None, None]
    blk = jnp.arange(n_slc)
    kw = jnp.pad(k_win, ((0, 0), (WINDOW, 0), (0, 0), (0, 0)))
    vw = jnp.pad(v_win, ((0, 0), (WINDOW, 0), (0, 0), (0, 0)))

    def block(i):
        q0 = i * Q_BLOCK
        qpos = q0 + jnp.arange(Q_BLOCK)
        qb = lax.dynamic_slice_in_dim(q, q0, Q_BLOCK, axis=1).reshape(b, Q_BLOCK, NSA_KV_HEADS, NSA_GROUP, d)
        sc = jnp.einsum('bqgrd,bcgd->bgrqc', qb, kc).astype(jnp.float32) * scale
        cmask = cmp_end[None, :] <= qpos[:, None]
        p_cmp = masked_softmax(sc, cmask)
        p_cmp = jnp.where(cmask.any(axis=-1)[:, None], p_cmp, 0.0)
        o_cmp = jnp.einsum('bgrqc,bcgd->bqgrd', p_cmp.astype(vc.dtype), vc)
        score = jnp.einsum('bgrqc,cn->bgqn', p_cmp, overlap)
        cur = qpos // SEL_LEN
        forced = (blk[None, :] == 0) | (blk[None, :] == cur[:, None]) | (blk[None, :] == cur[:, None] - 1)
        future = blk[None, :] > cur[:, None]
        score = jnp.where(forced, FORCE_SCORE, jnp.where(future, -1.0, score))
        _, idx = lax.top_k(score, n_top)
        kg = ksb[b_ix, g_ix, idx]
        vg = vsb[b_ix, g_ix, idx]
        tok = idx[..., None] * SEL_LEN + jnp.arange(SEL_LEN)
        smask = (tok <= qpos[None, None, :, None, None])[:, :, None]
        ss = jnp.einsum('bqgrd,bgqnld->bgrqnl', qb, kg).astype(jnp.float32) * scale
        ss = jnp.where(smask, ss, NEG_INF).reshape(b, NSA_KV_HEADS, NSA_GROUP, Q_BLOCK, n_top * SEL_LEN)
        p_sel = jax.nn.softmax(ss, axis=-1).astype(vg.dtype).reshape(b, NSA_KV_HEADS, NSA_GROUP, Q_BLOCK, n_top, SEL_LEN)
        o_sel = jnp.einsum('bgrqnl,bgqnld->bqgrd', p_sel, vg)
        kwb = lax.dynamic_slice_in_dim(kw, q0, WINDOW + Q_BLOCK, axis=1)
        vwb = lax.dynamic_slice_in_dim(vw, q0, WINDOW + Q_BLOCK, axis=1)
        wpos = q0 - WINDOW + jnp.arange(WINDOW + Q_BLOCK)
        wmask = ((wpos[None, :] <= qpos[:, None]) & (wpos[None, :] > qpos[:, None] - WINDOW)
                 & (wpos[None, :] >= 0))
        sw = jnp.einsum('bqgrd,bkgd->bgrqk', qb, kwb).astype(jnp.float32) * scale
        p_win = masked_softmax(sw, wmask).astype(vwb.dtype)
        o_win = jnp.einsum('bgrqk,bkgd->bqgrd', p_win, vwb)
        g = lax.dynamic_slice_in_dim(gates, q0, Q_BLOCK, axis=1).reshape(b, Q_BLOCK, NSA_KV_HEADS, NSA_GROUP, NSA_BRANCHES)
        o = g[..., 0:1] * o_cmp + g[..., 1:2] * o_sel + g[..., 2:3] * o_win
        return o.reshape(b, Q_BLOCK, h, d)

    return sweep_query_blocks(block, s // Q_BLOCK)

def stick_breaking_attention(q, k, v):
    b, s, h, d = q.shape
    scale = d ** -0.5
    kpos = jnp.arange(s)

    def block(i):
        q0 = i * Q_BLOCK
        qpos = q0 + jnp.arange(Q_BLOCK)
        qb = lax.dynamic_slice_in_dim(q, q0, Q_BLOCK, axis=1)
        z = jnp.einsum('bqhd,bkhd->bhqk', qb, k).astype(jnp.float32) * scale
        strict = kpos[None, :] < qpos[:, None]
        log_beta = jax.nn.log_sigmoid(z)
        log_rem = jnp.where(strict, jax.nn.log_sigmoid(-z), 0.0)
        suffix = lax.cumsum(log_rem, axis=3, reverse=True) - log_rem
        a = jnp.where(strict, jnp.exp(log_beta + suffix), 0.0).astype(v.dtype)
        return jnp.einsum('bhqk,bkhd->bqhd', a, v)

    return sweep_query_blocks(block, s // Q_BLOCK)

def first_inputs(seed: int = 0) -> dict:
    key = jax.random.key(seed)
    ks = iter(jax.random.split(key, 32))
    f32 = jnp.float32
    L = DEPTH

    def nrm(shape, fan_in):
        return jax.random.normal(next(ks), shape, f32) * (fan_in ** -0.5)

    def gain(shape):
        return 1.0 + 0.02 * jax.random.normal(next(ks), shape, f32)

    return {
        'x': jax.random.normal(next(ks), (BATCH, SEQ, D_MODEL), f32),
        'ffn1_norm': gain((L, D_MODEL)),
        'ffn1_w_gate': nrm((L, D_MODEL, D_FF), D_MODEL),
        'ffn1_w_up': nrm((L, D_MODEL, D_FF), D_MODEL),
        'ffn1_w_down': nrm((L, D_FF, D_MODEL), D_FF),
        'mix_norm': gain((L, D_MODEL)),
        'w_in': nrm((L, D_MODEL, D_IN), D_MODEL),
        'mla_q_norm': gain((L, MLA_Q_LORA)),
        'mla_w_uq': nrm((L, MLA_Q_LORA, MLA_HEADS * (MLA_NOPE + MLA_ROPE)), MLA_Q_LORA),
        'mla_kv_norm': gain((L, MLA_KV_LORA)),
        'mla_w_ukv': nrm((L, MLA_KV_LORA, MLA_HEADS * (MLA_NOPE + MLA_V)), MLA_KV_LORA),
        'nsa_gate_bias': 0.1 * jax.random.normal(next(ks), (L, NSA_HEADS * NSA_BRANCHES), f32),
        'nsa_cmp_pos_k': 0.1 * jax.random.normal(next(ks), (L, CMP_LEN, HEAD_DIM), f32),
        'nsa_cmp_w1_k': nrm((L, CMP_LEN * HEAD_DIM, CMP_HIDDEN), CMP_LEN * HEAD_DIM),
        'nsa_cmp_w2_k': nrm((L, CMP_HIDDEN, HEAD_DIM), CMP_HIDDEN),
        'nsa_cmp_pos_v': 0.1 * jax.random.normal(next(ks), (L, CMP_LEN, HEAD_DIM), f32),
        'nsa_cmp_w1_v': nrm((L, CMP_LEN * HEAD_DIM, CMP_HIDDEN), CMP_LEN * HEAD_DIM),
        'nsa_cmp_w2_v': nrm((L, CMP_HIDDEN, HEAD_DIM), CMP_HIDDEN),
        'w_out': nrm((L, D_MIX, D_MODEL), D_MIX),
        'ffn2_norm': gain((L, D_MODEL)),
        'ffn2_w_gate': nrm((L, D_MODEL, D_FF), D_MODEL),
        'ffn2_w_up': nrm((L, D_MODEL, D_FF), D_MODEL),
        'ffn2_w_down': nrm((L, D_FF, D_MODEL), D_FF),
        'final_norm': gain((D_MODEL,)),
    }

def first_block(x, ffn1_norm, ffn1_w_gate, ffn1_w_up, ffn1_w_down, mix_norm, w_in,
              mla_q_norm, mla_w_uq, mla_kv_norm, mla_w_ukv,
              nsa_gate_bias, nsa_cmp_pos_k, nsa_cmp_w1_k, nsa_cmp_w2_k,
              nsa_cmp_pos_v, nsa_cmp_w1_v, nsa_cmp_w2_v, w_out,
              ffn2_norm, ffn2_w_gate, ffn2_w_up, ffn2_w_down, final_norm):
    b, s, _ = x.shape
    pos = jnp.arange(s, dtype=jnp.int32)
    split_at = [int(c) for c in np.cumsum(IN_WIDTHS)[:-1]]
    for l in range(DEPTH):
        x = x + 0.5 * swiglu(rmsnorm(x, ffn1_norm[l]), ffn1_w_gate[l], ffn1_w_up[l], ffn1_w_down[l])
        h = rmsnorm(x, mix_norm[l])
        (c_q, c_kv, k_rope, n_q, n_kc, n_vc, n_ks, n_vs, n_kw, n_vw, n_gate,
         sb_q, sb_k, sb_v) = jnp.split(h @ w_in[l], split_at, axis=-1)
        o_mla = mla_attention(c_q, c_kv, k_rope, mla_q_norm[l], mla_w_uq[l],
                              mla_kv_norm[l], mla_w_ukv[l], pos)
        gates = jax.nn.sigmoid(n_gate + nsa_gate_bias[l]).reshape(b, s, NSA_HEADS, NSA_BRANCHES)
        o_nsa = nsa_attention(split_heads(n_q, NSA_HEADS),
                              split_heads(n_kc, NSA_KV_HEADS), split_heads(n_vc, NSA_KV_HEADS),
                              split_heads(n_ks, NSA_KV_HEADS), split_heads(n_vs, NSA_KV_HEADS),
                              split_heads(n_kw, NSA_KV_HEADS), split_heads(n_vw, NSA_KV_HEADS),
                              gates, nsa_cmp_pos_k[l], nsa_cmp_w1_k[l], nsa_cmp_w2_k[l],
                              nsa_cmp_pos_v[l], nsa_cmp_w1_v[l], nsa_cmp_w2_v[l], pos)
        o_sb = stick_breaking_attention(split_heads(sb_q, SB_HEADS), split_heads(sb_k, SB_HEADS),
                                        split_heads(sb_v, SB_HEADS))
        o = jnp.concatenate([o_mla.reshape(b, s, -1), o_nsa.reshape(b, s, -1),
                             o_sb.reshape(b, s, -1)], axis=-1)
        x = x + o @ w_out[l]
        x = x + 0.5 * swiglu(rmsnorm(x, ffn2_norm[l]), ffn2_w_gate[l], ffn2_w_up[l], ffn2_w_down[l])
    return rmsnorm(x, final_norm)


DEPTH_2 = 1

CHUNK = 128
GM_GROUPS = 8
GM_GROUP_DIM = 64
GM_WIDTH = GM_GROUPS * GM_GROUP_DIM
WINDOW_2 = 128
Q_HEADS = 8
KV_HEADS = 2
Q_PER_KV = Q_HEADS // KV_HEADS
ATTN_WIDTH = Q_HEADS * HEAD_DIM
KV_WIDTH = KV_HEADS * HEAD_DIM
REL_BUCKETS = 32
REL_MAX_EXACT = REL_BUCKETS // 2
REL_MAX_DIST = 128
N_GROUPS_MOE = 4
EXPERTS_PER_GROUP = 4
N_EXPERTS = N_GROUPS_MOE * EXPERTS_PER_GROUP
TOP_K = 2
EXPERT_FF = 512
MASK_VALUE = -1e30

SPLIT_SIZES = (GM_WIDTH, GM_WIDTH, ATTN_WIDTH, KV_WIDTH, KV_WIDTH, D_MODEL, D_MODEL)
SPLIT_POINTS = tuple(int(v) for v in np.cumsum(SPLIT_SIZES)[:-1])
IN_WIDTH = int(sum(SPLIT_SIZES))


def rms_norm(x, g):
    xf = x.astype(jnp.float32)
    y = xf * lax.rsqrt(jnp.mean(xf * xf, axis=-1, keepdims=True) + EPS)
    return (y * g.astype(jnp.float32)).astype(x.dtype)

def layer_norm(x, g):
    xf = x.astype(jnp.float32)
    mu = jnp.mean(xf, axis=-1, keepdims=True)
    xc = xf - mu
    y = xc * lax.rsqrt(jnp.mean(xc * xc, axis=-1, keepdims=True) + EPS)
    return (y * g.astype(jnp.float32)).astype(x.dtype)

def t5_causal_bucket(dist):
    is_small = dist < REL_MAX_EXACT
    nf = jnp.maximum(dist, 1).astype(jnp.float32)
    large = REL_MAX_EXACT + (
        jnp.log(nf / REL_MAX_EXACT) / math.log(REL_MAX_DIST / REL_MAX_EXACT)
        * (REL_BUCKETS - REL_MAX_EXACT)).astype(jnp.int32)
    large = jnp.minimum(large, REL_BUCKETS - 1)
    return jnp.where(is_small, dist, large)

def gmlp_chunk_mixer(u_raw, v_raw, v_norm_g, w_s, b_s):
    B, S, _ = u_raw.shape
    u = jax.nn.gelu(u_raw)
    v = layer_norm(jax.nn.gelu(v_raw), v_norm_g)
    v = v.reshape(B, S // CHUNK, CHUNK, GM_GROUPS, GM_GROUP_DIM)
    causal = jnp.tril(jnp.ones((CHUNK, CHUNK), dtype=bool))
    ws = jnp.where(causal[None], w_s, jnp.zeros((), w_s.dtype)).astype(v.dtype)
    sv = jnp.einsum("gts,bcsgd->bctgd", ws, v)
    sv = sv + b_s.T.astype(v.dtype)[None, None, :, :, None]
    return u * sv.reshape(B, S, GM_WIDTH)

def swa_sink_attention(q, k, v, sinks, rel_bias):
    B, S, _ = q.shape
    nb = S // WINDOW_2
    q = q.reshape(B, nb, WINDOW_2, KV_HEADS, Q_PER_KV, HEAD_DIM)
    k = k.reshape(B, nb, WINDOW_2, KV_HEADS, HEAD_DIM)
    v = v.reshape(B, nb, WINDOW_2, KV_HEADS, HEAD_DIM)
    k_prev = jnp.concatenate([jnp.zeros_like(k[:, :1]), k[:, :-1]], axis=1)
    v_prev = jnp.concatenate([jnp.zeros_like(v[:, :1]), v[:, :-1]], axis=1)
    kb = jnp.concatenate([k_prev, k], axis=2)
    vb = jnp.concatenate([v_prev, v], axis=2)

    scores = jnp.einsum("bnqkgd,bnskd->bnkgqs", q, kb,
                        preferred_element_type=jnp.float32) * (HEAD_DIM ** -0.5)

    qi = jnp.arange(WINDOW_2, dtype=jnp.int32)[:, None]
    sj = jnp.arange(2 * WINDOW_2, dtype=jnp.int32)[None, :]
    dist = qi + WINDOW_2 - sj
    in_window = (dist >= 0) & (dist < WINDOW_2)
    bucket = t5_causal_bucket(jnp.clip(dist, 0, WINDOW_2 - 1))
    bias = rel_bias.astype(jnp.float32)[bucket]
    bias = bias.transpose(2, 0, 1).reshape(KV_HEADS, Q_PER_KV, WINDOW_2, 2 * WINDOW_2)
    blk = jnp.arange(nb, dtype=jnp.int32)[:, None, None]
    valid = in_window[None] & ((blk > 0) | (sj[None] >= WINDOW_2))

    scores = scores + bias[None, None]
    scores = jnp.where(valid[None, :, None, None], scores, MASK_VALUE)
    sink = sinks.astype(jnp.float32).reshape(KV_HEADS, Q_PER_KV)[None, None, :, :, None, None]
    m = jnp.maximum(jnp.max(scores, axis=-1, keepdims=True), sink)
    p = jnp.exp(scores - m)
    denom = jnp.sum(p, axis=-1, keepdims=True) + jnp.exp(sink - m)
    probs = (p / denom).astype(vb.dtype)
    out = jnp.einsum("bnkgqs,bnskd->bnqkgd", probs, vb)
    return out.reshape(B, S, ATTN_WIDTH)

def hierarchical_moe(h, rg_w, rg_b, re_w, re_b, w_gate, w_up, w_down):
    B, S, D = h.shape
    t = h.reshape(-1, D)
    g_logits = jnp.dot(t, rg_w, preferred_element_type=jnp.float32) + rg_b.astype(jnp.float32)
    g_probs = jax.nn.softmax(g_logits, axis=-1)
    g_top_p, g_top_i = lax.top_k(g_probs, 1)
    e_all = jnp.einsum("td,gde->tge", t, re_w,
                       preferred_element_type=jnp.float32) + re_b.astype(jnp.float32)
    e_logits = jnp.take_along_axis(e_all, g_top_i[:, :, None], axis=1)[:, 0]
    e_top_v, e_top_i = lax.top_k(e_logits, TOP_K)
    w_top = jax.nn.softmax(e_top_v, axis=-1) * g_top_p
    expert_id = g_top_i * EXPERTS_PER_GROUP + e_top_i
    combine = jnp.einsum("tk,tke->te", w_top,
                         jax.nn.one_hot(expert_id, N_EXPERTS, dtype=jnp.float32))
    combine = combine.astype(t.dtype)
    out = jnp.zeros_like(t)
    for e in range(N_EXPERTS):
        hid = jax.nn.silu(t @ w_gate[e]) * (t @ w_up[e])
        out = out + combine[:, e:e + 1] * (hid @ w_down[e])
    return out.reshape(B, S, D)

def second_inputs(seed: int = 0) -> dict:
    key = jax.random.key(seed)
    ks = jax.random.split(key, 20)
    f32 = jnp.float32
    nrm = lambda k, shape, scale: jax.random.normal(k, shape, f32) * scale
    L = DEPTH_2
    return {
        "x": jax.random.normal(ks[0], (BATCH, SEQ, D_MODEL), f32),
        "attn_norm_g": 1.0 + nrm(ks[1], (L, D_MODEL), 0.02),
        "w_in": nrm(ks[2], (L, D_MODEL, IN_WIDTH), D_MODEL ** -0.5),
        "gm_v_norm_g": 1.0 + nrm(ks[3], (L, GM_WIDTH), 0.02),
        "gm_w_spatial": nrm(ks[4], (L, GM_GROUPS, CHUNK, CHUNK), CHUNK ** -0.5),
        "gm_b_spatial": 1.0 + nrm(ks[5], (L, GM_GROUPS, CHUNK), 0.02),
        "attn_sinks": nrm(ks[6], (L, Q_HEADS), 0.5),
        "rel_bias": nrm(ks[7], (REL_BUCKETS, Q_HEADS), 0.5),
        "w_proj_a": nrm(ks[8], (L, GM_WIDTH, D_MODEL), GM_WIDTH ** -0.5),
        "w_proj_b": nrm(ks[9], (L, ATTN_WIDTH, D_MODEL), ATTN_WIDTH ** -0.5),
        "w_out": nrm(ks[10], (L, D_MODEL, D_MODEL), D_MODEL ** -0.5),
        "ffn_norm_g": 1.0 + nrm(ks[11], (L, D_MODEL), 0.02),
        "router_group_w": nrm(ks[12], (L, D_MODEL, N_GROUPS_MOE), D_MODEL ** -0.5),
        "router_group_b": nrm(ks[13], (L, N_GROUPS_MOE), 0.01),
        "router_expert_w": nrm(ks[14], (L, N_GROUPS_MOE, D_MODEL, EXPERTS_PER_GROUP), D_MODEL ** -0.5),
        "router_expert_b": nrm(ks[15], (L, N_GROUPS_MOE, EXPERTS_PER_GROUP), 0.01),
        "expert_w_gate": nrm(ks[16], (L, N_EXPERTS, D_MODEL, EXPERT_FF), D_MODEL ** -0.5),
        "expert_w_up": nrm(ks[17], (L, N_EXPERTS, D_MODEL, EXPERT_FF), D_MODEL ** -0.5),
        "expert_w_down": nrm(ks[18], (L, N_EXPERTS, EXPERT_FF, D_MODEL), EXPERT_FF ** -0.5),
        "final_norm_g": 1.0 + nrm(ks[19], (D_MODEL,), 0.02),
    }

def second_block(x, attn_norm_g, w_in, gm_v_norm_g, gm_w_spatial, gm_b_spatial, attn_sinks,
              rel_bias, w_proj_a, w_proj_b, w_out, ffn_norm_g, router_group_w, router_group_b,
              router_expert_w, router_expert_b, expert_w_gate, expert_w_up, expert_w_down,
              final_norm_g):
    h = x
    for l in range(DEPTH_2):
        hn = rms_norm(h, attn_norm_g[l])
        proj = hn @ w_in[l]
        u_raw, v_raw, q, k, v, gate_a, gate_b = jnp.split(proj, SPLIT_POINTS, axis=-1)
        a = gmlp_chunk_mixer(u_raw, v_raw, gm_v_norm_g[l], gm_w_spatial[l], gm_b_spatial[l])
        b = swa_sink_attention(q, k, v, attn_sinks[l], rel_bias)
        merged = (jax.nn.sigmoid(gate_a) * (a @ w_proj_a[l])
                  + jax.nn.sigmoid(gate_b) * (b @ w_proj_b[l]))
        h = h + merged @ w_out[l]
        hn = rms_norm(h, ffn_norm_g[l])
        h = h + hierarchical_moe(hn, router_group_w[l], router_group_b[l], router_expert_w[l],
                                 router_expert_b[l], expert_w_gate[l], expert_w_up[l],
                                 expert_w_down[l])
    return rms_norm(h, final_norm_g)


def setup_inputs(seed=0):
    out = dict(first_inputs(seed))
    for name, value in second_inputs(seed + 1).items():
        if name != "x":
            out[name + "_2"] = value
    return out


def reference(
    x, ffn1_norm, ffn1_w_gate, ffn1_w_up, ffn1_w_down, mix_norm, w_in, mla_q_norm, mla_w_uq,
    mla_kv_norm, mla_w_ukv, nsa_gate_bias, nsa_cmp_pos_k, nsa_cmp_w1_k, nsa_cmp_w2_k,
    nsa_cmp_pos_v, nsa_cmp_w1_v, nsa_cmp_w2_v, w_out, ffn2_norm, ffn2_w_gate, ffn2_w_up,
    ffn2_w_down, final_norm, attn_norm_g_2, w_in_2, gm_v_norm_g_2, gm_w_spatial_2,
    gm_b_spatial_2, attn_sinks_2, rel_bias_2, w_proj_a_2, w_proj_b_2, w_out_2, ffn_norm_g_2,
    router_group_w_2, router_group_b_2, router_expert_w_2, router_expert_b_2, expert_w_gate_2,
    expert_w_up_2, expert_w_down_2, final_norm_g_2,
):
    x = first_block(
        x, ffn1_norm, ffn1_w_gate, ffn1_w_up, ffn1_w_down, mix_norm, w_in, mla_q_norm, mla_w_uq,
        mla_kv_norm, mla_w_ukv, nsa_gate_bias, nsa_cmp_pos_k, nsa_cmp_w1_k, nsa_cmp_w2_k,
        nsa_cmp_pos_v, nsa_cmp_w1_v, nsa_cmp_w2_v, w_out, ffn2_norm, ffn2_w_gate, ffn2_w_up,
        ffn2_w_down, final_norm,
    )
    return second_block(
        x, attn_norm_g_2, w_in_2, gm_v_norm_g_2, gm_w_spatial_2, gm_b_spatial_2, attn_sinks_2,
        rel_bias_2, w_proj_a_2, w_proj_b_2, w_out_2, ffn_norm_g_2, router_group_w_2,
        router_group_b_2, router_expert_w_2, router_expert_b_2, expert_w_gate_2, expert_w_up_2,
        expert_w_down_2, final_norm_g_2,
    )


_drawn_inputs = setup_inputs


def setup_inputs(seed=0):
    import zlib

    import numpy as np

    out = dict(_drawn_inputs(seed))
    spreads = {}
    factors = {'mla_q_norm': 5.514,
     'mla_kv_norm': 4.479,
     'nsa_gate_bias': 4.326,
     'nsa_cmp_pos_k': 8.0,
     'ffn2_norm': 2.926,
     'attn_norm_g_2': 3.288,
     'gm_v_norm_g_2': 6.896,
     'gm_b_spatial_2': 6.128,
     'attn_sinks_2': 61.112,
     'ffn_norm_g_2': 2.679,
     'router_group_b_2': 3.308,
     'router_expert_b_2': 32.913}
    for name, (base, spread) in spreads.items():
        noise = np.random.default_rng([zlib.crc32(name.encode()), seed]).standard_normal(out[name].shape)
        drawn = base * np.exp(spread * noise) if base else spread * noise
        out[name] = __import__('jax').numpy.asarray(drawn.astype(out[name].dtype))
    for name, factor in factors.items():
        out[name] = (out[name] * factor).astype(out[name].dtype)
    return out
```

```python
from contextlib import ExitStack

import numpy as np

import concourse.bass as bass
from concourse import mybir

ALU = mybir.AluOpType
ACT = mybir.ActivationFunctionType
AX = mybir.AxisListType
F32 = mybir.dt.float32

P = 128
S = 512
D = 1024
KC = D // P
TB = S // P
EPS = 1e-6
NEG = -1e30
DEPTH = 2
D_FF = 2816
FS = 256
GC = 0.7978845608028654
HD = 64

C_CQ, C_CKV, C_KR, C_NQ, C_KC, C_VC, C_KS, C_VS, C_KW, C_VW, C_G, C_SQ, C_SK, C_SV, C_END = (
    int(v) for v in np.cumsum([0, 256, 128, 32, 384, 128, 128, 128, 128, 128, 128, 18, 256, 256, 256]))

_CONST = {}
_CN = 0
for _name, _n in (("ident", 128), ("ones", 128), ("negones", 128), ("negtri", 128), ("causal", 128),
                  ("strict", 128), ("tril", 128), ("r_mla", 96), ("r_nsa", 128), ("cos_mla", 512),
                  ("sin_mla", 512), ("cos_nsa", 512), ("sin_nsa", 512), ("cmp_mask", 4 * 31),
                  ("cmp_valid", 4), ("desc4", 4), ("desc16", 16), ("group_rows", 4 * 128),
                  ("bucket_rows", 384), ("window_row", 384)):
    _CONST[_name] = (_CN, _CN + _n)
    _CN += _n


def constant_table():
    t = np.zeros((P, _CN), np.float32)

    def put(name, a):
        a = np.asarray(a, np.float32)
        t[:a.shape[0], _CONST[name][0]:_CONST[name][0] + a.shape[1]] = a

    r = np.arange(P)
    put("ident", np.eye(P))
    put("ones", np.ones((P, P)))
    put("negones", -np.ones((P, P)))
    put("negtri", -1.0 * (r[:, None] >= r[None, :]))
    put("causal", np.where(r[None, :] <= r[:, None], 0.0, NEG))
    put("strict", r[:, None] < r[None, :])
    put("tril", r[:, None] <= r[None, :])
    pos = np.arange(S, dtype=np.float32)

    def rope(rows, start, half):
        freq = np.float32(500000.0) ** (-np.arange(half, dtype=np.float32) / np.float32(half))
        ang = (pos[:, None] * freq[None, :].astype(np.float32)).astype(np.float32).T
        rot = np.zeros((rows, rows), np.float32)
        c, s = np.ones((rows, S), np.float32), np.zeros((rows, S), np.float32)
        for b in start:
            for i in range(half):
                rot[b + half + i, b + i] = -1.0
                rot[b + i, b + half + i] = 1.0
            c[b:b + 2 * half] = np.concatenate([np.cos(ang), np.cos(ang)])
            s[b:b + 2 * half] = np.concatenate([np.sin(ang), np.sin(ang)])
        return rot, c, s

    for name, args in (("mla", (96, (64,), 16)), ("nsa", (128, (0, 64), 8))):
        rot, c, s = rope(*args)
        put("r_" + name, rot)
        put("cos_" + name, c)
        put("sin_" + name, s)
    q = (np.arange(TB)[None, :, None] * P + r[:, None, None])
    put("cmp_mask", np.where(np.arange(31)[None, None, :] * 16 + 31 <= q, 0.0, NEG).reshape(P, -1))
    put("cmp_valid", (q[:, :, 0] >= 31))
    put("desc4", np.tile(4.0 - np.arange(4), (P, 1)))
    put("desc16", np.tile(16.0 - np.arange(16), (P, 1)))
    g = np.zeros((8, 4, 128), np.float32)
    for i in range(8):
        g[i, i // 2, (i % 2) * 64:(i % 2) * 64 + 64] = 1.0
    put("group_rows", g.reshape(8, -1))
    dist = 255 - np.arange(384)
    ok = (dist >= 0) & (dist < 128)
    nf = np.maximum(dist, 1).astype(np.float32)
    large = 16 + (np.log(nf / np.float32(16)) / np.float32(np.log(8.0)) * np.float32(16)).astype(np.int32)
    bucket = np.where(dist < 16, dist, np.minimum(large, 31))
    rows = np.zeros((32, 384), np.float32)
    for j in range(384):
        if ok[j]:
            rows[bucket[j], j] = 1.0
    put("bucket_rows", rows)
    put("window_row", np.tile(np.where(ok, 0.0, NEG), (8, 1)))
    return t


MIX = (
    [("cq", 0, 0, "act"), ("cq", 1, 0, "act"), ("ckv", 0, 1, "act"), ("kr", 0, 1, "act")]
    + [("nq", 0, 2, "act"), ("nq", 1, 2, "act"), ("nq", 2, 3, "act"), ("kc", 0, 3, "act")]
    + [("vc", 0, 4, "act"), ("ks", 0, 4, "act"), ("vs", 0, 5, "act"), ("kw", 0, 5, "act")]
    + [("vw", 0, 6, "act"), ("gate", 0, 6, "dve")]
    + [("sq", 0, 7, "act"), ("sq", 1, 7, "act"), ("sk", 0, 8, "act"), ("sk", 1, 8, "act")]
    + [("sv", 0, 9, "act"), ("sv", 1, 9, "act")]
    + [("uq", h, 10, "act") for h in range(6)]
    + [("kn", h, 11, "act") for h in range(6)]
    + [("mv", b, 11, "act") for b in range(TB)]
    + [("rope", i, None, "dve") for i in range(13)]
    + [("hid_k", 0, 13, "dve"), ("hid_v", 0, 15, "dve"), ("cmp", 0, None, "act")]
)
TICKET = {(j[0], j[1]): i for i, j in enumerate(MIX)}
HEADS = [("mla", h) for h in range(6)] + [("nsa", h) for h in range(6)]
SB_HEADS = 4
T_LIN = len(MIX)
T_HEAD = T_LIN + len(HEADS) + SB_HEADS
T_MIX = T_HEAD + KC
NSL = D_FF // FS
T_FF = NSL * KC
TL = 2 * T_FF + T_MIX
assert T_MIX % 2 == 0 and T_FF % 2 == 0
NHD = len(HEADS)
TLF = TL - NHD
LAST_TICKET = {}
for _i, _j in enumerate(MIX):
    if _j[2] is not None:
        LAST_TICKET[_j[2]] = _i
LAST_TICKET[12], LAST_TICKET[14] = LAST_TICKET[13], LAST_TICKET[15]

MIX_DMAS = [1, 1, 4, 3, 1, 1, 1, 1, 1, 1, 1, 1, 2, 2, 2, 2, 1, 1, 1, 1]
W_OUT0 = 16
NLM = len(MIX_DMAS)
SLOT_DMAS = [2 * NSL + sum(MIX_DMAS[s::3]) for s in range(3)]

UNITS = []
for _kind, _h in HEADS:
    for _i in range(TB):
        br = ["mla"] if _kind == "mla" else ["cmp", "sel", "win"]
        for _b in br:
            UNITS.append((_kind, _h, _i, _b, _b == br[0], _b == br[-1]))
NU = len(UNITS)
NSA_HALF = lambda h: (h // 3, h % 3)

SWA_UNITS = [(h, i) for h in range(8) for i in range(TB)]
NX = 16
MOE_SLICES = NX * 2


def run_slices(eng, n, up_step, down_step):
    up_step(0, 0)
    with eng.Fori(0, (n - 1) // 2) as i:
        up_step(i * 2 + 1, 1)
        down_step(i * 2, 0, False)
        up_step(i * 2 + 2, 0)
        down_step(i * 2 + 1, 1, False)
    if n % 2 == 0:
        up_step(n - 1, 1)
        down_step(n - 2, 0, False)
    down_step(n - 1, (n - 1) % 2, True)


def build(nc, a, out):
    with ExitStack() as ctx:
        def sb(name, shape):
            return ctx.enter_context(nc.sbuf_tensor(name, shape, F32))

        def sem(name):
            return ctx.enter_context(nc.semaphore(name))

        const = sb("const", [P, _CN])

        def cst(name, rows=P, lo=0, hi=None):
            c0, c1 = _CONST[name]
            return const[0:rows, c0 + lo:(c1 if hi is None else c0 + hi)]

        ident = cst("ident")
        x_T = sb("x_T", [P, KC, S])
        h_T = sb("h_T", [P, KC, S])
        o_T = sb("o_T", [P, KC, S])
        slot = [sb(f"weights{s}", [P, 2048]) for s in range(3)]
        hid = sb("hid", [P, 4, S])
        et = sb("exp_tile", [P, 2, S])
        rt = sb("recip_tile", [P, S])
        lora = sb("lora", [P, 4, S])
        rstd = sb("rstd", [P, S])
        arena = sb("arena", [P, 18000])
        probs = sb("probs", [P, 3, S])
        probs_T = sb("probs_T", [P, 2, S])
        gains = sb("gains", [P, 3 * DEPTH + 4, KC])
        lgains = sb("lora_gains", [P, DEPTH, 3])
        gbias = sb("gate_bias", [P, DEPTH, 18])
        cmp_w2 = sb("cmp_w2", [P, 2, HD])
        cmp_pos = sb("cmp_pos", [HD, 2, 32])
        hid_cmp = sb("hid_cmp", [P, 2, 62])
        cmp_t = sb("cmp_t", [P, 4, 62])
        bias_c = sb("bias_c", [P, 2])
        stats = sb("stats", [P, 4, 4])
        gates = sb("gates", [P, TB, 18])
        gates_e = sb("gates_e", [P, TB, 18])
        vcmp = sb("vcmp", [31, 2, HD])
        kcmp_T = sb("kcmp_T", [P, 31])
        lnst = sb("lnst", [P, 4, TB])
        sinks = sb("sinks", [P, 8])
        rel = sb("rel", [32, 8])
        bs = sb("bs", [8, P])
        rw = sb("rw", [P, KC, 20])
        rb = sb("rb", [P, 20])
        lg = sb("lg", [P, TB, 20])
        rx = sb("rx", [P, 14, TB, 16])
        comb = sb("comb", [P, TB, 16])
        comb_T = sb("comb_T", [16, S])
        eps = sb("eps", [P, 1])

        off = [0]

        def view(*dims):
            n = int(np.prod(dims))
            v = arena[:, off[0]:off[0] + n]
            off[0] += n
            if len(dims) == 2:
                v = v.rearrange("p (a b) -> p a b", b=dims[1])
            return v

        q6 = view(6, S)
        k6 = view(6, S)
        mv = view(TB, 384)
        nq = view(3, S)
        nk = view(4, S)
        vs = view(TB, P)
        vw = view(TB, P)
        sq_T = view(2, S)
        sk_T = view(2, S)
        sv = view(TB, 256)
        assert off[0] <= 18000, off[0]
        off[0] = 0
        u_T = view(4, S)
        vtok = view(TB, S)
        q2 = view(4, S)
        k2 = view(S)
        v2 = view(TB, P)
        sig_a = view(KC, S)
        sig_b = o_T
        bias_t = view(8, 256)
        gv = view(S)
        ab_T = view(8, S)
        assert off[0] <= 18000, off[0]
        ws_T = lora[:, 0:2, :].rearrange("p a (b c) -> p (a b) c", c=P)
        ws_n = lora[:, 2:4, :].rearrange("p a (b c) -> p (a b) c", c=P)
        rrow = rt[0:8, 0:384]
        cb = probs_T

        acc = [ctx.enter_context(nc.psum_tensor(f"acc{i}", [P, S], F32)) for i in range(2)]
        score = [ctx.enter_context(nc.psum_tensor(f"score{i}", [P, S], F32)) for i in range(4)]
        turn = [ctx.enter_context(nc.psum_tensor(f"turn{i}", [P, S], F32)) for i in range(2)]

        rel_dram = nc.dram_tensor("rel_scratch", [8, P, 384], F32, kind="Internal").ap()
        comb_dram = nc.dram_tensor("comb_scratch", [16, S], F32, kind="Internal").ap()

        params_loaded = sem("params_loaded")
        x_loaded = sem("x_loaded")
        w_loaded = [sem(f"w_loaded{s}") for s in range(3)]
        small_loaded = sem("small_loaded")
        acc_full = sem("acc_full")
        acc_free = [sem(f"acc_free{i}") for i in range(2)]
        x_final = sem("x_final")
        squared = sem("squared")
        ssq_full = sem("ssq_full")
        rstd_ready = sem("rstd_ready")
        h_ready = sem("h_ready")
        gu_full = sem("gu_full")
        sig_ready = sem("sig_ready")
        hid_done = sem("hid_done")
        lsq_ready = sem("lsq_ready")
        lssq_full = sem("lssq_full")
        lrstd_ready = sem("lrstd_ready")
        lora_ready = sem("lora_ready")
        rope_ready = sem("rope_ready")
        gate_exp = sem("gate_exp")
        gelu_pre = sem("gelu_pre")
        gelu_exp = sem("gelu_exp")
        hidc_ready = sem("hidc_ready")
        s_full = sem("s_full")
        max_ready = sem("max_ready")
        exp_ready = sem("exp_ready")
        p_ready = sem("p_ready")
        t_full = sem("t_full")
        pt_ready = sem("pt_ready")
        pv_done = sem("pv_done")
        z_full = sem("z_full")
        log_ready = sem("log_ready")
        sp_ready = sem("sp_ready")
        suffix_full = sem("suffix_full")
        a_exp = sem("a_exp")
        a_ready = sem("a_ready")
        eps_ready = sem("eps_ready")
        rel_full = sem("rel_full")
        comb_done = sem("comb_done")
        yt_full = sem("yt_full")
        xt_full = sem("xt_full")
        turned = sem("turned")
        g2_pre = sem("g2_pre")
        g2_exp = sem("g2_exp")
        ln_pre = sem("ln_pre")
        ln_rstd = sem("ln_rstd")
        vn_ready = sem("vn_ready")
        ws_loaded = sem("ws_loaded")
        ws_ready = sem("ws_ready")
        relrow_ready = sem("relrow_ready")
        rel_stored = sem("rel_stored")
        bias_loaded = sem("bias_loaded")
        merged_ready = sem("merged_ready")
        route_pre = sem("route_pre")
        route_exp = sem("route_exp")
        comb_stored = sem("comb_stored")
        cb_loaded = [sem(f"cb_loaded{i}") for i in range(2)]
        y_ready = sem("y_ready")
        y_stored = sem("y_stored")

        def at(l, per_layer, n):
            return l * per_layer + n

        B1, BM, B2 = 0, T_FF, T_FF + T_MIX
        F1, FM, F2 = 0, T_FF, T_FF + T_MIX - NHD
        TG = 4 * NSL
        NZ = SB_HEADS * TB

        def NZ_AT(h, j):
            return h * TB + j

        def full_at(l, base, n):
            return at(l, TLF, base + n + 1)

        def mix_full(l, n):
            return full_at(l, FM, n if n <= T_LIN else n - NHD)

        def free_at(l, base, n):
            return at(l, TL // 2, base // 2 + n // 2 + 1)

        def gu_at(l, base, n):
            return at(l, TG, base + n + 1)

        def dmajor(name, p=P):
            return a[name].rearrange("l (c p) f -> l p c f", p=p)

        w_gate = [dmajor("ffn1_w_gate"), dmajor("ffn2_w_gate")]
        w_up = [dmajor("ffn1_w_up"), dmajor("ffn2_w_up")]
        w_down = [dmajor("ffn1_w_down"), dmajor("ffn2_w_down")]
        w_in, w_out = dmajor("w_in"), dmajor("w_out")
        w_uq, w_ukv = dmajor("mla_w_uq"), dmajor("mla_w_ukv")
        x_tok = a["x"].rearrange("a (b p) d -> p (a b) d", p=P)
        y_tok = out.rearrange("a (b p) d -> p (a b) d", p=P)
        x_in = arena[:, 0:4096].rearrange("p (b d) -> p b d", d=D)
        y_out = x_in
        w_in2, w_out2 = dmajor("w_in_2")[0], dmajor("w_out_2")[0]
        w_pa, w_pb = dmajor("w_proj_a_2")[0], dmajor("w_proj_b_2")[0]
        x_gate = a["expert_w_gate_2"].rearrange("a e (c p) f -> (a e) p c f", p=P)
        x_up = a["expert_w_up_2"].rearrange("a e (c p) f -> (a e) p c f", p=P)
        x_down = a["expert_w_down_2"].rearrange("a e (c p) f -> (a e) p c f", p=P)

        def s3(s, c, n):
            return slot[s][:, 0:c * n].rearrange("p (c n) -> p c n", n=n)

        SECOND = ([("u", 0), ("u", 256), ("v", 0), ("v", 256), ("q", 0), ("q", 256), ("kv", 0)]
                  + [("gate", c) for c in range(0, 2048, 256)]
                  + [("pa", 0), ("pa", 512), ("pb", 0), ("pb", 512)]
                  + [("wo", c) for c in range(0, 1024, 256)])
        SEC_DMAS = [4 if n == "q" else 1 for n, _ in SECOND]
        NSEC = len(SECOND)

        SEC_T = ([("u", c, c // 2) for c in range(4)]
                 + [("v", b, 2 + b // 2) for b in range(4)]
                 + [("q", c, 4 + c // 2) for c in range(4)] + [("k", 0, 6), ("vtok", 0, 6)]
                 + [("gate", c, 7 + c // 2) for c in range(16)]
                 + [("wst", b, None) for b in range(2)]
                 + [("sv", c, None) for c in range(4)]
                 + [("swa", h, None) for h in range(8)]
                 + [("pa", c, 15 + c // 4) for c in range(8)]
                 + [("pb", c, 17 + c // 4) for c in range(8)]
                 + [("wo", c, 19 + c // 2) for c in range(8)]
                 + [("route", 0, None), ("combt", 0, None)])
        NT2 = len(SEC_T)
        assert NT2 % 2 == 0 and NSEC % 3 == 2
        T2 = {(n, i): j for j, (n, i, _) in enumerate(SEC_T)}
        LAST2 = {ld: j for j, (_, _, ld) in enumerate(SEC_T) if ld is not None}
        SWA0 = T2["swa", 0]

        def full2(n):
            return n - max(0, min(n - SWA0, 8))

        BMOE, FMOE = NT2, NT2 - 8

        block = ctx.enter_context(nc.Block())

        @block.sync
        def _(sp):
            sp.dma_start(const[:, :], a["const"]).then_inc(params_loaded, 16)
            sp.dma_start(x_in, x_tok).then_inc(x_loaded, 16)
            with nc.allow_non_contiguous_dma(reason="small parameter vectors, once"):
                for i, name in enumerate(("ffn1_norm", "mix_norm", "ffn2_norm")):
                    for l in range(DEPTH):
                        sp.dma_start(gains[:, 3 * l + i, :],
                                     a[name][l].rearrange("(c p) -> p c", p=P)).then_inc(params_loaded, 16)
                for i, name in enumerate(("attn_norm_g_2", "ffn_norm_g_2")):
                    sp.dma_start(gains[:, 3 * DEPTH + 1 + i, :],
                                 a[name][0].rearrange("(c p) -> p c", p=P)).then_inc(params_loaded, 16)
                for i, name in ((0, "final_norm"), (3, "final_norm_g_2")):
                    sp.dma_start(gains[:, 3 * DEPTH + i, :],
                                 a[name].rearrange("(c p) -> p c", p=P)).then_inc(params_loaded, 16)
                for l in range(DEPTH):
                    sp.dma_start(lgains[:, l, 0:2],
                                 a["mla_q_norm"][l].rearrange("(c p) -> p c", p=P)).then_inc(params_loaded, 16)
                    sp.dma_start(lgains[:, l, 2:3],
                                 a["mla_kv_norm"][l].rearrange("(c p) -> p c", p=P)).then_inc(params_loaded, 16)
                sp.dma_start(gbias[:, :, :],
                             a["nsa_gate_bias"].partition_broadcast(P)).then_inc(params_loaded, 16)
                sp.dma_start(sinks[:, :],
                             a["attn_sinks_2"][0].partition_broadcast(P)).then_inc(params_loaded, 16)
                sp.dma_start(rel[:, :], a["rel_bias_2"]).then_inc(params_loaded, 16)
                sp.dma_start(bs[:, :], a["gm_b_spatial_2"][0]).then_inc(params_loaded, 16)
                sp.dma_start(rb[:, 0:4], a["router_group_b_2"][0].partition_broadcast(P)).then_inc(params_loaded, 16)
                sp.dma_start(rb[:, 4:20], a["router_expert_b_2"][0].rearrange("g e -> (g e)")
                             .partition_broadcast(P)).then_inc(params_loaded, 16)
                sp.dma_start(rw[:, :, 0:4],
                             a["router_group_w_2"][0].rearrange("(c p) g -> p c g", p=P)).then_inc(params_loaded, 16)
                for g in range(4):
                    sp.dma_start(rw[:, :, 4 + 4 * g:8 + 4 * g],
                                 a["router_expert_w_2"][0, g].rearrange("(c p) e -> p c e", p=P)
                                 ).then_inc(params_loaded, 16)

            def ffn(l, ph):
                gub, fb = ph * 2 * NSL, (F1, F2)[ph]

                def up(sl, par):
                    for s, w in ((0, w_gate), (1, w_up)):
                        if not isinstance(sl, int) or sl > 0:
                            sp.wait_ge(gu_full, gu_at(l, gub, sl * 2))
                        elif ph == 0:
                            sp.wait_ge(gu_full, gu_at(l, 0, 0))
                        else:
                            sp.wait_ge(acc_full, mix_full(l, T_HEAD + 2 * (2 + s) + 2))
                        sp.dma_start(s3(s, KC, FS), w[ph][l][:, :, bass.ds(sl * FS, FS)]).then_inc(w_loaded[s], 16)

                def down(sl, par, last):
                    if not isinstance(sl, int) or sl > 0:
                        sp.wait_ge(acc_full, full_at(l, fb, sl * KC))
                    elif ph == 0:
                        sp.wait_ge(acc_full, full_at(l, 0, 0))
                    else:
                        sp.wait_ge(acc_full, mix_full(l, T_HEAD + 4))
                    sp.dma_start(s3(2, 2, D), w_down[ph][l][:, bass.ds(sl * 2, 2), :]).then_inc(w_loaded[2], 16)

                run_slices(sp, NSL, up, down)

            def mix_loads(l):
                wi = w_in[l]

                def cols(s, c0, n, at_=0, w=256):
                    sp.dma_start(s3(s, KC, w)[:, :, at_:at_ + n], wi[:, :, c0:c0 + n]).then_inc(w_loaded[s], 16)

                for n in range(NLM):
                    s = n % 3
                    if n < 2:
                        sp.wait_ge(gu_full, gu_at(l, 2 * NSL, 0))
                    elif n == 2:
                        sp.wait_ge(acc_full, mix_full(l, 0))
                    else:
                        o = n - 3
                        sp.wait_ge(acc_full, mix_full(l, (LAST_TICKET[o] if o < W_OUT0 else
                                                          T_HEAD + 2 * (o - W_OUT0) + 1) + 1))
                    if n == 0:
                        cols(s, C_CQ, 256)
                    elif n == 1:
                        cols(s, C_CKV, 160, w=160)
                    elif n == 2:
                        for c in range(2):
                            for g in range(2):
                                cols(s, C_NQ + HD * (3 * g + c), HD, at_=128 * c + 64 * g)
                    elif n == 3:
                        for g in range(2):
                            cols(s, C_NQ + HD * (3 * g + 2), HD, at_=64 * g)
                        cols(s, C_KC, 128, at_=128)
                    elif n == 4:
                        cols(s, C_VC, 256)
                    elif n == 5:
                        cols(s, C_VS, 256)
                    elif n == 6:
                        cols(s, C_VW, 146, w=146)
                    elif n == 7:
                        cols(s, C_SQ, 256)
                    elif n == 8:
                        cols(s, C_SK, 256)
                    elif n == 9:
                        cols(s, C_SV, 256)
                    elif n == 10:
                        sp.dma_start(s3(s, 2, 576), w_uq[l]).then_inc(w_loaded[s], 16)
                    elif n == 11:
                        sp.dma_start(s3(s, 1, 768), w_ukv[l]).then_inc(w_loaded[s], 16)
                    elif n < 16:
                        w1 = a["nsa_cmp_w1_k" if n < 14 else "nsa_cmp_w1_v"][l].rearrange("(l d) j -> d l j", d=HD)
                        for g in range(2):
                            sp.dma_start(s3(s, 16, P)[g * HD:(g + 1) * HD], w1[:, 16 * (n % 2):16 * (n % 2) + 16, :]
                                         ).then_inc(w_loaded[s], 16)
                    else:
                        sp.dma_start(s3(s, KC, 256), w_out[l][:, :, (n - W_OUT0) * 256:(n - W_OUT0 + 1) * 256]
                                     ).then_inc(w_loaded[s], 16)

            with sp.Fori(0, DEPTH) as l:
                sp.wait_ge(acc_full, full_at(l, 0, 0))
                with nc.allow_non_contiguous_dma(reason="small parameters"):
                    sp.dma_start(cmp_w2[:, 0, :], a["nsa_cmp_w2_k"][l]).then_inc(small_loaded, 16)
                    sp.dma_start(cmp_w2[:, 1, :], a["nsa_cmp_w2_v"][l]).then_inc(small_loaded, 16)
                    sp.dma_start(cmp_pos[:, 0, :], a["nsa_cmp_pos_k"][l].rearrange("l d -> d l")
                                 ).then_inc(small_loaded, 16)
                    sp.dma_start(cmp_pos[:, 1, :], a["nsa_cmp_pos_v"][l].rearrange("l d -> d l")
                                 ).then_inc(small_loaded, 16)
                ffn(l, 0)
                mix_loads(l)
                ffn(l, 1)

            L = DEPTH
            sp.wait_ge(x_final, KC * 3 * DEPTH)
            sp.dma_start(ws_n, a["gm_w_spatial_2"][0].rearrange("g t s -> t g s")).then_inc(ws_loaded, 16)
            sp.dma_start(gv, a["gm_v_norm_g_2"][0].partition_broadcast(P)).then_inc(ws_loaded, 16)
            for n, (name, c0) in enumerate(SECOND):
                s = n % 3
                if n < 2:
                    sp.wait_ge(gu_full, gu_at(L, 0, 0))
                elif n == 2:
                    sp.wait_ge(acc_full, full_at(L, 0, 0))
                else:
                    sp.wait_ge(acc_full, full_at(L, 0, full2(LAST2[n - 3] + 1)))
                if name == "q":
                    for c in range(2):
                        for g in range(2):
                            h = c0 // 128 + c + 4 * g
                            sp.dma_start(s3(s, KC, 256)[:, :, 128 * c + 64 * g:128 * c + 64 * g + 64],
                                         w_in2[:, :, 1024 + HD * h:1024 + HD * h + HD]).then_inc(w_loaded[s], 16)
                elif name in ("pa", "pb"):
                    sp.dma_start(s3(s, 4, 512), (w_pa if name == "pa" else w_pb)[:, :, c0:c0 + 512]
                                 ).then_inc(w_loaded[s], 16)
                elif name == "wo":
                    sp.dma_start(s3(s, KC, 256), w_out2[:, :, c0:c0 + 256]).then_inc(w_loaded[s], 16)
                else:
                    first = {"u": 0, "v": 512, "kv": 1536, "gate": 1792}[name]
                    sp.dma_start(s3(s, KC, 256), w_in2[:, :, first + c0:first + c0 + 256]
                                 ).then_inc(w_loaded[s], 16)
                if n == 6:
                    sp.wait_ge(relrow_ready, 1)
                    sp.dma_start(rel_dram, rrow.unsqueeze(1).broadcast_to([8, P, 384])).then_inc(rel_stored, 16)
                    sp.wait_ge(rel_stored, 16)
                    sp.dma_start(bias_t, bass.AP(rel_dram.tensor, 127, [[383, P], [384 * P, 8], [1, 256]])
                                 ).then_inc(bias_loaded, 16)
            sp.wait_ge(acc_free[T2["combt", 0] % 2], free_at(L, 0, T2["combt", 0] + 2))
            sp.dma_start(comb_dram, comb_T[:, :]).then_inc(comb_stored, 16)
            sp.wait_ge(comb_stored, 16)

            def x_ups(e, half, sl):
                par = half
                for s, w in ((0, x_gate), (1, x_up)):
                    if not isinstance(sl, int) or sl > 0:
                        sp.wait_ge(gu_full, gu_at(L, 0, sl * 2))
                    else:
                        sp.wait_ge(acc_full, full_at(L, 0, full2(LAST2[NSEC - 2 + s] + 1)))
                    sp.dma_start(s3(s, KC, FS), w[e][:, :, half * FS:(half + 1) * FS]).then_inc(w_loaded[s], 16)
                if not isinstance(sl, int) or sl > 1:
                    sp.wait_ge(hid_done, L * TG + 2 + sl * 2 - 2)
                sp.dma_start(cb[:, par, :], comb_dram[bass.ds(e, 1), :][0].partition_broadcast(P)).then_inc(cb_loaded[par], 16)

            def x_downs(e, half, sl):
                if not isinstance(sl, int) or sl > 0:
                    sp.wait_ge(acc_full, full_at(L, FMOE, sl * KC))
                else:
                    sp.wait_ge(acc_full, full_at(L, 0, full2(LAST2[NSEC - 3] + 1)))
                sp.dma_start(s3(2, 2, D), x_down[e][:, 2 * half:2 * half + 2, :]).then_inc(w_loaded[2], 16)

            x_ups(0, 0, 0)
            x_ups(0, 1, 1)
            x_downs(0, 0, 0)
            with sp.Fori(0, NX - 1) as i:
                x_ups(i + 1, 0, i * 2 + 2)
                x_downs(i, 1, i * 2 + 1)
                x_ups(i + 1, 1, i * 2 + 3)
                x_downs(i + 1, 0, i * 2 + 2)
            x_downs(NX - 1, 1, MOE_SLICES - 1)

            for b in range(TB):
                sp.wait_ge(y_ready, 2 * b + 2)
                sp.dma_start(y_tok[:, b, :], y_out[:, b, :]).then_inc(y_stored, 16)
            sp.wait_ge(y_stored, 16 * TB)

        N_PARAMS = 16 * (1 + 3 * DEPTH + 4 + 2 * DEPTH + 11)
        L = DEPTH
        OUT_HEADS = [("mla", h) for h in range(6)] + [("nsa", h) for h in range(6)]
        ROPES = ([(q6[0:96, h, :], "mla", ("uq", h)) for h in range(6)]
                 + [(lora[0:96, 3, :], "mla", ("kr", 0))]
                 + [(nq[:, c, :], "nsa", ("nq", c)) for c in range(3)]
                 + [(nk[:, i, :], "nsa", (n, 0)) for i, n in enumerate(("kc", "ks", "kw"))])
        EVAC = {("cq", 0): (lora[:, 0, :], 1.0), ("cq", 1): (lora[:, 1, :], 1.0), ("ckv", 0): (lora[:, 2, :], 1.0),
                ("kr", 0): (lora[0:96, 3, :], 1.0), ("kc", 0): (nk[:, 0, :], 1.0), ("ks", 0): (nk[:, 1, :], 1.0),
                ("kw", 0): (nk[:, 2, :], 1.0), ("vc", 0): (nk[:, 3, :], 1.0),
                ("vs", 0): (vs.rearrange("p a b -> p (a b)"), 1.0), ("vw", 0): (vw.rearrange("p a b -> p (a b)"), 1.0)}
        for i in range(3):
            EVAC["nq", i] = (nq[:, i, :], HD ** -0.5)
        for i in range(2):
            EVAC["sq", i] = (sq_T[:, i, :], HD ** -0.5)
            EVAC["sk", i] = (sk_T[:, i, :], 1.0)
            EVAC["sv", i] = (sv[:, 2 * i:2 * i + 2, :].rearrange("p a b -> p (a b)"), 1.0)
        for i in range(6):
            EVAC["uq", i] = (q6[0:96, i, :], 96.0 ** -0.5)
            EVAC["kn", i] = (k6[0:HD, i, :], 1.0)
        for i in range(TB):
            EVAC["mv", i] = (mv[:, i, :], 1.0)

        def taken(eng, l, base, n):
            eng.wait_ge(acc_free[n % 2], free_at(l, base, n + 2))

        def unit_info(n):
            kind, h, i, br, first, last = UNITS[n]
            blk = slice(i * P, (i + 1) * P)
            w = (i + 1) * P
            if kind == "mla":
                q, k = q6[0:96, h, blk], k6[0:96, h, 0:w]
                v = [mv[:, j, h * HD:(h + 1) * HD] for j in range(i + 1)]
            else:
                g, c = NSA_HALF(h)
                r = slice(g * HD, (g + 1) * HD)
                q = nq[r, c, blk]
                if br == "cmp":
                    w = 31
                    k, v = kcmp_T[r, :], [vcmp[:, g, :]]
                else:
                    k = nk[r, 1 if br == "sel" else 2, 0:w]
                    vt = vs if br == "sel" else vw
                    v = [vt[:, j, g * HD:(g + 1) * HD] for j in range(i + 1)]
            return dict(q=q, k=k, v=v, w=w, i=i, h=h, br=br, first=first, last=last,
                        out=slice((h % 2) * HD, (h % 2) * HD + HD), blk=blk,
                        head=(0 if kind == "mla" else 6) + h,
                        end=last and i == TB - 1, begin=first and i == 0)

        def swa_info(n):
            h, i = SWA_UNITS[n]
            g, c = h // 4, h % 4
            lo = max(0, i - 1)
            r = slice(g * HD, (g + 1) * HD)
            return dict(q=q2[r, c, i * P:(i + 1) * P], k=k2[r, lo * P:(i + 1) * P],
                        v=[v2[:, j, g * HD:(g + 1) * HD] for j in range(lo, i + 1)],
                        w=(i + 1 - lo) * P, i=i, h=h, first=True, last=True, br="swa",
                        out=slice((h % 2) * HD, (h % 2) * HD + HD), blk=slice(i * P, (i + 1) * P),
                        head=h, end=i == TB - 1, begin=i == 0)

        NSW = len(SWA_UNITS)
        U2 = DEPTH * NU

        @block.tensor
        def _(pe):
            mm = nc.tensor.matmul

            def acc_wait(l, base, n):
                pe.wait_ge(acc_free[n % 2], free_at(l, base, n))
                return acc[n % 2]

            def slot_wait(s, l, n_dmas):
                pe.wait_ge(w_loaded[s], at(l, 16 * SLOT_DMAS[s], 16 * n_dmas))

            def norm(k):
                for c in range(KC):
                    pe.wait_ge(squared, k * KC + c + 1)
                    m = mm(turn[0][:, :], cst("ones"), h_T[:, c, :], start=c == 0, stop=c == KC - 1)
                m.then_inc(ssq_full, 1)

            def slices(l, base, free_base, gub, dma_base, n, k, per=1):
                def up(sl, par):
                    if isinstance(sl, int) and sl == 0:
                        pe.wait_ge(h_ready, k * KC + KC)
                    for c in range(2):
                        pe.wait_ge(hid_done, at(l, TG, gub + sl * 2 + c + 1))
                        for w in range(2):
                            if c == 0:
                                slot_wait(w, l, dma_base[w] + sl + 1)
                            for kc in range(KC):
                                m = mm(score[2 * w + c][:, :], s3(w, KC, FS)[:, kc, c * P:(c + 1) * P],
                                       h_T[:, kc, :], start=kc == 0, stop=kc == KC - 1)
                        m.then_inc(gu_full, 1)

                def down(sl, par, last):
                    slot_wait(2, l, dma_base[2] + sl + 1)
                    pe.wait_ge(hid_done, at(l, TG, gub + sl * 2 + 4))
                    for c in range(KC):
                        pe.wait_ge(acc_free[c % 2], at(l, TL // 2, free_base // 2 + sl * (KC // 2) + c // 2 + 1))
                        for j in range(2):
                            m = mm(acc[c % 2][:, :], s3(2, 2, D)[:, j, c * P:(c + 1) * P],
                                   hid[:, 2 * par + j, :], start=j == 0, stop=j == 1)
                        m.then_inc(acc_full, 1)

                run_slices(pe, n, up, down)

            def linear(ps, s, width, col, m_cols, rhs, n_k, out_rows=None):
                for kc in range(n_k):
                    m = mm(ps[0:m_cols, :], s3(s, n_k, width)[:, kc, col:col + m_cols], rhs[:, kc, :],
                           start=kc == 0, stop=kc == n_k - 1)
                return m

            def by_token(ps, s, width, col, n, blocks, n_k=KC, src=h_T):
                for j, b in enumerate(blocks):
                    for kc in range(n_k):
                        m = mm(ps[:, j * n:(j + 1) * n], src[:, kc, b * P:(b + 1) * P],
                               s3(s, n_k, width)[:, kc, col:col + n], start=kc == 0, stop=kc == n_k - 1)
                return m

            def attend(l, per, u0, n_units, info, s_done, fr, fbase, head0):
                def scores(n):
                    u = info(n)
                    if n >= 4:
                        pe.wait_ge(s_done, at(l, per, u0 + n - 3))
                    mm(score[n % 4][:, 0:u["w"]], u["q"], u["k"], start=True, stop=True).then_inc(s_full, 1)

                def turns(n):
                    u = info(n)
                    pe.wait_ge(p_ready, at(l, per, u0 + n + 1))
                    if n >= 2:
                        pe.wait_ge(pt_ready, at(l, per, u0 + n - 1))
                    w = min(u["w"], P)
                    for j in range(len(u["v"])):
                        m = nc.tensor.transpose(turn[n % 2][0:w, j * P:(j + 1) * P],
                                                probs[:, n % 3, j * P:j * P + w], ident)
                    m.then_inc(t_full, 1)

                def values(n):
                    u = info(n)
                    w = min(u["w"], P)
                    t = head0 + u["head"]
                    if u["begin"]:
                        acc_wait(fr, fbase, t)
                    pe.wait_ge(pt_ready, at(l, per, u0 + n + 1))
                    for j, v in enumerate(u["v"]):
                        m = mm(acc[t % 2][u["out"], u["blk"]], v[0:w, :], probs_T[0:w, n % 2, j * P:(j + 1) * P],
                               start=u["first"] and j == 0, stop=u["last"] and j == len(u["v"]) - 1,
                               skip_group_check=True)
                    m.then_inc(pv_done, 1)

                AHEAD = 3
                for n in range(min(AHEAD, n_units)):
                    scores(n)
                for n in range(n_units + 1):
                    if n + AHEAD < n_units:
                        scores(n + AHEAD)
                    if n < n_units:
                        turns(n)
                    if n >= 1:
                        values(n - 1)

            def mix(l):
                pe.wait_ge(h_ready, at(l, 3 * KC, 2 * KC))
                d0 = [NSL] * 3
                for n, (name, i, ld, who) in enumerate(MIX):
                    if ld is not None:
                        s = ld % 3
                        slot_wait(s, l, NSL + sum(MIX_DMAS[s:ld + 1:3]))
                        if name in ("hid_k", "hid_v"):
                            s0 = (ld - 1) % 3
                            slot_wait(s0, l, NSL + sum(MIX_DMAS[s0:ld:3]))
                    if (name, i) == ("kc", 0):
                        pe.wait_ge(lsq_ready, l + 1)
                        for j in range(2):
                            mm(turn[0][:, :], cst("ones"), probs[:, j, :], start=j == 0, stop=j == 1)
                        mm(turn[1][:, :], cst("ones"), probs[:, 2, :], start=True, stop=True).then_inc(lssq_full, 1)
                    if name == "uq" and i == 0:
                        pe.wait_ge(lora_ready, l + 1)
                    if name == "rope":
                        taken(pe, l, BM, TICKET[ROPES[i][2]])
                    if name == "hid_k":
                        pe.wait_ge(rope_ready, at(l, len(ROPES), len(ROPES)))
                        pe.wait_ge(small_loaded, at(l, 64, 64))
                    if name == "hid_v":
                        taken(pe, l, BM, TICKET["vc", 0])
                    if name == "cmp":
                        pe.wait_ge(hidc_ready, at(l, 2, 2))
                    ps = acc_wait(l, BM, n)
                    if name in ("cq", "sq", "sk") or (name == "nq" and i < 2):
                        m = linear(ps, s, 256, 128 * i, 128, h_T, KC)
                    elif name == "nq" or name in ("ckv", "vc"):
                        m = linear(ps, s, 160 if name == "ckv" else 256, 0, 128, h_T, KC)
                    elif name == "kr":
                        m = linear(ps, s, 160, 64, 96, h_T, KC)
                    elif name in ("kc", "ks", "kw"):
                        m = linear(ps, s, 256, 128, 128, h_T, KC)
                    elif name == "vs":
                        m = by_token(ps, s, 256, 0, P, range(TB))
                    elif name == "vw":
                        m = by_token(ps, s, 146, 0, P, range(TB))
                    elif name == "gate":
                        m = by_token(ps, s, 146, P, 18, range(TB))
                    elif name == "sv":
                        m = by_token(ps, s, 256, 0, 256, (2 * i, 2 * i + 1))
                    elif name == "uq":
                        m = linear(ps, s, 576, 96 * i, 96, lora, 2)
                    elif name == "kn":
                        m = mm(ps[0:HD, :], s3(s, 1, 768)[:, 0, 128 * i:128 * i + HD], lora[:, 2, :],
                               start=True, stop=True)
                    elif name == "mv":
                        wv = slot[s][:, 0:768].rearrange("p (h t d) -> p h t d", t=2, d=HD)[:, :, 1, :]
                        m = mm(ps[:, 0:384], lora[:, 2, i * P:(i + 1) * P], wv, start=True, stop=True)
                    elif name == "rope":
                        t, kind, _ = ROPES[i]
                        r = 96 if kind == "mla" else P
                        m = mm(ps[0:r, :], cst("r_" + kind, rows=r), t, start=True, stop=True)
                    elif name in ("hid_k", "hid_v"):
                        kv = 0 if name == "hid_k" else 1
                        src = nk[:, 0 if kv == 0 else 3, :]
                        w1 = [s3(x % 3, 16, P) for x in (ld - 1, ld)]
                        for g in range(2):
                            r = slice(g * HD, (g + 1) * HD)
                            for j in range(32):
                                mm(ps[:, g * 31:g * 31 + 31], w1[j // 16][r, j % 16, :], src[r, j:j + 481:16],
                                   start=j == 0, stop=j == 31)
                            pe.drain()
                        for j in range(32):
                            m = mm(ps[:, 62:63], w1[j // 16][0:HD, j % 16, :], cmp_pos[:, kv, j:j + 1],
                                   start=j == 0, stop=j == 31)
                    elif name == "cmp":
                        for g in range(2):
                            mm(ps[g * HD:(g + 1) * HD, 0:31], cmp_w2[:, 0, :], hid_cmp[:, 0, g * 31:g * 31 + 31],
                               start=True, stop=True)
                        for g in range(2):
                            m = mm(ps[0:31, 64 + g * HD:128 + g * HD], hid_cmp[:, 1, g * 31:g * 31 + 31],
                                   cmp_w2[:, 1, :], start=True, stop=True)
                    m.then_inc(acc_full, 1)
                taken(pe, l, BM, TICKET["cmp", 0])
                attend(l, NU, 0, NU, unit_info, exp_ready, l, BM, T_LIN)
                pe.wait_ge(exp_ready, at(l, NU, NU))
                for h in range(SB_HEADS):
                    r, c = slice((h % 2) * HD, (h % 2) * HD + HD), h // 2
                    for j in range(TB):
                        if h:
                            pe.wait_ge(a_exp, at(l, NZ, NZ_AT(h - 1, j) + 1))
                        mm(score[j][:, 0:S - j * P], sk_T[r, c, j * P:(j + 1) * P], sq_T[r, c, j * P:S],
                           start=True, stop=True).then_inc(z_full, 1)
                    pe.wait_ge(sp_ready, at(l, NZ, NZ_AT(h, TB - 1) + 1))
                    for j in range(TB):
                        m = mm(score[j][:, 0:S - j * P], cst("negtri"), hid[:, j, 0:S - j * P],
                               start=False, stop=j == TB - 1, skip_group_check=True)
                        for jj in range(j + 1, TB):
                            m = mm(score[j][:, (jj - j) * P:S - j * P], cst("negones"), hid[:, jj, 0:S - jj * P],
                                   start=False, stop=jj == TB - 1, skip_group_check=True)
                        m.then_inc(suffix_full, 1)
                    ps = acc_wait(l, BM, T_LIN + NHD + h)
                    for j in range(TB):
                        pe.wait_ge(a_ready, at(l, NZ, NZ_AT(h, j) + 1))
                        m = mm(ps[r, j * P:S], sv[:, j, h * HD:(h + 1) * HD], lora[:, j, 0:S - j * P],
                               start=j == 0, stop=j == TB - 1, skip_group_check=True)
                    m.then_inc(acc_full, 1)
                taken(pe, l, BM, T_LIN + NHD + SB_HEADS - 2)
                taken(pe, l, BM, T_LIN + NHD + SB_HEADS - 1)
                for c in range(KC):
                    ld = W_OUT0 + c // 2
                    slot_wait(ld % 3, l, NSL + sum(MIX_DMAS[ld % 3:ld + 1:3]))
                    ps = acc_wait(l, BM, T_HEAD + c)
                    linear(ps, ld % 3, 256, (c % 2) * P, P, o_T, KC).then_inc(acc_full, 1)

            pe.sem_inc(acc_free[0], 1)
            pe.sem_inc(acc_free[1], 1)
            pe.sem_inc(acc_full, 1)
            pe.sem_inc(gu_full, 1)
            pe.sem_inc(hid_done, 2)
            pe.wait_ge(params_loaded, N_PARAMS)
            pe.wait_ge(x_loaded, 16)
            for c in range(KC):
                if c >= 2:
                    pe.wait_ge(x_final, c - 1)
                for b in range(TB):
                    m = nc.tensor.transpose(turn[c % 2][:, b * P:(b + 1) * P], x_in[:, b, c * P:(c + 1) * P], ident)
                m.then_inc(xt_full, 1)
            pe.wait_ge(x_final, KC)
            with pe.Fori(0, DEPTH) as l:
                norm(l * 3)
                slices(l, F1, B1, 0, [0, 0, 0], NSL, l * 3)
                norm(l * 3 + 1)
                mix(l)
                norm(l * 3 + 2)
                slices(l, F2, B2, 2 * NSL, [NSL + sum(MIX_DMAS[s::3]) for s in range(3)], NSL, l * 3 + 2)

            norm(3 * L)
            norm(3 * L + 1)
            pe.wait_ge(h_ready, KC * (3 * L + 2))
            mm(turn[0][0:8, 0:384], rel[:, :], cst("bucket_rows", rows=32), start=True, stop=True
               ).then_inc(rel_full, 1)
            for n, (name, i, ld) in enumerate(SEC_T):
                if ld is not None:
                    s = ld % 3
                    slot_wait(s, L, sum(SEC_DMAS[s:ld + 1:3]))
                if (name, i) == ("wst", 0):
                    pe.wait_ge(ws_loaded, 32)
                if (name, i) == ("sv", 0):
                    pe.wait_ge(vn_ready, 1)
                    taken(pe, L, 0, T2["wst", 0])
                    taken(pe, L, 0, T2["wst", 1])
                if name == "swa":
                    if i == 0:
                        taken(pe, L, 0, T2["sv", 3])
                        taken(pe, L, 0, T2["k", 0])
                        attend(L, NU, 0, NSW, swa_info, max_ready, L, 0, SWA0)
                    continue
                if (name, i) == ("pa", 0):
                    taken(pe, L, 0, T2["swa", 6])
                    taken(pe, L, 0, T2["swa", 7])
                if (name, i) == ("wo", 0):
                    pe.wait_ge(merged_ready, KC)
                if name == "route":
                    norm(3 * L + 2)
                    pe.wait_ge(h_ready, KC * (3 * L + 3))
                if name == "combt":
                    pe.wait_ge(comb_done, 1)
                ps = acc_wait(L, 0, n)
                if name in ("u", "q", "gate"):
                    m = linear(ps, s, 256, (i % 2) * P, P, h_T, KC)
                elif name == "v":
                    m = by_token(ps, s, 256, 0, 256, (2 * (i % 2), 2 * (i % 2) + 1))
                elif name == "k":
                    m = linear(ps, s, 256, 0, P, h_T, KC)
                elif name == "vtok":
                    m = by_token(ps, s, 256, P, P, range(TB))
                elif name == "wst":
                    for g in range(4):
                        m = nc.tensor.transpose(ps[:, g * P:(g + 1) * P], ws_n[:, 4 * i + g, :], ident)
                elif name == "sv":
                    for b in range(TB):
                        for g in range(2):
                            mm(ps[g * HD:(g + 1) * HD, b * P:(b + 1) * P],
                               vtok[:, b, (2 * i + g) * HD:(2 * i + g + 1) * HD], ws_T[:, 2 * i + g, :],
                               start=True, stop=False, skip_group_check=True)
                        m = mm(ps[:, b * P:(b + 1) * P], cst("group_rows", 8, i * P, (i + 1) * P), bs[:, :],
                               start=False, stop=True, skip_group_check=True)
                elif name in ("pa", "pb"):
                    m = linear(ps, s, 512, (i % 4) * P, P, ab_T if name == "pa" else ab_T[:, 4:8, :], 4)
                elif name == "wo":
                    m = linear(ps, s, 256, (i % 2) * P, P, sig_a, KC)
                elif name == "route":
                    for b in range(TB):
                        for kc in range(KC):
                            m = mm(ps[:, b * 20:(b + 1) * 20], h_T[:, kc, b * P:(b + 1) * P], rw[:, kc, :],
                                   start=kc == 0, stop=kc == KC - 1)
                elif name == "combt":
                    for b in range(TB):
                        m = nc.tensor.transpose(ps[0:16, b * P:(b + 1) * P], comb[:, b, :], ident)
                m.then_inc(acc_full, 1)
            slices(L, FMOE, BMOE, 0, [sum(SEC_DMAS[s::3]) for s in range(3)], MOE_SLICES, 3 * L + 2)
            norm(3 * L + 3)
            pe.wait_ge(h_ready, KC * (3 * L + 4))
            for n in range(2 * TB):
                if n >= 2:
                    pe.wait_ge(y_ready, n - 1)
                for c in range(4):
                    m = nc.tensor.transpose(turn[n % 2][:, c * P:(c + 1) * P],
                                            h_T[:, 4 * (n % 2) + c, (n // 2) * P:(n // 2 + 1) * P], ident)
                m.then_inc(yt_full, 1)

        @block.scalar
        def _(act):
            fn = nc.scalar.activation

            def norm(k):
                for c in range(KC):
                    act.wait_ge(x_final, k * KC + c + 1)
                    fn(h_T[:, c, :], x_T[:, c, :], ACT.Square).then_inc(squared, 1)
                act.wait_ge(ssq_full, k + 1)
                fn(rstd[:, :], turn[0][:, :], ACT.Ln, scale=1.0 / D, bias=eps[:, :])
                act.drain()
                fn(rstd[:, :], rstd[:, :], ACT.Exp, scale=-0.5).then_inc(rstd_ready, 1)

            def slices(l, gub, n):
                def up(sl, par):
                    for c in range(2):
                        act.wait_ge(gu_full, gu_at(l, gub, sl * 2 + c + 1))
                        fn(et[:, c, :], score[c][:, :], ACT.Exp, scale=-1.0).then_inc(sig_ready, 1)

                run_slices(act, n, up, lambda *x: None)

            def attend(l, per, u0, n_units, info, fr, fbase, head0, dest, sink):
                def exps(n):
                    u = info(n)
                    w, st = u["w"], n % 4
                    act.wait_ge(max_ready, at(l, per, u0 + n + 1))
                    if n >= 3 and not sink:
                        act.wait_ge(t_full, at(l, per, u0 + n - 2))
                    src = probs[:, n % 3, 0:w] if sink else score[st][:, 0:w]
                    m = fn(probs[:, n % 3, 0:w], src, ACT.Exp, bias=stats[:, 0, st:st + 1],
                           accum_out=stats[:, 1, st:st + 1])
                    if sink:
                        m = fn(stats[:, 3, st:st + 1], sinks[:, u["h"]:u["h"] + 1], ACT.Exp,
                               bias=stats[:, 0, st:st + 1])
                    m.then_inc(exp_ready, 1)

                def evac_turn(n):
                    u = info(n)
                    r, w = min(u["w"], P), len(u["v"]) * P
                    act.wait_ge(t_full, at(l, per, u0 + n + 1))
                    if n >= 2:
                        act.wait_ge(pv_done, at(l, per, u0 + n - 1))
                    fn(probs_T[0:r, n % 2, 0:w], turn[n % 2][0:r, 0:w], ACT.Copy).then_inc(pt_ready, 1)

                def head_out(n):
                    u = info(n)
                    if u["end"]:
                        t = head0 + u["head"]
                        act.wait_ge(pv_done, at(l, per, u0 + n + 1))
                        fn(dest[u["out"], u["head"] // 2, :], acc[t % 2][u["out"], :], ACT.Copy
                           ).then_inc(acc_free[t % 2], 1)

                exps(0)
                for n in range(n_units + 1):
                    if n + 1 < n_units:
                        exps(n + 1)
                    if n < n_units:
                        evac_turn(n)
                    if n >= 1:
                        head_out(n - 1)

            def mix(l):
                for n, (name, i, ld, who) in enumerate(MIX):
                    if who == "act":
                        act.wait_ge(acc_full, mix_full(l, n + 1))
                        if name == "cmp":
                            fn(kcmp_T[:, :], acc[n % 2][:, 0:31], ACT.Copy)
                            m = fn(vcmp.rearrange("p a b -> p (a b)"), acc[n % 2][0:31, 64:192], ACT.Copy)
                        else:
                            t, sc = EVAC[name, i]
                            m = fn(t, acc[n % 2][0:t.shape[0], 0:t.shape[1]], ACT.Copy, scale=sc)
                        m.then_inc(acc_free[n % 2], 1)
                    if (name, i) == ("ckv", 0):
                        act.drain()
                        fn(probs[:, :, :], lora[:, 0:3, :], ACT.Square).then_inc(lsq_ready, 1)
                    if (name, i) == ("ks", 0):
                        act.wait_ge(lssq_full, l + 1)
                        fn(et[:, 0, :], turn[0][:, :], ACT.Ln, scale=1.0 / 256, bias=eps[:, :])
                        fn(et[:, 1, :], turn[1][:, :], ACT.Ln, scale=1.0 / 128, bias=eps[:, :])
                        act.drain()
                        fn(et[:, :, :], et[:, :, :], ACT.Exp, scale=-0.5).then_inc(lrstd_ready, 1)
                    if name == "gate":
                        taken(act, l, BM, n)
                        fn(gates_e[:, :, :], gates[:, :, :], ACT.Exp, scale=-1.0).then_inc(gate_exp, 1)
                    if name in ("hid_k", "hid_v"):
                        kv = 0 if name == "hid_k" else 1
                        act.wait_ge(gelu_pre, at(l, 2, kv + 1))
                        fn(cmp_t[:, 2, :], cmp_t[:, 1, :], ACT.Exp, scale=-2 * GC).then_inc(gelu_exp, 1)
                attend(l, NU, 0, NU, unit_info, l, BM, T_LIN, o_T, False)
                for h in range(SB_HEADS):
                    for j in range(TB):
                        n = S - j * P
                        act.drain()
                        act.wait_ge(z_full, at(l, NZ, NZ_AT(h, j) + 1))
                        if j >= 2:
                            act.wait_ge(sp_ready, at(l, NZ, NZ_AT(h, j - 2) + 1))
                        fn(et[:, j % 2, 0:n], score[j][:, 0:n], ACT.Abs)
                        act.drain()
                        fn(et[:, j % 2, 0:n], et[:, j % 2, 0:n], ACT.Exp, scale=-1.0)
                        act.drain()
                        fn(et[:, j % 2, 0:n], et[:, j % 2, 0:n], ACT.Ln, bias=1.0).then_inc(log_ready, 1)
                    for j in range(TB):
                        n = S - j * P
                        act.wait_ge(suffix_full, at(l, NZ, NZ_AT(h, j) + 1))
                        fn(lora[:, j, 0:n], score[j][:, 0:n], ACT.Exp).then_inc(a_exp, 1)
                    t = T_LIN + NHD + h
                    act.wait_ge(acc_full, mix_full(l, t + 1))
                    r = slice((h % 2) * HD, (h % 2) * HD + HD)
                    fn(o_T[r, 6 + h // 2, :], acc[t % 2][r, :], ACT.Copy).then_inc(acc_free[t % 2], 1)

            act.wait_ge(eps_ready, 1)
            act.wait_ge(params_loaded, N_PARAMS)
            with act.Fori(0, DEPTH) as l:
                norm(l * 3)
                slices(l, 0, NSL)
                norm(l * 3 + 1)
                mix(l)
                norm(l * 3 + 2)
                slices(l, 2 * NSL, NSL)

            norm(3 * L)
            norm(3 * L + 1)
            for n, (name, i, ld) in enumerate(SEC_T):
                if name in ("u", "v", "q", "k", "vtok", "gate"):
                    act.wait_ge(acc_full, full_at(L, 0, full2(n + 1)))
                    ps = acc[n % 2][:, :]
                    if name == "u":
                        m = fn(u_T[:, i, :], ps, ACT.Copy)
                    elif name == "v":
                        b, hf = i % 2, i // 2
                        m = fn(vtok[:, 2 * b:2 * b + 2, hf * 256:(hf + 1) * 256],
                               ps.rearrange("p (a b) -> p a b", b=256), ACT.Copy)
                    elif name == "q":
                        m = fn(q2[:, i, :], ps, ACT.Copy, scale=HD ** -0.5)
                    elif name == "k":
                        m = fn(k2, ps, ACT.Copy)
                    elif name == "vtok":
                        m = fn(v2.rearrange("p a b -> p (a b)"), ps, ACT.Copy)
                    else:
                        m = fn((sig_a if i < 8 else sig_b)[:, i % 8, :], ps, ACT.Exp, scale=-1.0)
                    m.then_inc(acc_free[n % 2], 1)
                if (name, i) == ("vtok", 0):
                    for j in range(8):
                        act.wait_ge(gelu_pre, 2 * L + j + 1)
                        fn(probs[:, j % 2, :], probs[:, j % 2, :], ACT.Exp, scale=-2 * GC).then_inc(gelu_exp, 1)
                    act.wait_ge(ln_pre, 1)
                    fn(lnst[:, 2, :], lnst[:, 1, :], ACT.Ln, scale=1.0 / 512, bias=eps[:, :])
                    act.drain()
                    fn(lnst[:, 3, :], lnst[:, 2, :], ACT.Exp, scale=-0.5).then_inc(ln_rstd, 1)
                if (name, i) == ("swa", 0):
                    attend(L, NU, 0, NSW, swa_info, L, 0, SWA0, ab_T[:, 4:8, :], True)
                if name == "route":
                    norm(3 * L + 2)
                    act.wait_ge(route_pre, 1)
                    fn(rx[:, 1, :, 0:4], rx[:, 0, :, 0:4], ACT.Exp).then_inc(route_exp, 1)
                    act.wait_ge(route_pre, 2)
                    fn(rx[:, 11, :, 0:1], rx[:, 10, :, 0:1], ACT.Exp).then_inc(route_exp, 1)
            slices(L, 0, MOE_SLICES)
            norm(3 * L + 3)
            for n in range(2 * TB):
                act.wait_ge(yt_full, n + 1)
                fn(y_out[:, n // 2, (n % 2) * S:(n % 2 + 1) * S], turn[n % 2][:, :], ACT.Copy).then_inc(y_ready, 1)

        @block.vector
        def _(dve):
            V = nc.vector

            def norm(k, dest=h_T):
                dve.wait_ge(rstd_ready, k + 1)
                for c in range(KC):
                    V.scalar_tensor_tensor(dest[:, c, :], x_T[:, c, :], gains[:, bass.ds(k, 1), c:c + 1][:, 0, :],
                                           rstd[:, :], ALU.mult, ALU.mult).then_inc(h_ready, 1)
                    if dest is x_T:
                        dve.drain().then_inc(x_final, 1)

            def slices(l, base, gub, n, coef, experts=False):
                def up(sl, par):
                    for c in range(2):
                        dve.wait_ge(sig_ready, at(l, TG, gub + sl * 2 + c + 1))
                        V.tensor_scalar(et[:, c, :], et[:, c, :], 1.0, None, ALU.add)
                        dve.drain()
                        V.reciprocal(rt[:, :], et[:, c, :])
                        dve.drain()
                        V.tensor_tensor(rt[:, :], rt[:, :], score[c][:, :], ALU.mult)
                        dve.drain()
                        if experts:
                            if c == 0:
                                dve.wait_ge(cb_loaded[par], sl * 8 + (16 - 8 * par))
                            V.tensor_tensor(rt[:, :], rt[:, :], cb[:, par, :], ALU.mult)
                            dve.drain()
                        V.tensor_tensor(hid[:, 2 * par + c, :], rt[:, :], score[2 + c][:, :], ALU.mult
                                        ).then_inc(hid_done, 1)

                def down(sl, par, last):
                    for c in range(KC):
                        dve.wait_ge(acc_full, full_at(l, base, sl * KC + c + 1))
                        V.scalar_tensor_tensor(x_T[:, c, :], acc[c % 2][:, :], coef, x_T[:, c, :],
                                               ALU.mult, ALU.add).then_inc(acc_free[c % 2], 1)
                        if last:
                            dve.drain().then_inc(x_final, 1)

                run_slices(dve, n, up, down)

            def attend(l, per, u0, n_units, info, sink):
                def maxima(n):
                    u = info(n)
                    w, st, i = u["w"], n % 4, u["i"]
                    ps = score[st]
                    dve.wait_ge(s_full, at(l, per, u0 + n + 1))
                    if sink:
                        if n >= 3:
                            dve.wait_ge(t_full, at(l, per, u0 + n - 2))
                        pr = probs[:, n % 3, 0:w]
                        V.tensor_tensor(pr, ps[:, 0:w], bias_t[:, u["h"], 256 - w:256], ALU.add)
                        dve.drain()
                        V.tensor_reduce(stats[:, 2, st:st + 1], pr, AX.X, ALU.max)
                        dve.drain()
                        V.tensor_scalar(stats[:, 0, st:st + 1], stats[:, 2, st:st + 1],
                                        sinks[:, u["h"]:u["h"] + 1], -1.0, ALU.max, ALU.mult
                                        ).then_inc(max_ready, 1)
                        return
                    if u["br"] == "cmp":
                        V.tensor_tensor(ps[:, 0:31], ps[:, 0:31], cst("cmp_mask", lo=i * 31, hi=i * 31 + 31), ALU.add)
                    else:
                        V.tensor_tensor(ps[:, i * P:w], ps[:, i * P:w], cst("causal"), ALU.add)
                    dve.drain()
                    V.tensor_reduce(stats[:, 0, st:st + 1], ps[:, 0:w], AX.X, ALU.max, negate=True
                                    ).then_inc(max_ready, 1)

                def normalize(n):
                    u = info(n)
                    w, st = u["w"], n % 4
                    dve.wait_ge(exp_ready, at(l, per, u0 + n + 1))
                    if sink:
                        V.tensor_tensor(stats[:, 1, st:st + 1], stats[:, 1, st:st + 1], stats[:, 3, st:st + 1], ALU.add)
                        dve.drain()
                    V.reciprocal(stats[:, 2, st:st + 1], stats[:, 1, st:st + 1])
                    dve.drain()
                    pr = probs[:, n % 3, 0:w]
                    if u["br"] in ("cmp", "sel", "win"):
                        g = u["h"] * 3 + ("cmp", "sel", "win").index(u["br"])
                        V.tensor_scalar(pr, pr, stats[:, 2, st:st + 1], gates[:, u["i"], g:g + 1],
                                        ALU.mult, ALU.mult).then_inc(p_ready, 1)
                    else:
                        V.tensor_scalar(pr, pr, stats[:, 2, st:st + 1], None, ALU.mult).then_inc(p_ready, 1)

                maxima(0)
                for n in range(n_units):
                    if n + 1 < n_units:
                        maxima(n + 1)
                    normalize(n)

            def gelu_pre_ops(x, t):
                dve.drain()
                V.tensor_tensor(t, x, x, ALU.mult)
                dve.drain()
                V.tensor_scalar(t, t, 0.044715, 1.0, ALU.mult, ALU.add)
                dve.drain()
                V.tensor_tensor(t, t, x, ALU.mult)
                dve.drain()
                V.tensor_scalar(t, t, -54.0, None, ALU.max).then_inc(gelu_pre, 1)

            def mix(l):
                for n, (name, i, ld, who) in enumerate(MIX):
                    ps = acc[n % 2]
                    if who == "dve":
                        dve.drain()
                        dve.wait_ge(acc_full, mix_full(l, n + 1))
                    if name == "gate":
                        V.tensor_tensor(gates[:, :, :], ps[:, 0:72].rearrange("p (b g) -> p b g", g=18),
                                        gbias[:, bass.ds(l, 1), :].broadcast_to([P, TB, 18]), ALU.add
                                        ).then_inc(acc_free[n % 2], 1)
                        dve.wait_ge(gate_exp, l + 1)
                        V.tensor_scalar(gates_e[:, :, :], gates_e[:, :, :], 1.0, None, ALU.add)
                        dve.drain()
                        V.reciprocal(gates[:, :, :], gates_e[:, :, :])
                        dve.drain()
                        g3 = gates.rearrange("p b (h r) -> p b h r", r=3)[:, :, :, 0]
                        V.tensor_tensor(g3, g3, cst("cmp_valid").unsqueeze(2).broadcast_to([P, TB, 6]), ALU.mult)
                        dve.wait_ge(lrstd_ready, l + 1)
                        for c in range(3):
                            m = V.scalar_tensor_tensor(lora[:, c, :], lora[:, c, :],
                                                       lgains[:, bass.ds(l, 1), c:c + 1][:, 0, :],
                                                       et[:, c // 2, :], ALU.mult, ALU.mult)
                        m.then_inc(lora_ready, 1)
                    elif name == "rope":
                        t, kind, _ = ROPES[i]
                        r = t.shape[0]
                        V.tensor_tensor(rt[0:r, :], ps[0:r, :], cst("sin_" + kind, rows=r), ALU.mult
                                        ).then_inc(acc_free[n % 2], 1)
                        V.tensor_tensor(t, t, cst("cos_" + kind, rows=r), ALU.mult)
                        dve.drain()
                        if i == 6:
                            V.tensor_tensor(k6[HD:96, :, :], t[HD:96, :].unsqueeze(1).broadcast_to([32, 6, S]),
                                            rt[HD:96, :].unsqueeze(1).broadcast_to([32, 6, S]), ALU.add
                                            ).then_inc(rope_ready, 1)
                        else:
                            V.tensor_tensor(t, t, rt[0:r, :], ALU.add).then_inc(rope_ready, 1)
                    elif name in ("hid_k", "hid_v"):
                        kv = 0 if name == "hid_k" else 1
                        V.tensor_copy(bias_c[:, kv:kv + 1], ps[:, 62:63])
                        dve.drain()
                        V.tensor_scalar(cmp_t[:, 0, :], ps[:, 0:62], bias_c[:, kv:kv + 1], None, ALU.add
                                        ).then_inc(acc_free[n % 2], 1)
                        dve.drain()
                        gelu_pre_ops(cmp_t[:, 0, :], cmp_t[:, 1, :])
                        dve.wait_ge(gelu_exp, at(l, 2, kv + 1))
                        V.tensor_scalar(cmp_t[:, 2, :], cmp_t[:, 2, :], 1.0, None, ALU.add)
                        dve.drain()
                        V.reciprocal(cmp_t[:, 3, :], cmp_t[:, 2, :])
                        dve.drain()
                        V.tensor_tensor(hid_cmp[:, kv, :], cmp_t[:, 0, :], cmp_t[:, 3, :], ALU.mult
                                        ).then_inc(hidc_ready, 1)
                attend(l, NU, 0, NU, unit_info, False)
                for h in range(SB_HEADS):
                    def softplus(j):
                        n = S - j * P
                        dve.wait_ge(log_ready, at(l, NZ, NZ_AT(h, j) + 1))
                        V.scalar_tensor_tensor(hid[:, j, 0:n], score[j][:, 0:n], 0.0, et[:, j % 2, 0:n],
                                               ALU.max, ALU.add)
                        dve.drain()
                        V.tensor_tensor(hid[:, j, 0:P], hid[:, j, 0:P], cst("strict"), ALU.mult).then_inc(sp_ready, 1)

                    for j in range(TB):
                        softplus(j)
                    for j in range(TB):
                        dve.wait_ge(a_exp, at(l, NZ, NZ_AT(h, j) + 1))
                        V.scalar_tensor_tensor(lora[:, j, 0:P], lora[:, j, 0:P], 1.0, cst("strict"),
                                               ALU.min, ALU.mult).then_inc(a_ready, 1)
                for c in range(KC):
                    dve.wait_ge(acc_full, mix_full(l, T_HEAD + c + 1))
                    V.tensor_tensor(x_T[:, c, :], acc[(T_HEAD + c) % 2][:, :], x_T[:, c, :], ALU.add
                                    ).then_inc(acc_free[(T_HEAD + c) % 2], 1)
                    dve.drain().then_inc(x_final, 1)

            def first_max(x, top, hit, desc, n, best, out_):
                V.tensor_reduce(rx[:, 12, :, top:top + 1], x, AX.X, ALU.max)
                dve.drain()
                V.tensor_tensor(hit, x, rx[:, 12, :, top:top + 1].broadcast_to([P, TB, n]), ALU.is_equal)
                dve.drain()
                V.tensor_tensor(hit, hit, cst(desc).unsqueeze(1).broadcast_to([P, TB, n]), ALU.mult)
                dve.drain()
                V.tensor_reduce(rx[:, 12, :, best:best + 1], hit, AX.X, ALU.max)
                dve.drain()
                V.tensor_tensor(out_, hit, rx[:, 12, :, best:best + 1].broadcast_to([P, TB, n]), ALU.is_equal)
                dve.drain()

            def route(n, ps):
                V.tensor_tensor(lg[:, :, :], ps[:, 0:80].rearrange("p (b g) -> p b g", g=20),
                                rb[:, :].unsqueeze(1).broadcast_to([P, TB, 20]), ALU.add
                                ).then_inc(acc_free[n % 2], 1)
                dve.drain()
                gl = lg[:, :, 0:4]
                first_max(gl, 0, rx[:, 2, :, 0:4], "desc4", 4, 1, rx[:, 3, :, 0:4])
                V.tensor_tensor(rx[:, 0, :, 0:4], gl, rx[:, 12, :, 0:1].broadcast_to([P, TB, 4]), ALU.subtract
                                ).then_inc(route_pre, 1)
                V.tensor_scalar(rx[:, 4, :, 0:4], rx[:, 3, :, 0:4], -NEG, NEG, ALU.mult, ALU.add)
                dve.drain()
                V.tensor_tensor(rx[:, 5, :, :].rearrange("p b (g e) -> p b g e", e=4),
                                lg[:, :, 4:20].rearrange("p b (g e) -> p b g e", e=4),
                                rx[:, 4, :, 0:4].unsqueeze(3).broadcast_to([P, TB, 4, 4]), ALU.add)
                dve.drain()
                first_max(rx[:, 5, :, :], 2, rx[:, 6, :, :], "desc16", 16, 3, rx[:, 7, :, :])
                V.tensor_scalar(rx[:, 8, :, :], rx[:, 7, :, :], NEG, None, ALU.mult)
                dve.drain()
                V.tensor_tensor(rx[:, 8, :, :], rx[:, 8, :, :], rx[:, 5, :, :], ALU.add)
                dve.drain()
                first_max(rx[:, 8, :, :], 4, rx[:, 6, :, :], "desc16", 16, 5, rx[:, 9, :, :])
                V.tensor_tensor(rx[:, 10, :, 0:1], rx[:, 12, :, 4:5], rx[:, 12, :, 2:3], ALU.subtract
                                ).then_inc(route_pre, 1)
                dve.wait_ge(route_exp, 1)
                V.tensor_reduce(rx[:, 12, :, 6:7], rx[:, 1, :, 0:4], AX.X, ALU.add)
                dve.wait_ge(route_exp, 2)
                V.tensor_scalar(rx[:, 12, :, 7:8], rx[:, 11, :, 0:1], 1.0, None, ALU.add)
                dve.drain()
                V.tensor_tensor(rx[:, 12, :, 7:8], rx[:, 12, :, 7:8], rx[:, 12, :, 6:7], ALU.mult)
                dve.drain()
                V.reciprocal(rx[:, 12, :, 8:9], rx[:, 12, :, 7:8])
                dve.drain()
                V.tensor_tensor(rx[:, 12, :, 9:10], rx[:, 12, :, 8:9], rx[:, 11, :, 0:1], ALU.mult)
                dve.drain()
                V.tensor_tensor(rx[:, 6, :, :], rx[:, 7, :, :], rx[:, 12, :, 8:9].broadcast_to([P, TB, 16]), ALU.mult)
                V.tensor_tensor(rx[:, 8, :, :], rx[:, 9, :, :], rx[:, 12, :, 9:10].broadcast_to([P, TB, 16]), ALU.mult)
                dve.drain()
                V.tensor_tensor(comb[:, :, :], rx[:, 6, :, :], rx[:, 8, :, :], ALU.add).then_inc(comb_done, 1)

            V.memset(eps[:, :], EPS).then_inc(eps_ready, 1)
            dve.wait_ge(params_loaded, N_PARAMS)
            for c in range(KC):
                dve.wait_ge(xt_full, c + 1)
                V.tensor_copy(x_T[:, c, :], turn[c % 2][:, :]).then_inc(x_final, 1)
            with dve.Fori(0, DEPTH) as l:
                norm(l * 3)
                slices(l, F1, 0, NSL, 0.5)
                norm(l * 3 + 1)
                mix(l)
                norm(l * 3 + 2)
                slices(l, F2, 2 * NSL, NSL, 0.5)

            norm(3 * L, x_T)
            norm(3 * L + 1)
            dve.wait_ge(rel_full, 1)
            V.tensor_tensor(rrow, turn[0][0:8, 0:384], cst("window_row", rows=8), ALU.add).then_inc(relrow_ready, 1)
            taken(dve, L, 0, T2["v", 3])
            taken(dve, L, 0, T2["v", 2])
            gx = [u_T[:, c, :] for c in range(4)] + [vtok[:, b, :] for b in range(TB)]
            gelu_pre_ops(gx[0], probs[:, 0, :])
            for j in range(8):
                t = probs[:, j % 2, :]
                if j + 1 < 8:
                    gelu_pre_ops(gx[j + 1], probs[:, (j + 1) % 2, :])
                dve.wait_ge(gelu_exp, 2 * L + j + 1)
                V.tensor_scalar(t, t, 1.0, None, ALU.add)
                dve.drain()
                V.reciprocal(t, t)
                dve.drain()
                V.tensor_tensor(gx[j], gx[j], t, ALU.mult)
            dve.drain()
            for b in range(TB):
                V.tensor_reduce(lnst[:, 0, b:b + 1], vtok[:, b, :], AX.X, ALU.add)
            dve.drain()
            V.tensor_scalar(lnst[:, 0, :], lnst[:, 0, :], 1.0 / 512, None, ALU.mult)
            dve.drain()
            for b in range(TB):
                V.tensor_scalar(vtok[:, b, :], vtok[:, b, :], lnst[:, 0, b:b + 1], None, ALU.subtract)
            dve.drain()
            for b in range(TB):
                dve.drain()
                V.tensor_tensor(probs[:, 0, :], vtok[:, b, :], vtok[:, b, :], ALU.mult)
                dve.drain()
                m = V.tensor_reduce(lnst[:, 1, b:b + 1], probs[:, 0, :], AX.X, ALU.add)
            m.then_inc(ln_pre, 1)
            dve.wait_ge(ln_rstd, 1)
            dve.wait_ge(ws_loaded, 32)
            for b in range(TB):
                m = V.scalar_tensor_tensor(vtok[:, b, :], vtok[:, b, :], lnst[:, 3, b:b + 1], gv, ALU.mult, ALU.mult)
            m.then_inc(vn_ready, 1)
            for n, (name, i, ld) in enumerate(SEC_T):
                ps = acc[n % 2]
                if name in ("wst", "sv", "pa", "pb", "wo", "route", "combt"):
                    dve.wait_ge(acc_full, full_at(L, 0, full2(n + 1)))
                if name == "gate":
                    taken(dve, L, 0, n)
                    t = (sig_a if i < 8 else sig_b)[:, i % 8, :]
                    V.tensor_scalar(t, t, 1.0, None, ALU.add)
                    dve.drain()
                    V.reciprocal(t, t)
                elif name == "wst":
                    V.tensor_tensor(ws_T[:, 4 * i:4 * i + 4, :], ps[:, :].rearrange("p (g t) -> p g t", t=P),
                                    cst("tril").unsqueeze(1).broadcast_to([P, 4, P]), ALU.mult
                                    ).then_inc(acc_free[n % 2], 1)
                elif name == "sv":
                    V.tensor_tensor(ab_T[:, i, :], ps[:, :], u_T[:, i, :], ALU.mult).then_inc(acc_free[n % 2], 1)
                elif (name, i) == ("swa", 0):
                    dve.wait_ge(bias_loaded, 16)
                    attend(L, NU, 0, NSW, swa_info, True)
                elif name == "pa":
                    V.tensor_tensor(sig_a[:, i, :], ps[:, :], sig_a[:, i, :], ALU.mult).then_inc(acc_free[n % 2], 1)
                elif name == "pb":
                    dve.drain()
                    V.tensor_tensor(rt[:, :], ps[:, :], sig_b[:, i, :], ALU.mult).then_inc(acc_free[n % 2], 1)
                    dve.drain()
                    V.tensor_tensor(sig_a[:, i, :], sig_a[:, i, :], rt[:, :], ALU.add).then_inc(merged_ready, 1)
                elif name == "wo":
                    V.tensor_tensor(x_T[:, i, :], ps[:, :], x_T[:, i, :], ALU.add).then_inc(acc_free[n % 2], 1)
                    dve.drain().then_inc(x_final, 1)
                    if i == KC - 1:
                        norm(3 * L + 2)
                elif name == "route":
                    route(n, ps)
                elif name == "combt":
                    V.tensor_copy(comb_T[:, :], ps[0:16, :]).then_inc(acc_free[n % 2], 1)
            slices(L, FMOE, 0, MOE_SLICES, 1.0, experts=True)
            norm(3 * L + 3)



def kernel(**inputs):
    import concourse.bacc as bacc
    from concourse.bass_utils import run_bass_kernel_spmd as run

    nc = bacc.Bacc("TRN2", target_bir_lowering=False, num_devices=1)
    arrays, args = {}, {}
    tensors = {**inputs, "const": constant_table()}
    for name, value in tensors.items():
        v = np.ascontiguousarray(value)
        arrays[f"in_{name}"] = v
        args[name] = nc.dram_tensor(f"in_{name}", v.shape, mybir.dt.from_np(v.dtype), kind="ExternalInput").ap()
    out = nc.dram_tensor("out", (1, S, D), F32, kind="ExternalOutput").ap()
    build(nc, args, out)
    r = run(nc, [arrays], core_ids=[0])
    return r.results[0]["out"]
```

```python
from contextlib import ExitStack

import numpy as np

import concourse.bass as bass
from concourse import mybir

ALU = mybir.AluOpType
ACT = mybir.ActivationFunctionType
AX = mybir.AxisListType
F32 = mybir.dt.float32

P = 128
S = 512
D = 1024
KC = D // P
TB = S // P
EPS = 1e-6
NEG = -1e30
DEPTH = 2
D_FF = 2816
FS = 256
GC = 0.7978845608028654
HD = 64

C_CQ, C_CKV, C_KR, C_NQ, C_KC, C_VC, C_KS, C_VS, C_KW, C_VW, C_G, C_SQ, C_SK, C_SV, C_END = (
    int(v) for v in np.cumsum([0, 256, 128, 32, 384, 128, 128, 128, 128, 128, 128, 18, 256, 256, 256]))

_CONST = {}
_CN = 0
for _name, _n in (("ident", 128), ("ones", 128), ("negones", 128), ("negtri", 128), ("causal", 128),
                  ("strict", 128), ("tril", 128), ("r_mla", 96), ("r_nsa", 128), ("cos_mla", 512),
                  ("sin_mla", 512), ("cos_nsa", 512), ("sin_nsa", 512), ("cmp_mask", 4 * 31),
                  ("cmp_valid", 4), ("desc4", 4), ("desc16", 16), ("group_rows", 4 * 128),
                  ("bucket_rows", 384), ("window_row", 384), ("iota", 512), ("slot_number", 4)):
    _CONST[_name] = (_CN, _CN + _n)
    _CN += _n


def constant_table():
    t = np.zeros((P, _CN), np.float32)

    def put(name, a):
        a = np.asarray(a, np.float32)
        t[:a.shape[0], _CONST[name][0]:_CONST[name][0] + a.shape[1]] = a

    r = np.arange(P)
    put("ident", np.eye(P))
    put("ones", np.ones((P, P)))
    put("negones", -np.ones((P, P)))
    put("negtri", -1.0 * (r[:, None] >= r[None, :]))
    put("causal", np.where(r[None, :] <= r[:, None], 0.0, NEG))
    put("strict", r[:, None] < r[None, :])
    put("tril", r[:, None] <= r[None, :])
    pos = np.arange(S, dtype=np.float32)

    def rope(rows, start, half):
        freq = np.float32(500000.0) ** (-np.arange(half, dtype=np.float32) / np.float32(half))
        ang = (pos[:, None] * freq[None, :].astype(np.float32)).astype(np.float32).T
        rot = np.zeros((rows, rows), np.float32)
        c, s = np.ones((rows, S), np.float32), np.zeros((rows, S), np.float32)
        for b in start:
            for i in range(half):
                rot[b + half + i, b + i] = -1.0
                rot[b + i, b + half + i] = 1.0
            c[b:b + 2 * half] = np.concatenate([np.cos(ang), np.cos(ang)])
            s[b:b + 2 * half] = np.concatenate([np.sin(ang), np.sin(ang)])
        return rot, c, s

    for name, args in (("mla", (96, (64,), 16)), ("nsa", (128, (0, 64), 8))):
        rot, c, s = rope(*args)
        put("r_" + name, rot)
        put("cos_" + name, c)
        put("sin_" + name, s)
    q = (np.arange(TB)[None, :, None] * P + r[:, None, None])
    put("cmp_mask", np.where(np.arange(31)[None, None, :] * 16 + 31 <= q, 0.0, NEG).reshape(P, -1))
    put("cmp_valid", (q[:, :, 0] >= 31))
    put("desc4", np.tile(4.0 - np.arange(4), (P, 1)))
    put("desc16", np.tile(16.0 - np.arange(16), (P, 1)))
    g = np.zeros((8, 4, 128), np.float32)
    for i in range(8):
        g[i, i // 2, (i % 2) * 64:(i % 2) * 64 + 64] = 1.0
    put("group_rows", g.reshape(8, -1))
    dist = 255 - np.arange(384)
    ok = (dist >= 0) & (dist < 128)
    nf = np.maximum(dist, 1).astype(np.float32)
    large = 16 + (np.log(nf / np.float32(16)) / np.float32(np.log(8.0)) * np.float32(16)).astype(np.int32)
    bucket = np.where(dist < 16, dist, np.minimum(large, 31))
    rows = np.zeros((32, 384), np.float32)
    for j in range(384):
        if ok[j]:
            rows[bucket[j], j] = 1.0
    put("bucket_rows", rows)
    put("iota", np.tile(np.arange(S), (P, 1)))
    put("slot_number", r[:, None] + P * np.arange(S // P)[None, :])
    put("window_row", np.tile(np.where(ok, 0.0, NEG), (8, 1)))
    return t


MIX = (
    [("cq", 0, 0, "act"), ("cq", 1, 0, "act"), ("ckv", 0, 1, "act"), ("kr", 0, 1, "act")]
    + [("nq", 0, 2, "act"), ("nq", 1, 2, "act"), ("nq", 2, 3, "act"), ("kc", 0, 3, "act")]
    + [("vc", 0, 4, "act"), ("ks", 0, 4, "act"), ("vs", 0, 5, "act"), ("kw", 0, 5, "act")]
    + [("vw", 0, 6, "act"), ("gate", 0, 6, "dve")]
    + [("sq", 0, 7, "act"), ("sq", 1, 7, "act"), ("sk", 0, 8, "act"), ("sk", 1, 8, "act")]
    + [("sv", 0, 9, "act"), ("sv", 1, 9, "act")]
    + [("uq", h, 10, "act") for h in range(6)]
    + [("kn", h, 11, "act") for h in range(6)]
    + [("mv", b, 11, "act") for b in range(TB)]
    + [("xs_v", g, None, "act") for g in range(2)]
    + [("rope", i, None, "dve") for i in (10, 0, 1, 2, 3)]
    + [("xs_k", g, None, "act") for g in range(2)]
    + [("rope", i, None, "dve") for i in (4, 5, 6, 7, 8, 9, 11, 12)]
    + [("hid_k", 0, 12, "dve"), ("hid_v", 0, 13, "dve"), ("cmp", 0, None, "act")]
)
TICKET = {(j[0], j[1]): i for i, j in enumerate(MIX)}
HEADS = [("mla", h) for h in range(6)] + [("nsa", h) for h in range(6)]
SB_HEADS = 4
T_LIN = len(MIX)
T_HEAD = T_LIN + len(HEADS) + SB_HEADS
T_MIX = T_HEAD + KC
NSL = D_FF // FS
T_FF = NSL * KC
TL = 2 * T_FF + T_MIX
assert T_MIX % 2 == 0 and T_FF % 2 == 0
NHD = len(HEADS)
TLF = TL - NHD
LAST_TICKET = {}
for _i, _j in enumerate(MIX):
    if _j[2] is not None:
        LAST_TICKET[_j[2]] = _i

MIX_DMAS = [1, 1, 4, 3, 1, 1, 1, 1, 1, 1, 1, 1, 2, 2, 1, 1, 1, 1]
W_OUT0 = 14
NLM = len(MIX_DMAS)
W_DONE = {n % 3: T_HEAD + 2 * (n - W_OUT0) + 2 for n in range(W_OUT0, NLM)}
SLOT_DMAS = [2 * NSL + sum(MIX_DMAS[s::3]) for s in range(3)]

SB_PLACE = {0: (0, 0), 1: (1, P), 2: (2, 0), 3: (1, 0)}
UNITS = []
for _kind, _h in HEADS:
    for _i in range(TB):
        br = ["mla"] if _kind == "mla" else ["cmp", "sel", "win"]
        for _b in br:
            UNITS.append((_kind, _h, _i, _b, _b == br[0], _b == br[-1]))
NU = len(UNITS)
NSA_HALF = lambda h: (h // 3, h % 3)

SWA_UNITS = [(h, i) for h in range(8) for i in range(TB)]
NX = 16
XF = 512


def run_slices(eng, n, up_step, down_step):
    up_step(0, 0)
    with eng.Fori(0, (n - 1) // 2) as i:
        up_step(i * 2 + 1, 1)
        down_step(i * 2, 0, False)
        up_step(i * 2 + 2, 0)
        down_step(i * 2 + 1, 1, False)
    if n % 2 == 0:
        up_step(n - 1, 1)
        down_step(n - 2, 0, False)
    down_step(n - 1, (n - 1) % 2, True)


def build(nc, a, out):
    with ExitStack() as ctx:
        def sb(name, shape):
            return ctx.enter_context(nc.sbuf_tensor(name, shape, F32))

        def sem(name):
            return ctx.enter_context(nc.semaphore(name))

        const = sb("const", [P, _CN])

        def cst(name, rows=P, lo=0, hi=None):
            c0, c1 = _CONST[name]
            return const[0:rows, c0 + lo:(c1 if hi is None else c0 + hi)]

        ident = cst("ident")
        x_T = sb("x_T", [P, KC, S])
        h_T = sb("h_T", [P, KC, S])
        o_T = sb("o_T", [P, KC, S])
        slot = [sb(f"weights{s}", [P, 2048]) for s in range(3)]
        hid = sb("hid", [P, 4, S])
        et = sb("exp_tile", [P, 2, S])
        rt = sb("recip_tile", [P, S])
        lora = sb("lora", [P, 4, S])
        rstd = sb("rstd", [P, S])
        arena = sb("arena", [P, 18000])
        probs = sb("probs", [P, 3, S])
        probs_T = sb("probs_T", [P, 2, S])
        gains = sb("gains", [P, 3 * DEPTH + 4, KC])
        lgains = sb("lora_gains", [P, DEPTH, 3])
        gbias = sb("gate_bias", [P, DEPTH, 18])
        cmp_w2 = sb("cmp_w2", [P, 2, HD])
        cmp_pos = sb("cmp_pos", [P, 2, 16])
        hid_cmp = sb("hid_cmp", [P, 2, 62])
        cmp_t = sb("cmp_t", [P, 4, 62])
        bias_c = sb("bias_c", [P, 2])
        stats = sb("stats", [P, 4, 4])
        gates = sb("gates", [P, TB, 18])
        gates_e = sb("gates_e", [P, TB, 18])
        vcmp = sb("vcmp", [31, 2, HD])
        kcmp_T = sb("kcmp_T", [P, 31])
        lnst = sb("lnst", [P, 4, TB])
        sinks = sb("sinks", [P, 8])
        rel = sb("rel", [32, 8])
        bs = sb("bs", [8, P])
        rw = sb("rw", [P, KC, 20])
        rb = sb("rb", [P, 20])
        lg = sb("lg", [P, TB, 20])
        rx = sb("rx", [P, 14, TB, 16])
        comb = sb("comb", [P, TB, 16])
        member = sb("member", [P, TB, 16])
        rank = sb("rank", [P, TB, 16])
        passes = sb("passes", [P, 2])
        n_passes = ctx.enter_context(nc.sbuf_tensor("n_passes", [P, 1], mybir.dt.int32))
        eps = sb("eps", [P, 1])

        off = [0]

        def view(*dims):
            n = int(np.prod(dims))
            v = arena[:, off[0]:off[0] + n]
            off[0] += n
            if len(dims) == 2:
                v = v.rearrange("p (a b) -> p a b", b=dims[1])
            return v

        q6 = view(6, S)
        k6 = view(6, S)
        mv = view(TB, 384)
        nq = view(3, S)
        nk = view(4, S)
        vs = view(TB, P)
        vw = view(TB, P)
        sq_T = view(2, S)
        sk_T = view(2, S)
        sv = view(TB, 256)
        pairs = [view(2, S), view(2, S)]
        assert off[0] <= 18000, off[0]
        off[0] = 0
        u_T = view(4, S)
        vtok = view(TB, S)
        q2 = view(4, S)
        k2 = view(S)
        v2 = view(TB, P)
        sig_a = view(KC, S)
        sig_b = o_T
        bias_t = view(8, 256)
        gv = view(S)
        ab_T = view(8, S)
        assert off[0] <= 18000, off[0]
        ws_T = lora[:, 0:2, :].rearrange("p a (b c) -> p (a b) c", c=P)
        ws_n = lora[:, 2:4, :].rearrange("p a (b c) -> p (a b) c", c=P)
        rrow = rt[0:8, 0:384]
        big = [arena[:, k * 4096:(k + 1) * 4096].rearrange("p (c f) -> p c f", f=XF) for k in range(4)]
        xg_w, xu_w = [big[0], big[2]], [big[1], big[3]]
        xd = ([t[:, :].rearrange("p (c d) -> p c d", d=D) for t in slot]
              + [h_T[:, 0:4, :].rearrange("p a b -> p (a b)").rearrange("p (c d) -> p c d", d=D)])
        xd_w = [xd[0:2], xd[2:4]]
        h_tok = o_T[:, :, :].rearrange("p a b -> p (a b)").rearrange("p (b d) -> p b d", d=D)
        mine_T = [h_T[:, 4 + 2 * q:6 + 2 * q, :].rearrange("p a (c t) -> p (a c) t", t=P) for q in range(2)]
        pick = [lora[:, q, :].rearrange("p (b t) -> p b t", t=P) for q in range(2)]
        place = [lora[:, 2 + q, :] for q in range(2)]
        rows = [probs_T[:, :, :], arena[:, 16384:16384 + 2 * S].rearrange("p (a t) -> p a t", t=S)]
        rows_T = hid[0:16, 2:4, :]
        xhid, xhid_T, y_slot = hid[:, 0, :], hid[:, 1, :], hid[:, 2:4, :]

        acc = [ctx.enter_context(nc.psum_tensor(f"acc{i}", [P, S], F32)) for i in range(2)]
        score = [ctx.enter_context(nc.psum_tensor(f"score{i}", [P, S], F32)) for i in range(4)]
        turn = [ctx.enter_context(nc.psum_tensor(f"turn{i}", [P, S], F32)) for i in range(2)]

        sb_bank = [score[0:3], [score[3], turn[0], turn[1]]]
        sb_a = [lora, probs]
        sb_e = q6

        def sb_cols(t, j, lo, hi):
            b, o = SB_PLACE[j]
            return t[:, b, o + lo:o + hi]

        SB_BANKS = ((0, S), (1, S), (2, 2 * P))

        rel_dram = nc.dram_tensor("rel_scratch", [8, P, 384], F32, kind="Internal").ap()
        rows_dram = nc.dram_tensor("rows_scratch", [16, 2, S], F32, kind="Internal").ap()

        params_loaded = sem("params_loaded")
        x_loaded = sem("x_loaded")
        w_loaded = [sem(f"w_loaded{s}") for s in range(3)]
        small_loaded = sem("small_loaded")
        acc_full = sem("acc_full")
        acc_free = [sem(f"acc_free{i}") for i in range(2)]
        x_final = sem("x_final")
        squared = sem("squared")
        summed = sem("summed")
        ssq_full = sem("ssq_full")
        rstd_ready = sem("rstd_ready")
        h_ready = sem("h_ready")
        gu_full = sem("gu_full")
        sig_ready = sem("sig_ready")
        hid_done = sem("hid_done")
        lsq_ready = sem("lsq_ready")
        lssq_full = sem("lssq_full")
        lrstd_ready = sem("lrstd_ready")
        lora_ready = sem("lora_ready")
        rope_ready = sem("rope_ready")
        gate_exp = sem("gate_exp")
        gelu_pre = sem("gelu_pre")
        gelu_exp = sem("gelu_exp")
        hidc_ready = sem("hidc_ready")
        s_full = sem("s_full")
        max_ready = sem("max_ready")
        exp_ready = sem("exp_ready")
        p_ready = sem("p_ready")
        t_full = sem("t_full")
        pt_ready = sem("pt_ready")
        pv_done = sem("pv_done")
        z_full = sem("z_full")
        log_ready = sem("log_ready")
        sp_ready = sem("sp_ready")
        suffix_full = sem("suffix_full")
        a_exp = sem("a_exp")
        a_ready = sem("a_ready")
        eps_ready = sem("eps_ready")
        rel_full = sem("rel_full")
        comb_done = sem("comb_done")
        yt_full = sem("yt_full")
        xt_full = sem("xt_full")
        turned = sem("turned")
        g2_pre = sem("g2_pre")
        g2_exp = sem("g2_exp")
        ln_pre = sem("ln_pre")
        ln_rstd = sem("ln_rstd")
        vn_ready = sem("vn_ready")
        ws_loaded = sem("ws_loaded")
        ws_ready = sem("ws_ready")
        relrow_ready = sem("relrow_ready")
        rel_stored = sem("rel_stored")
        bias_loaded = sem("bias_loaded")
        merged_ready = sem("merged_ready")
        route_pre = sem("route_pre")
        route_exp = sem("route_exp")
        rows_stored = sem("rows_stored")
        member_ready = sem("member_ready")
        rank_ready = sem("rank_ready")
        passes_ready = sem("passes_ready")
        htok_full = sem("htok_full")
        htok_ready = sem("htok_ready")
        xgate_loaded = [sem(f"xgate_loaded{i}") for i in range(2)]
        xup_loaded = [sem(f"xup_loaded{i}") for i in range(2)]
        xdown_loaded = [sem(f"xdown_loaded{i}") for i in range(2)]
        rows_loaded = [sem(f"rows_loaded{i}") for i in range(2)]
        pick_ready = sem("pick_ready")
        gathered = sem("gathered")
        mine_ready = sem("mine_ready")
        xgu_full = sem("xgu_full")
        xsig_ready = sem("xsig_ready")
        xhid_ready = sem("xhid_ready")
        xhid_turned = sem("xhid_turned")
        xhidt_ready = sem("xhidt_ready")
        xdown_full = sem("xdown_full")
        yslot_ready = sem("yslot_ready")
        place_ready = sem("place_ready")
        scattered = sem("scattered")
        scatter_taken = sem("scatter_taken")
        y_ready = sem("y_ready")
        y_stored = sem("y_stored")

        def at(l, per_layer, n):
            return l * per_layer + n

        B1, BM, B2 = 0, T_FF, T_FF + T_MIX
        F1, FM, F2 = 0, T_FF, T_FF + T_MIX - NHD
        TG = 4 * NSL
        def full_at(l, base, n):
            return at(l, TLF, base + n + 1)

        def mix_full(l, n):
            return full_at(l, FM, n if n <= T_LIN else n - NHD)

        def free_at(l, base, n):
            return at(l, TL // 2, base // 2 + n // 2 + 1)

        def gu_at(l, base, n):
            return at(l, TG, base + n + 1)

        def dmajor(name, p=P):
            return a[name].rearrange("l (c p) f -> l p c f", p=p)

        w_gate = [dmajor("ffn1_w_gate"), dmajor("ffn2_w_gate")]
        w_up = [dmajor("ffn1_w_up"), dmajor("ffn2_w_up")]
        w_down = [dmajor("ffn1_w_down"), dmajor("ffn2_w_down")]
        w_in, w_out = dmajor("w_in"), dmajor("w_out")
        w_uq, w_ukv = dmajor("mla_w_uq"), dmajor("mla_w_ukv")
        x_tok = a["x"].rearrange("a (b p) d -> p (a b) d", p=P)
        y_tok = out.rearrange("a (b p) d -> p (a b) d", p=P)
        x_in = arena[:, 0:4096].rearrange("p (b d) -> p b d", d=D)
        y_out = x_in
        w_in2, w_out2 = dmajor("w_in_2")[0], dmajor("w_out_2")[0]
        w_pa, w_pb = dmajor("w_proj_a_2")[0], dmajor("w_proj_b_2")[0]
        x_gate = a["expert_w_gate_2"].rearrange("a e (c p) f -> (a e) p c f", p=P)
        x_up = a["expert_w_up_2"].rearrange("a e (c p) f -> (a e) p c f", p=P)
        x_down = a["expert_w_down_2"].rearrange("a e (c p) f -> (a e) p c f", p=P)

        def s3(s, c, n):
            return slot[s][:, 0:c * n].rearrange("p (c n) -> p c n", n=n)

        SECOND = ([("u", 0), ("u", 256), ("v", 0), ("v", 256), ("q", 0), ("q", 256), ("kv", 0)]
                  + [("gate", c) for c in range(0, 2048, 256)]
                  + [("pa", 0), ("pa", 512), ("pb", 0), ("pb", 512)]
                  + [("wo", c) for c in range(0, 1024, 256)])
        SEC_DMAS = [4 if n == "q" else 1 for n, _ in SECOND]
        NSEC = len(SECOND)

        SEC_T = ([("u", c, c // 2) for c in range(4)]
                 + [("v", b, 2 + b // 2) for b in range(4)]
                 + [("q", c, 4 + c // 2) for c in range(4)] + [("k", 0, 6), ("vtok", 0, 6)]
                 + [("gate", c, 7 + c // 2) for c in range(16)]
                 + [("wst", b, None) for b in range(2)]
                 + [("sv", c, None) for c in range(4)]
                 + [("swa", h, None) for h in range(8)]
                 + [("pa", c, 15 + c // 4) for c in range(8)]
                 + [("pb", c, 17 + c // 4) for c in range(8)]
                 + [("wo", c, 19 + c // 2) for c in range(8)]
                 + [("route", 0, None), ("rank", 0, None), ("combt", 0, None), ("rankt", 0, None)])
        NT2 = len(SEC_T)
        assert NT2 % 2 == 0 and NSEC % 3 == 2
        T2 = {(n, i): j for j, (n, i, _) in enumerate(SEC_T)}
        LAST2 = {ld: j for j, (_, _, ld) in enumerate(SEC_T) if ld is not None}
        SWA0 = T2["swa", 0]

        def full2(n):
            return n - max(0, min(n - SWA0, 8))

        block = ctx.enter_context(nc.Block())

        @block.sync
        def _(sp):
            sp.dma_start(const[:, :], a["const"]).then_inc(params_loaded, 16)
            sp.dma_start(x_in, x_tok).then_inc(x_loaded, 16)
            with nc.allow_non_contiguous_dma(reason="small parameter vectors, once"):
                for i, name in enumerate(("ffn1_norm", "mix_norm", "ffn2_norm")):
                    for l in range(DEPTH):
                        sp.dma_start(gains[:, 3 * l + i, :],
                                     a[name][l].rearrange("(c p) -> p c", p=P)).then_inc(params_loaded, 16)
                for i, name in enumerate(("attn_norm_g_2", "ffn_norm_g_2")):
                    sp.dma_start(gains[:, 3 * DEPTH + 1 + i, :],
                                 a[name][0].rearrange("(c p) -> p c", p=P)).then_inc(params_loaded, 16)
                for i, name in ((0, "final_norm"), (3, "final_norm_g_2")):
                    sp.dma_start(gains[:, 3 * DEPTH + i, :],
                                 a[name].rearrange("(c p) -> p c", p=P)).then_inc(params_loaded, 16)
                for l in range(DEPTH):
                    sp.dma_start(lgains[:, l, 0:2],
                                 a["mla_q_norm"][l].rearrange("(c p) -> p c", p=P)).then_inc(params_loaded, 16)
                    sp.dma_start(lgains[:, l, 2:3],
                                 a["mla_kv_norm"][l].rearrange("(c p) -> p c", p=P)).then_inc(params_loaded, 16)
                sp.dma_start(gbias[:, :, :],
                             a["nsa_gate_bias"].partition_broadcast(P)).then_inc(params_loaded, 16)
                sp.dma_start(sinks[:, :],
                             a["attn_sinks_2"][0].partition_broadcast(P)).then_inc(params_loaded, 16)
                sp.dma_start(rel[:, :], a["rel_bias_2"]).then_inc(params_loaded, 16)
                sp.dma_start(bs[:, :], a["gm_b_spatial_2"][0]).then_inc(params_loaded, 16)
                sp.dma_start(rb[:, 0:4], a["router_group_b_2"][0].partition_broadcast(P)).then_inc(params_loaded, 16)
                sp.dma_start(rb[:, 4:20], a["router_expert_b_2"][0].rearrange("g e -> (g e)")
                             .partition_broadcast(P)).then_inc(params_loaded, 16)
                sp.dma_start(rw[:, :, 0:4],
                             a["router_group_w_2"][0].rearrange("(c p) g -> p c g", p=P)).then_inc(params_loaded, 16)
                for g in range(4):
                    sp.dma_start(rw[:, :, 4 + 4 * g:8 + 4 * g],
                                 a["router_expert_w_2"][0, g].rearrange("(c p) e -> p c e", p=P)
                                 ).then_inc(params_loaded, 16)

            def ffn(l, ph):
                gub, fb = ph * 2 * NSL, (F1, F2)[ph]

                def up(sl, par):
                    for s, w in ((0, w_gate), (1, w_up)):
                        if not isinstance(sl, int) or sl > 0:
                            sp.wait_ge(gu_full, gu_at(l, gub, sl * 2))
                        elif ph == 0:
                            sp.wait_ge(gu_full, gu_at(l, 0, 0))
                        else:
                            sp.wait_ge(acc_full, mix_full(l, W_DONE[s]))
                        sp.dma_start(s3(s, KC, FS), w[ph][l][:, :, bass.ds(sl * FS, FS)]).then_inc(w_loaded[s], 16)

                def down(sl, par, last):
                    if not isinstance(sl, int) or sl > 0:
                        sp.wait_ge(acc_full, full_at(l, fb, sl * KC))
                    elif ph == 0:
                        sp.wait_ge(acc_full, full_at(l, 0, 0))
                    else:
                        sp.wait_ge(acc_full, mix_full(l, W_DONE[2]))
                    sp.dma_start(s3(2, 2, D), w_down[ph][l][:, bass.ds(sl * 2, 2), :]).then_inc(w_loaded[2], 16)

                run_slices(sp, NSL, up, down)

            def mix_loads(l):
                wi = w_in[l]

                def cols(s, c0, n, at_=0, w=256):
                    sp.dma_start(s3(s, KC, w)[:, :, at_:at_ + n], wi[:, :, c0:c0 + n]).then_inc(w_loaded[s], 16)

                for n in range(NLM):
                    s = n % 3
                    if n < 2:
                        sp.wait_ge(gu_full, gu_at(l, 2 * NSL, 0))
                    elif n == 2:
                        sp.wait_ge(acc_full, mix_full(l, 0))
                    else:
                        o = n - 3
                        sp.wait_ge(acc_full, mix_full(l, (LAST_TICKET[o] if o < W_OUT0 else
                                                          T_HEAD + 2 * (o - W_OUT0) + 1) + 1))
                    if n == 0:
                        cols(s, C_CQ, 256)
                    elif n == 1:
                        cols(s, C_CKV, 160, w=160)
                    elif n == 2:
                        for c in range(2):
                            for g in range(2):
                                cols(s, C_NQ + HD * (3 * g + c), HD, at_=128 * c + 64 * g)
                    elif n == 3:
                        for g in range(2):
                            cols(s, C_NQ + HD * (3 * g + 2), HD, at_=64 * g)
                        cols(s, C_KC, 128, at_=128)
                    elif n == 4:
                        cols(s, C_VC, 256)
                    elif n == 5:
                        cols(s, C_VS, 256)
                    elif n == 6:
                        cols(s, C_VW, 146, w=146)
                    elif n == 7:
                        cols(s, C_SQ, 256)
                    elif n == 8:
                        cols(s, C_SK, 256)
                    elif n == 9:
                        cols(s, C_SV, 256)
                    elif n == 10:
                        sp.dma_start(s3(s, 2, 576), w_uq[l]).then_inc(w_loaded[s], 16)
                    elif n == 11:
                        sp.dma_start(s3(s, 1, 768), w_ukv[l]).then_inc(w_loaded[s], 16)
                    elif n < W_OUT0:
                        w1 = a["nsa_cmp_w1_k" if n == 12 else "nsa_cmp_w1_v"][l].rearrange("(c q d) j -> q d c j", q=2, d=HD)
                        for q in range(2):
                            sp.dma_start(s3(s, 16, P)[q * HD:(q + 1) * HD], w1[q]).then_inc(w_loaded[s], 16)
                    else:
                        sp.dma_start(s3(s, KC, 256), w_out[l][:, :, (n - W_OUT0) * 256:(n - W_OUT0 + 1) * 256]
                                     ).then_inc(w_loaded[s], 16)

            with sp.Fori(0, DEPTH) as l:
                sp.wait_ge(acc_full, full_at(l, 0, 0))
                with nc.allow_non_contiguous_dma(reason="small parameters"):
                    sp.dma_start(cmp_w2[:, 0, :], a["nsa_cmp_w2_k"][l]).then_inc(small_loaded, 16)
                    sp.dma_start(cmp_w2[:, 1, :], a["nsa_cmp_w2_v"][l]).then_inc(small_loaded, 16)
                    sp.dma_start(cmp_pos[:, 0, :], a["nsa_cmp_pos_k"][l].rearrange("(c q) d -> (q d) c", q=2)
                                 ).then_inc(small_loaded, 16)
                    sp.dma_start(cmp_pos[:, 1, :], a["nsa_cmp_pos_v"][l].rearrange("(c q) d -> (q d) c", q=2)
                                 ).then_inc(small_loaded, 16)
                ffn(l, 0)
                mix_loads(l)
                ffn(l, 1)

            L = DEPTH
            sp.wait_ge(x_final, KC * 3 * DEPTH)
            sp.dma_start(ws_n, a["gm_w_spatial_2"][0].rearrange("g t s -> t g s")).then_inc(ws_loaded, 16)
            sp.dma_start(gv, a["gm_v_norm_g_2"][0].partition_broadcast(P)).then_inc(ws_loaded, 16)
            for n, (name, c0) in enumerate(SECOND):
                s = n % 3
                if n < 2:
                    sp.wait_ge(gu_full, gu_at(L, 0, 0))
                elif n == 2:
                    sp.wait_ge(acc_full, full_at(L, 0, 0))
                else:
                    sp.wait_ge(acc_full, full_at(L, 0, full2(LAST2[n - 3] + 1)))
                if name == "q":
                    for c in range(2):
                        for g in range(2):
                            h = c0 // 128 + c + 4 * g
                            sp.dma_start(s3(s, KC, 256)[:, :, 128 * c + 64 * g:128 * c + 64 * g + 64],
                                         w_in2[:, :, 1024 + HD * h:1024 + HD * h + HD]).then_inc(w_loaded[s], 16)
                elif name in ("pa", "pb"):
                    sp.dma_start(s3(s, 4, 512), (w_pa if name == "pa" else w_pb)[:, :, c0:c0 + 512]
                                 ).then_inc(w_loaded[s], 16)
                elif name == "wo":
                    sp.dma_start(s3(s, KC, 256), w_out2[:, :, c0:c0 + 256]).then_inc(w_loaded[s], 16)
                else:
                    first = {"u": 0, "v": 512, "kv": 1536, "gate": 1792}[name]
                    sp.dma_start(s3(s, KC, 256), w_in2[:, :, first + c0:first + c0 + 256]
                                 ).then_inc(w_loaded[s], 16)
                if n == 6:
                    sp.wait_ge(relrow_ready, 1)
                    sp.dma_start(rel_dram, rrow.unsqueeze(1).broadcast_to([8, P, 384])).then_inc(rel_stored, 16)
                    sp.wait_ge(rel_stored, 16)
                    sp.dma_start(bias_t, bass.AP(rel_dram.tensor, 127, [[383, P], [384 * P, 8], [1, 256]])
                                 ).then_inc(bias_loaded, 16)
            sp.wait_ge(acc_full, full_at(L, 0, full2(T2["wo", KC - 1] + 1)))

            def x_weights(e, n, q):
                sp.wait_ge(xgu_full, n + 1)
                sp.dma_start(xg_w[q], x_gate[e]).then_inc(xgate_loaded[q], 16)
                sp.dma_start(xu_w[q], x_up[e]).then_inc(xup_loaded[q], 16)

            def x_rest(e, n, q):
                sp.wait_ge(xdown_full, n + 1)
                for t in range(2):
                    sp.dma_start(xd_w[q][t], x_down[e][:, 2 * t:2 * t + 2, :]).then_inc(xdown_loaded[q], 16)
                sp.wait_ge(place_ready, n + 1)
                sp.dma_start(rows[q],
                             rows_dram[bass.ds(e, 1)][0].partition_broadcast(P)).then_inc(rows_loaded[q], 16)

            x_weights(0, 0, 0)
            for q in range(2):
                n = T2["combt" if q == 0 else "rankt", 0]
                sp.wait_ge(acc_free[n % 2], free_at(L, 0, n + 2))
            sp.dma_start(rows_dram, rows_T).then_inc(rows_stored, 16)
            sp.wait_ge(rows_stored, 16)
            sp.wait_ge(htok_ready, 2 * TB)
            sp.wait_ge(passes_ready, 1)
            n_p = sp.value_load(n_passes[0:1, 0:1], min_val=1, max_val=TB)
            x_rest(0, 0, 0)
            x_weights(1, 1, 1)
            x_rest(1, 1, 1)
            with sp.Fori(2, NX // 2 + 1) as i:
                for q in range(2):
                    x_weights(i * 2 + (q - 2), i * 2 + (q - 2), q)
                    x_rest(i * 2 + (q - 2), i * 2 + (q - 2), q)
            with sp.If(n_p > 1):
                with sp.Fori(1, n_p) as ps_:
                    with sp.Fori(1, NX // 2 + 1) as i:
                        n = sp.snap(ps_ * NX + i * 2)
                        for q in range(2):
                            x_weights(i * 2 + (q - 2), n + (q - 2), q)
                            x_rest(i * 2 + (q - 2), n + (q - 2), q)

            for b in range(TB):
                sp.wait_ge(y_ready, 2 * b + 2)
                sp.dma_start(y_tok[:, b, :], y_out[:, b, :]).then_inc(y_stored, 16)
            sp.wait_ge(y_stored, 16 * TB)

        N_PARAMS = 16 * (1 + 3 * DEPTH + 4 + 2 * DEPTH + 11)
        L = DEPTH
        OUT_HEADS = [("mla", h) for h in range(6)] + [("nsa", h) for h in range(6)]
        ROPES = ([(q6[0:96, h, :], "mla", ("uq", h)) for h in range(6)]
                 + [(lora[0:96, 3, :], "mla", ("kr", 0))]
                 + [(nq[:, c, :], "nsa", ("nq", c)) for c in range(3)]
                 + [(nk[:, i, :], "nsa", (n, 0)) for i, n in enumerate(("kc", "ks", "kw"))])
        EVAC = {("cq", 0): (lora[:, 0, :], 1.0), ("cq", 1): (lora[:, 1, :], 1.0), ("ckv", 0): (lora[:, 2, :], 1.0),
                ("kr", 0): (lora[0:96, 3, :], 1.0), ("kc", 0): (nk[:, 0, :], 1.0), ("ks", 0): (nk[:, 1, :], 1.0),
                ("kw", 0): (nk[:, 2, :], 1.0), ("vc", 0): (nk[:, 3, :], 1.0),
                ("vs", 0): (vs.rearrange("p a b -> p (a b)"), 1.0), ("vw", 0): (vw.rearrange("p a b -> p (a b)"), 1.0)}
        for i in range(3):
            EVAC["nq", i] = (nq[:, i, :], HD ** -0.5)
        for i in range(2):
            EVAC["sq", i] = (sq_T[:, i, :], HD ** -0.5)
            EVAC["sk", i] = (sk_T[:, i, :], 1.0)
            EVAC["sv", i] = (sv[:, 2 * i:2 * i + 2, :].rearrange("p a b -> p (a b)"), 1.0)
            EVAC["xs_k", i] = (pairs[0][:, i, :], 1.0)
            EVAC["xs_v", i] = (pairs[1][:, i, :], 1.0)
        for i in range(6):
            EVAC["uq", i] = (q6[0:96, i, :], 96.0 ** -0.5)
            EVAC["kn", i] = (k6[0:HD, i, :], 1.0)
        for i in range(TB):
            EVAC["mv", i] = (mv[:, i, :], 1.0)

        def taken(eng, l, base, n):
            eng.wait_ge(acc_free[n % 2], free_at(l, base, n + 2))

        def unit_info(n):
            kind, h, i, br, first, last = UNITS[n]
            blk = slice(i * P, (i + 1) * P)
            w = (i + 1) * P
            if kind == "mla":
                q, k = q6[0:96, h, blk], k6[0:96, h, 0:w]
                v = [mv[:, j, h * HD:(h + 1) * HD] for j in range(i + 1)]
            else:
                g, c = NSA_HALF(h)
                r = slice(g * HD, (g + 1) * HD)
                q = nq[r, c, blk]
                if br == "cmp":
                    w = 31
                    k, v = kcmp_T[r, :], [vcmp[:, g, :]]
                else:
                    k = nk[r, 1 if br == "sel" else 2, 0:w]
                    vt = vs if br == "sel" else vw
                    v = [vt[:, j, g * HD:(g + 1) * HD] for j in range(i + 1)]
            return dict(q=q, k=k, v=v, w=w, i=i, h=h, br=br, first=first, last=last,
                        out=slice((h % 2) * HD, (h % 2) * HD + HD), blk=blk,
                        head=(0 if kind == "mla" else 6) + h,
                        end=last and i == TB - 1, begin=first and i == 0)

        def swa_info(n):
            h, i = SWA_UNITS[n]
            g, c = h // 4, h % 4
            lo = max(0, i - 1)
            r = slice(g * HD, (g + 1) * HD)
            return dict(q=q2[r, c, i * P:(i + 1) * P], k=k2[r, lo * P:(i + 1) * P],
                        v=[v2[:, j, g * HD:(g + 1) * HD] for j in range(lo, i + 1)],
                        w=(i + 1 - lo) * P, i=i, h=h, first=True, last=True, br="swa",
                        out=slice((h % 2) * HD, (h % 2) * HD + HD), blk=slice(i * P, (i + 1) * P),
                        head=h, end=i == TB - 1, begin=i == 0)

        NSW = len(SWA_UNITS)
        U2 = DEPTH * NU

        @block.tensor
        def _(pe):
            mm = nc.tensor.matmul

            def acc_wait(l, base, n):
                pe.wait_ge(acc_free[n % 2], free_at(l, base, n))
                return acc[n % 2]

            def slot_wait(s, l, n_dmas):
                pe.wait_ge(w_loaded[s], at(l, 16 * SLOT_DMAS[s], 16 * n_dmas))

            def norm(k):
                pe.wait_ge(summed, k + 1)
                mm(turn[0][:, :], cst("ones"), h_T[:, 0, :], start=True, stop=False)
                pe.wait_ge(squared, k * KC + KC)
                mm(turn[0][:, :], cst("ones"), h_T[:, KC - 1, :], start=False, stop=True).then_inc(ssq_full, 1)

            def slices(l, base, free_base, gub, dma_base, n, k):
                def up(sl, par):
                    for c in range(2):
                        pe.wait_ge(hid_done, at(l, TG, gub + sl * 2 + c + 1))
                        for w in range(2):
                            if c == 0:
                                slot_wait(w, l, dma_base[w] + sl + 1)
                            for kc in range(KC):
                                if isinstance(sl, int) and sl + c + w == 0:
                                    pe.wait_ge(h_ready, k * KC + kc + 1)
                                m = mm(score[2 * w + c][:, :], s3(w, KC, FS)[:, kc, c * P:(c + 1) * P],
                                       h_T[:, kc, :], start=kc == 0, stop=kc == KC - 1)
                        m.then_inc(gu_full, 1)

                def down(sl, par, last):
                    slot_wait(2, l, dma_base[2] + sl + 1)
                    pe.wait_ge(hid_done, at(l, TG, gub + sl * 2 + 4))
                    for c in range(KC):
                        pe.wait_ge(acc_free[c % 2], at(l, TL // 2, free_base // 2 + sl * (KC // 2) + c // 2 + 1))
                        for j in range(2):
                            m = mm(acc[c % 2][:, :], s3(2, 2, D)[:, j, c * P:(c + 1) * P],
                                   hid[:, 2 * par + j, :], start=j == 0, stop=j == 1)
                        m.then_inc(acc_full, 1)

                run_slices(pe, n, up, down)

            def linear(ps, s, width, col, m_cols, rhs, n_k, ready=None):
                for kc in range(n_k):
                    if ready is not None:
                        pe.wait_ge(h_ready, ready + kc + 1)
                    m = mm(ps[0:m_cols, :], s3(s, n_k, width)[:, kc, col:col + m_cols], rhs[:, kc, :],
                           start=kc == 0, stop=kc == n_k - 1)
                return m

            def by_token(ps, s, width, col, n, blocks, n_k=KC, src=h_T):
                for j, b in enumerate(blocks):
                    for kc in range(n_k):
                        m = mm(ps[:, j * n:(j + 1) * n], src[:, kc, b * P:(b + 1) * P],
                               s3(s, n_k, width)[:, kc, col:col + n], start=kc == 0, stop=kc == n_k - 1)
                return m

            def attend(l, per, u0, n_units, info, s_done, fr, fbase, head0):
                def scores(n):
                    u = info(n)
                    if n >= 4:
                        pe.wait_ge(s_done, at(l, per, u0 + n - 3))
                    mm(score[n % 4][:, 0:u["w"]], u["q"], u["k"], start=True, stop=True).then_inc(s_full, 1)

                def turns(n):
                    u = info(n)
                    pe.wait_ge(p_ready, at(l, per, u0 + n + 1))
                    if n >= 2:
                        pe.wait_ge(pt_ready, at(l, per, u0 + n - 1))
                    w = min(u["w"], P)
                    for j in range(len(u["v"])):
                        m = nc.tensor.transpose(turn[n % 2][0:w, j * P:(j + 1) * P],
                                                probs[:, n % 3, j * P:j * P + w], ident)
                    m.then_inc(t_full, 1)

                def values(n):
                    u = info(n)
                    w = min(u["w"], P)
                    t = head0 + u["head"]
                    if u["begin"]:
                        acc_wait(fr, fbase, t)
                    pe.wait_ge(pt_ready, at(l, per, u0 + n + 1))
                    for j, v in enumerate(u["v"]):
                        m = mm(acc[t % 2][u["out"], u["blk"]], v[0:w, :], probs_T[0:w, n % 2, j * P:(j + 1) * P],
                               start=u["first"] and j == 0, stop=u["last"] and j == len(u["v"]) - 1,
                               skip_group_check=True)
                    m.then_inc(pv_done, 1)

                AHEAD = 3
                for n in range(min(AHEAD, n_units)):
                    scores(n)
                for n in range(n_units + 1):
                    if n + AHEAD < n_units:
                        scores(n + AHEAD)
                    if n < n_units:
                        turns(n)
                    if n >= 1:
                        values(n - 1)

            def mix(l):
                for n, (name, i, ld, who) in enumerate(MIX):
                    if ld is not None:
                        s = ld % 3
                        slot_wait(s, l, NSL + sum(MIX_DMAS[s:ld + 1:3]))
                    if (name, i) == ("kc", 0):
                        pe.wait_ge(lsq_ready, l + 1)
                        for j in range(2):
                            mm(turn[0][:, :], cst("ones"), probs[:, j, :], start=j == 0, stop=j == 1)
                        mm(turn[1][:, :], cst("ones"), probs[:, 2, :], start=True, stop=True).then_inc(lssq_full, 1)
                    if name == "uq" and i == 0:
                        pe.wait_ge(lora_ready, l + 1)
                    if name == "rope":
                        taken(pe, l, BM, TICKET[ROPES[i][2]])
                    if name == "xs_k":
                        pe.wait_ge(rope_ready, at(l, len(ROPES), 1))
                    if name == "xs_v":
                        taken(pe, l, BM, TICKET["vc", 0])
                    if name == "hid_k":
                        pe.wait_ge(rope_ready, at(l, len(ROPES), len(ROPES)))
                        pe.wait_ge(small_loaded, at(l, 64, 64))
                        taken(pe, l, BM, TICKET["xs_k", 1])
                        taken(pe, l, BM, TICKET["xs_k", 0])
                    if name == "hid_v":
                        taken(pe, l, BM, TICKET["xs_v", 1])
                        taken(pe, l, BM, TICKET["xs_v", 0])
                    if name == "cmp":
                        pe.wait_ge(hidc_ready, at(l, 2, 2))
                    ps = acc_wait(l, BM, n)
                    if name in ("cq", "sq", "sk") or (name == "nq" and i < 2):
                        m = linear(ps, s, 256, 128 * i, 128, h_T, KC,
                                   at(l, 3 * KC, KC) if n == 0 else None)
                    elif name == "nq" or name in ("ckv", "vc"):
                        m = linear(ps, s, 160 if name == "ckv" else 256, 0, 128, h_T, KC)
                    elif name == "kr":
                        m = linear(ps, s, 160, 64, 96, h_T, KC)
                    elif name in ("kc", "ks", "kw"):
                        m = linear(ps, s, 256, 128, 128, h_T, KC)
                    elif name == "vs":
                        m = by_token(ps, s, 256, 0, P, range(TB))
                    elif name == "vw":
                        m = by_token(ps, s, 146, 0, P, range(TB))
                    elif name == "gate":
                        m = by_token(ps, s, 146, P, 18, range(TB))
                    elif name == "sv":
                        m = by_token(ps, s, 256, 0, 256, (2 * i, 2 * i + 1))
                    elif name == "uq":
                        m = linear(ps, s, 576, 96 * i, 96, lora, 2)
                    elif name == "kn":
                        m = mm(ps[0:HD, :], s3(s, 1, 768)[:, 0, 128 * i:128 * i + HD], lora[:, 2, :],
                               start=True, stop=True)
                    elif name == "mv":
                        wv = slot[s][:, 0:768].rearrange("p (h t d) -> p h t d", t=2, d=HD)[:, :, 1, :]
                        m = mm(ps[:, 0:384], lora[:, 2, i * P:(i + 1) * P], wv, start=True, stop=True)
                    elif name == "rope":
                        t, kind, _ = ROPES[i]
                        r = 96 if kind == "mla" else P
                        m = mm(ps[0:r, :], cst("r_" + kind, rows=r), t, start=True, stop=True)
                    elif name in ("hid_k", "hid_v"):
                        kv = 0 if name == "hid_k" else 1
                        w1 = s3(s, 16, P)
                        for c in range(16):
                            mm(ps[:, 0:62].rearrange("p (g w) -> p g w", g=2), w1[:, c, :],
                               pairs[kv][:, :, 2 * c:2 * c + 481:16], start=c == 0, stop=c == 15)
                        for c in range(16):
                            m = mm(ps[:, 62:63], w1[:, c, :], cmp_pos[:, kv, c:c + 1],
                                   start=c == 0, stop=c == 15)
                    elif name in ("xs_k", "xs_v"):
                        src = nk[:, 0 if name == "xs_k" else 3, :]
                        pick = cst("ident", lo=i * HD, hi=(i + 1) * HD)
                        mm(ps[0:HD, :], pick, src, start=True, stop=True)
                        mm(ps[HD:P, 0:S - 1], pick, src[:, 1:S], start=True, stop=True)
                        m = mm(ps[HD:P, S - 1:S], pick, src[:, 0:1], start=True, stop=True)
                    elif name == "cmp":
                        for g in range(2):
                            mm(ps[g * HD:(g + 1) * HD, 0:31], cmp_w2[:, 0, :], hid_cmp[:, 0, g * 31:g * 31 + 31],
                               start=True, stop=True)
                        for g in range(2):
                            m = mm(ps[0:31, 64 + g * HD:128 + g * HD], hid_cmp[:, 1, g * 31:g * 31 + 31],
                                   cmp_w2[:, 1, :], start=True, stop=True)
                    m.then_inc(acc_full, 1)
                taken(pe, l, BM, TICKET["cmp", 0])
                attend(l, NU, 0, NU, unit_info, exp_ready, l, BM, T_LIN)
                pe.wait_ge(exp_ready, at(l, NU, NU))
                def remaining(h):
                    r, c = slice((h % 2) * HD, (h % 2) * HD + HD), h // 2
                    if h >= 2:
                        pe.wait_ge(a_exp, at(l, SB_HEADS, h - 1))
                    for j in range(TB):
                        b, o = SB_PLACE[j]
                        m = mm(sb_bank[h % 2][b][:, o:o + S - j * P], sk_T[r, c, j * P:(j + 1) * P],
                               sq_T[r, c, j * P:S], start=j != 3, stop=True, skip_group_check=True)
                    m.then_inc(z_full, 1)

                def suffixes(h):
                    pe.wait_ge(sp_ready, at(l, SB_HEADS, h + 1))
                    for j in range(TB):
                        b, o = SB_PLACE[j]
                        ps = sb_bank[h % 2][b]
                        m = mm(ps[:, o:o + S - j * P], cst("negtri"), sb_cols(hid, j, 0, S - j * P),
                               start=False, stop=j == TB - 1, skip_group_check=True)
                        for jj in range(j + 1, TB):
                            m = mm(ps[:, o + (jj - j) * P:o + S - j * P], cst("negones"),
                                   sb_cols(hid, jj, 0, S - jj * P),
                                   start=False, stop=jj == TB - 1, skip_group_check=True)
                    m.then_inc(suffix_full, 1)

                def sb_values(h):
                    r = slice((h % 2) * HD, (h % 2) * HD + HD)
                    ps = acc_wait(l, BM, T_LIN + NHD + h)
                    pe.wait_ge(a_ready, at(l, SB_HEADS, h + 1))
                    for j in range(TB):
                        m = mm(ps[r, j * P:S], sv[:, j, h * HD:(h + 1) * HD], sb_cols(sb_a[h % 2], j, 0, S - j * P),
                               start=j == 0, stop=j == TB - 1, skip_group_check=True)
                    m.then_inc(acc_full, 1)

                remaining(0)
                for h in range(SB_HEADS):
                    if h + 1 < SB_HEADS:
                        remaining(h + 1)
                    suffixes(h)
                    if h >= 1:
                        sb_values(h - 1)
                sb_values(SB_HEADS - 1)
                taken(pe, l, BM, T_LIN + NHD + SB_HEADS - 2)
                taken(pe, l, BM, T_LIN + NHD + SB_HEADS - 1)
                for c in range(KC):
                    ld = W_OUT0 + c // 2
                    slot_wait(ld % 3, l, NSL + sum(MIX_DMAS[ld % 3:ld + 1:3]))
                    ps = acc_wait(l, BM, T_HEAD + c)
                    linear(ps, ld % 3, 256, (c % 2) * P, P, o_T, KC).then_inc(acc_full, 1)

            pe.sem_inc(acc_free[0], 1)
            pe.sem_inc(acc_free[1], 1)
            pe.sem_inc(acc_full, 1)
            pe.sem_inc(gu_full, 1)
            pe.sem_inc(hid_done, 2)
            pe.sem_inc(mine_ready, 1)
            pe.sem_inc(xgu_full, 2)
            pe.sem_inc(xdown_full, 2)
            pe.sem_inc(place_ready, 2)
            pe.sem_inc(scatter_taken, 2)
            pe.wait_ge(params_loaded, N_PARAMS)
            pe.wait_ge(x_loaded, 16)
            for c in range(KC):
                if c >= 2:
                    pe.wait_ge(x_final, c - 1)
                for b in range(TB):
                    m = nc.tensor.transpose(turn[c % 2][:, b * P:(b + 1) * P], x_in[:, b, c * P:(c + 1) * P], ident)
                m.then_inc(xt_full, 1)
            pe.wait_ge(x_final, KC)
            with pe.Fori(0, DEPTH) as l:
                norm(l * 3)
                slices(l, F1, B1, 0, [0, 0, 0], NSL, l * 3)
                norm(l * 3 + 1)
                mix(l)
                norm(l * 3 + 2)
                slices(l, F2, B2, 2 * NSL, [NSL + sum(MIX_DMAS[s::3]) for s in range(3)], NSL, l * 3 + 2)

            norm(3 * L)
            norm(3 * L + 1)
            pe.wait_ge(h_ready, KC * (3 * L + 1) + 1)
            mm(turn[0][0:8, 0:384], rel[:, :], cst("bucket_rows", rows=32), start=True, stop=True
               ).then_inc(rel_full, 1)
            for n, (name, i, ld) in enumerate(SEC_T):
                if ld is not None:
                    s = ld % 3
                    slot_wait(s, L, sum(SEC_DMAS[s:ld + 1:3]))
                if (name, i) == ("wst", 0):
                    pe.wait_ge(ws_loaded, 32)
                if (name, i) == ("sv", 0):
                    pe.wait_ge(vn_ready, 1)
                    taken(pe, L, 0, T2["wst", 0])
                    taken(pe, L, 0, T2["wst", 1])
                if name == "swa":
                    if i == 0:
                        taken(pe, L, 0, T2["sv", 3])
                        taken(pe, L, 0, T2["k", 0])
                        attend(L, NU, 0, NSW, swa_info, max_ready, L, 0, SWA0)
                    continue
                if (name, i) == ("pa", 0):
                    taken(pe, L, 0, T2["swa", 6])
                    taken(pe, L, 0, T2["swa", 7])
                if (name, i) == ("wo", 0):
                    pe.wait_ge(merged_ready, KC)
                if name == "route":
                    norm(3 * L + 2)
                    pe.wait_ge(h_ready, KC * (3 * L + 3))
                if name == "rank":
                    for j in range(2 * TB):
                        b, hf = j // 2, j % 2
                        if j >= 2:
                            pe.wait_ge(htok_ready, j - 1)
                        for c in range(4):
                            m = nc.tensor.transpose(turn[j % 2][:, c * P:(c + 1) * P],
                                                    h_T[:, 4 * hf + c, b * P:(b + 1) * P], ident)
                        m.then_inc(htok_full, 1)
                    pe.wait_ge(member_ready, 1)
                if name == "combt":
                    pe.wait_ge(comb_done, 1)
                if name == "rankt":
                    pe.wait_ge(rank_ready, 1)
                ps = acc_wait(L, 0, n)
                if name in ("u", "q", "gate"):
                    m = linear(ps, s, 256, (i % 2) * P, P, h_T, KC, KC * (3 * L + 1) if n == 0 else None)
                elif name == "v":
                    m = by_token(ps, s, 256, 0, 256, (2 * (i % 2), 2 * (i % 2) + 1))
                elif name == "k":
                    m = linear(ps, s, 256, 0, P, h_T, KC)
                elif name == "vtok":
                    m = by_token(ps, s, 256, P, P, range(TB))
                elif name == "wst":
                    for g in range(4):
                        m = nc.tensor.transpose(ps[:, g * P:(g + 1) * P], ws_n[:, 4 * i + g, :], ident)
                elif name == "sv":
                    for b in range(TB):
                        for g in range(2):
                            mm(ps[g * HD:(g + 1) * HD, b * P:(b + 1) * P],
                               vtok[:, b, (2 * i + g) * HD:(2 * i + g + 1) * HD], ws_T[:, 2 * i + g, :],
                               start=True, stop=False, skip_group_check=True)
                        m = mm(ps[:, b * P:(b + 1) * P], cst("group_rows", 8, i * P, (i + 1) * P), bs[:, :],
                               start=False, stop=True, skip_group_check=True)
                elif name in ("pa", "pb"):
                    m = linear(ps, s, 512, (i % 4) * P, P, ab_T if name == "pa" else ab_T[:, 4:8, :], 4)
                elif name == "wo":
                    m = linear(ps, s, 256, (i % 2) * P, P, sig_a, KC)
                elif name == "route":
                    for b in range(TB):
                        for kc in range(KC):
                            m = mm(ps[:, b * 20:(b + 1) * 20], h_T[:, kc, b * P:(b + 1) * P], rw[:, kc, :],
                                   start=kc == 0, stop=kc == KC - 1)
                elif name == "rank":
                    for b in range(TB):
                        for j in range(b + 1):
                            mm(ps[:, b * 16:(b + 1) * 16], cst("strict" if j == b else "ones"), member[:, j, :],
                               start=j == 0, stop=j == b)
                    for b in range(TB):
                        m = mm(ps[:, 64:80], cst("ones"), member[:, b, :], start=b == 0, stop=b == TB - 1)
                elif name in ("combt", "rankt"):
                    for b in range(TB):
                        m = nc.tensor.transpose(ps[0:16, b * P:(b + 1) * P],
                                                (comb if name == "combt" else rank)[:, b, :], ident)
                m.then_inc(acc_full, 1)

            def gather(pair, q):
                pe.wait_ge(pick_ready, pair * 2 + q + 1)
                pe.wait_ge(mine_ready, pair * 2 + q + 1)
                for c in range(KC):
                    for b in range(TB):
                        m = mm(turn[c // 4][:, (c % 4) * P:(c % 4 + 1) * P], h_tok[:, b, c * P:(c + 1) * P],
                               pick[q][:, b, :], start=b == 0, stop=b == TB - 1)
                m.then_inc(gathered, 1)

            def gate_up(pair, q):
                pe.wait_ge(mine_ready, pair * 2 + q + 2)
                for w, (wt, sem_) in enumerate(((xg_w, xgate_loaded), (xu_w, xup_loaded))):
                    pe.wait_ge(sem_[q], pair * 16 + 16)
                    for c in range(KC):
                        m = mm(score[w][:, :], mine_T[q][:, c, :], wt[q][:, c, :], start=c == 0, stop=c == KC - 1)
                m.then_inc(xgu_full, 1)

            def turn_hidden(pair, q):
                pe.wait_ge(xhid_ready, pair * 2 + q + 1)
                for c in range(4):
                    m = nc.tensor.transpose(score[0][:, c * P:(c + 1) * P], xhid[:, c * P:(c + 1) * P], ident)
                m.then_inc(xhid_turned, 1)

            def down_x(pair, q):
                pe.wait_ge(xhidt_ready, pair * 2 + q + 1)
                pe.wait_ge(xdown_loaded[q], pair * 32 + 32)
                for hf in range(2):
                    for c in range(4):
                        m = mm(score[2 + hf][:, :], xhid_T[:, c * P:(c + 1) * P],
                               xd_w[q][c // 2][:, c % 2, hf * S:(hf + 1) * S], start=c == 0, stop=c == 3)
                m.then_inc(xdown_full, 1)

            def scatter(pair, q):
                pe.wait_ge(yslot_ready, pair * 2 + q + 1)
                pe.wait_ge(place_ready, pair * 2 + q + 3)
                for c in range(KC):
                    pe.wait_ge(scatter_taken, pair * 16 + 8 * q + c + 1)
                    mm(acc[c % 2][:, :], y_slot[:, c // 4, (c % 4) * P:(c % 4 + 1) * P], place[q],
                       start=True, stop=True).then_inc(scattered, 1)

            def step(pair, q, first=False, last=False):
                gate_up(pair, q)
                if not last:
                    gather(pair + q, 1 - q)
                turn_hidden(pair, q)
                if not first:
                    scatter(pair - 1 + q, 1 - q)
                down_x(pair, q)

            acc_wait(L, 0, NT2)
            acc_wait(L, 0, NT2 + 1)
            pe.wait_ge(htok_ready, 2 * TB)
            pe.wait_ge(passes_ready, 1)
            n_p = pe.value_load(n_passes[0:1, 0:1], min_val=1, max_val=TB)
            with pe.Fori(0, n_p) as ps_:
                pair0 = pe.snap(ps_ * (NX // 2))
                gather(pair0, 0)
                step(pair0, 0, first=True)
                with pe.Fori(0, NX // 2 - 1) as i:
                    pair = pe.snap(pair0 + i)
                    step(pair, 1)
                    step(pair + 1, 0)
                step(pair0 + (NX // 2 - 1), 1, last=True)
                scatter(pair0 + (NX // 2 - 1), 1)
            norm(3 * L + 3)
            pe.wait_ge(h_ready, KC * (3 * L + 4))
            for n in range(2 * TB):
                if n >= 2:
                    pe.wait_ge(y_ready, n - 1)
                for c in range(4):
                    m = nc.tensor.transpose(turn[n % 2][:, c * P:(c + 1) * P],
                                            h_T[:, 4 * (n % 2) + c, (n // 2) * P:(n // 2 + 1) * P], ident)
                m.then_inc(yt_full, 1)

        @block.scalar
        def _(act):
            fn = nc.scalar.activation

            def norm(k):
                for c in range(KC):
                    act.wait_ge(x_final, k * KC + c + 1)
                    fn(h_T[:, c, :], x_T[:, c, :], ACT.Square).then_inc(squared, 1)
                act.wait_ge(ssq_full, k + 1)
                fn(rstd[:, :], turn[0][:, :], ACT.Ln, scale=1.0 / D, bias=eps[:, :])
                act.drain()
                fn(rstd[:, :], rstd[:, :], ACT.Exp, scale=-0.5).then_inc(rstd_ready, 1)

            def slices(l, gub, n):
                def up(sl, par):
                    for c in range(2):
                        act.wait_ge(gu_full, gu_at(l, gub, sl * 2 + c + 1))
                        fn(et[:, c, :], score[c][:, :], ACT.Exp, scale=-1.0).then_inc(sig_ready, 1)

                run_slices(act, n, up, lambda *x: None)

            def attend(l, per, u0, n_units, info, fr, fbase, head0, dest, sink):
                def exps(n):
                    u = info(n)
                    w, st = u["w"], n % 4
                    act.wait_ge(max_ready, at(l, per, u0 + n + 1))
                    if n >= 3 and not sink:
                        act.wait_ge(t_full, at(l, per, u0 + n - 2))
                    src = probs[:, n % 3, 0:w] if sink else score[st][:, 0:w]
                    m = fn(probs[:, n % 3, 0:w], src, ACT.Exp, bias=stats[:, 0, st:st + 1],
                           accum_out=stats[:, 1, st:st + 1])
                    if sink:
                        m = fn(stats[:, 3, st:st + 1], sinks[:, u["h"]:u["h"] + 1], ACT.Exp,
                               bias=stats[:, 0, st:st + 1])
                    m.then_inc(exp_ready, 1)

                def evac_turn(n):
                    u = info(n)
                    r, w = min(u["w"], P), len(u["v"]) * P
                    act.wait_ge(t_full, at(l, per, u0 + n + 1))
                    if n >= 2:
                        act.wait_ge(pv_done, at(l, per, u0 + n - 1))
                    fn(probs_T[0:r, n % 2, 0:w], turn[n % 2][0:r, 0:w], ACT.Copy).then_inc(pt_ready, 1)

                def head_out(n):
                    u = info(n)
                    if u["end"]:
                        t = head0 + u["head"]
                        act.wait_ge(pv_done, at(l, per, u0 + n + 1))
                        fn(dest[u["out"], u["head"] // 2, :], acc[t % 2][u["out"], :], ACT.Copy
                           ).then_inc(acc_free[t % 2], 1)

                exps(0)
                for n in range(n_units + 1):
                    if n + 1 < n_units:
                        exps(n + 1)
                    if n < n_units:
                        evac_turn(n)
                    if n >= 1:
                        head_out(n - 1)

            def mix(l):
                for n, (name, i, ld, who) in enumerate(MIX):
                    if who == "act":
                        act.wait_ge(acc_full, mix_full(l, n + 1))
                        if name == "cmp":
                            fn(kcmp_T[:, :], acc[n % 2][:, 0:31], ACT.Copy)
                            m = fn(vcmp.rearrange("p a b -> p (a b)"), acc[n % 2][0:31, 64:192], ACT.Copy)
                        else:
                            t, sc = EVAC[name, i]
                            m = fn(t, acc[n % 2][0:t.shape[0], 0:t.shape[1]], ACT.Copy, scale=sc)
                        m.then_inc(acc_free[n % 2], 1)
                    if (name, i) == ("ckv", 0):
                        act.drain()
                        fn(probs[:, :, :], lora[:, 0:3, :], ACT.Square).then_inc(lsq_ready, 1)
                    if (name, i) == ("ks", 0):
                        act.wait_ge(lssq_full, l + 1)
                        fn(et[:, 0, :], turn[0][:, :], ACT.Ln, scale=1.0 / 256, bias=eps[:, :])
                        fn(et[:, 1, :], turn[1][:, :], ACT.Ln, scale=1.0 / 128, bias=eps[:, :])
                        act.drain()
                        fn(et[:, :, :], et[:, :, :], ACT.Exp, scale=-0.5).then_inc(lrstd_ready, 1)
                    if name == "gate":
                        taken(act, l, BM, n)
                        fn(gates_e[:, :, :], gates[:, :, :], ACT.Exp, scale=-1.0).then_inc(gate_exp, 1)
                    if name in ("hid_k", "hid_v"):
                        kv = 0 if name == "hid_k" else 1
                        act.wait_ge(gelu_pre, at(l, 2, kv + 1))
                        fn(cmp_t[:, 2, :], cmp_t[:, 1, :], ACT.Exp, scale=-2 * GC).then_inc(gelu_exp, 1)
                attend(l, NU, 0, NU, unit_info, l, BM, T_LIN, o_T, False)
                def logs(h):
                    act.drain()
                    act.wait_ge(z_full, at(l, SB_HEADS, h + 1))
                    if h >= 1:
                        act.wait_ge(sp_ready, at(l, SB_HEADS, h))
                    for b, n in SB_BANKS:
                        fn(sb_e[:, b, 0:n], sb_bank[h % 2][b][:, 0:n], ACT.Abs)
                    e = arena[:, 0:2 * S + 2 * P]
                    act.drain()
                    fn(e, e, ACT.Exp, scale=-1.0)
                    act.drain()
                    fn(e, e, ACT.Ln, bias=1.0).then_inc(log_ready, 1)

                def shares(h):
                    act.wait_ge(suffix_full, at(l, SB_HEADS, h + 1))
                    if h >= 2:
                        act.wait_ge(acc_full, mix_full(l, T_LIN + NHD + h - 1))
                    for b, n in SB_BANKS:
                        m = fn(sb_a[h % 2][:, b, 0:n], sb_bank[h % 2][b][:, 0:n], ACT.Exp)
                    m.then_inc(a_exp, 1)

                def sb_out(h):
                    t = T_LIN + NHD + h
                    act.wait_ge(acc_full, mix_full(l, t + 1))
                    r = slice((h % 2) * HD, (h % 2) * HD + HD)
                    fn(o_T[r, 6 + h // 2, :], acc[t % 2][r, :], ACT.Copy).then_inc(acc_free[t % 2], 1)

                logs(0)
                for h in range(SB_HEADS):
                    if h + 1 < SB_HEADS:
                        logs(h + 1)
                    shares(h)
                    if h >= 1:
                        sb_out(h - 1)
                sb_out(SB_HEADS - 1)

            act.wait_ge(eps_ready, 1)
            act.wait_ge(params_loaded, N_PARAMS)
            with act.Fori(0, DEPTH) as l:
                norm(l * 3)
                slices(l, 0, NSL)
                norm(l * 3 + 1)
                mix(l)
                norm(l * 3 + 2)
                slices(l, 2 * NSL, NSL)

            norm(3 * L)
            norm(3 * L + 1)
            for n, (name, i, ld) in enumerate(SEC_T):
                if name in ("u", "v", "q", "k", "vtok", "gate"):
                    act.wait_ge(acc_full, full_at(L, 0, full2(n + 1)))
                    ps = acc[n % 2][:, :]
                    if name == "u":
                        m = fn(u_T[:, i, :], ps, ACT.Copy)
                    elif name == "v":
                        b, hf = i % 2, i // 2
                        m = fn(vtok[:, 2 * b:2 * b + 2, hf * 256:(hf + 1) * 256],
                               ps.rearrange("p (a b) -> p a b", b=256), ACT.Copy)
                    elif name == "q":
                        m = fn(q2[:, i, :], ps, ACT.Copy, scale=HD ** -0.5)
                    elif name == "k":
                        m = fn(k2, ps, ACT.Copy)
                    elif name == "vtok":
                        m = fn(v2.rearrange("p a b -> p (a b)"), ps, ACT.Copy)
                    else:
                        m = fn((sig_a if i < 8 else sig_b)[:, i % 8, :], ps, ACT.Exp, scale=-1.0)
                    m.then_inc(acc_free[n % 2], 1)
                if name == "gate" and i < 8:
                    act.wait_ge(gelu_pre, 2 * L + i + 1)
                    fn(probs[:, i % 2, :], probs[:, i % 2, :], ACT.Exp, scale=-2 * GC).then_inc(gelu_exp, 1)
                if name == "gate" and i == 10:
                    act.wait_ge(ln_pre, 1)
                    fn(lnst[:, 2, :], lnst[:, 1, :], ACT.Ln, scale=1.0 / 512, bias=eps[:, :])
                    act.drain()
                    fn(lnst[:, 3, :], lnst[:, 2, :], ACT.Exp, scale=-0.5).then_inc(ln_rstd, 1)
                if (name, i) == ("swa", 0):
                    attend(L, NU, 0, NSW, swa_info, L, 0, SWA0, ab_T[:, 4:8, :], True)
                if name == "route":
                    norm(3 * L + 2)
                    for j in range(2 * TB):
                        act.wait_ge(htok_full, j + 1)
                        fn(h_tok[:, j // 2, (j % 2) * S:(j % 2 + 1) * S], turn[j % 2][:, :], ACT.Copy
                           ).then_inc(htok_ready, 1)
                    act.wait_ge(route_pre, 1)
                    fn(rx[:, 1, :, 0:4], rx[:, 0, :, 0:4], ACT.Exp).then_inc(route_exp, 1)
                    act.wait_ge(route_pre, 2)
                    fn(rx[:, 11, :, 0:1], rx[:, 10, :, 0:1], ACT.Exp).then_inc(route_exp, 1)

            def mine_out(pair, q):
                act.wait_ge(gathered, pair * 2 + q + 1)
                for t in range(2):
                    m = fn(mine_T[q][:, 4 * t:4 * t + 4, :], turn[t][:, :].rearrange("p (c t) -> p c t", t=P), ACT.Copy)
                m.then_inc(mine_ready, 1)

            def step(pair, q, last=False):
                act.wait_ge(xgu_full, pair * 2 + q + 3)
                fn(et[:, 0, :], score[0][:, :], ACT.Exp, scale=-1.0).then_inc(xsig_ready, 1)
                if not last:
                    mine_out(pair + q, 1 - q)
                act.wait_ge(xhid_turned, pair * 2 + q + 1)
                fn(xhid_T, score[0][:, :], ACT.Copy).then_inc(xhidt_ready, 1)
                act.wait_ge(xdown_full, pair * 2 + q + 3)
                for t in range(2):
                    m = fn(y_slot[:, t, :], score[2 + t][:, :], ACT.Copy)
                m.then_inc(yslot_ready, 1)

            act.wait_ge(passes_ready, 1)
            n_p = act.value_load(n_passes[0:1, 0:1], min_val=1, max_val=TB)
            with act.Fori(0, n_p) as ps_:
                pair0 = act.snap(ps_ * (NX // 2))
                mine_out(pair0, 0)
                step(pair0, 0)
                with act.Fori(0, NX // 2 - 1) as i:
                    pair = act.snap(pair0 + i)
                    step(pair, 1)
                    step(pair + 1, 0)
                step(pair0 + (NX // 2 - 1), 1, last=True)
            norm(3 * L + 3)
            for n in range(2 * TB):
                act.wait_ge(yt_full, n + 1)
                fn(y_out[:, n // 2, (n % 2) * S:(n % 2 + 1) * S], turn[n % 2][:, :], ACT.Copy).then_inc(y_ready, 1)

        @block.vector
        def _(dve):
            V = nc.vector

            def norm(k, dest=h_T):
                dve.wait_ge(rstd_ready, k + 1)
                for c in range(KC):
                    V.scalar_tensor_tensor(dest[:, c, :], x_T[:, c, :], gains[:, bass.ds(k, 1), c:c + 1][:, 0, :],
                                           rstd[:, :], ALU.mult, ALU.mult).then_inc(h_ready, 1)
                    if dest is x_T:
                        dve.drain().then_inc(x_final, 1)
                        square_sum(k + 1, c - 1)

            def square_sum(k, c):
                if 1 <= c < KC - 1:
                    dve.wait_ge(squared, k * KC + c + 1)
                    m = V.tensor_tensor(h_T[:, 0, :], h_T[:, 0, :], h_T[:, c, :], ALU.add)
                    if c == KC - 2:
                        m.then_inc(summed, 1)

            def slices(l, base, gub, n, coef, k):
                def up(sl, par, chunks=(0, 1)):
                    for c in chunks:
                        dve.wait_ge(sig_ready, at(l, TG, gub + sl * 2 + c + 1))
                        V.tensor_scalar(et[:, c, :], et[:, c, :], 1.0, None, ALU.add)
                        dve.drain()
                        V.reciprocal(rt[:, :], et[:, c, :])
                        dve.drain()
                        V.tensor_tensor(rt[:, :], rt[:, :], score[c][:, :], ALU.mult)
                        dve.drain()
                        V.tensor_tensor(hid[:, 2 * par + c, :], rt[:, :], score[2 + c][:, :], ALU.mult
                                        ).then_inc(hid_done, 1)

                def down(sl, par, last):
                    for c in range(KC):
                        dve.wait_ge(acc_full, full_at(l, base, sl * KC + c + 1))
                        V.scalar_tensor_tensor(x_T[:, c, :], acc[c % 2][:, :], coef, x_T[:, c, :],
                                               ALU.mult, ALU.add).then_inc(acc_free[c % 2], 1)
                        if last:
                            dve.drain().then_inc(x_final, 1)
                            square_sum(k, c - 1)

                def step(sl, par):
                    up(sl, par, (0,))
                    down(sl - 1, 1 - par, False)
                    up(sl, par, (1,))

                up(0, 0)
                with dve.Fori(0, (n - 1) // 2) as i:
                    step(i * 2 + 1, 1)
                    step(i * 2 + 2, 0)
                if n % 2 == 0:
                    step(n - 1, 1)
                down(n - 1, (n - 1) % 2, True)

            def attend(l, per, u0, n_units, info, sink):
                def maxima(n):
                    u = info(n)
                    w, st, i = u["w"], n % 4, u["i"]
                    ps = score[st]
                    dve.wait_ge(s_full, at(l, per, u0 + n + 1))
                    if sink:
                        if n >= 3:
                            dve.wait_ge(t_full, at(l, per, u0 + n - 2))
                        pr = probs[:, n % 3, 0:w]
                        V.tensor_tensor(pr, ps[:, 0:w], bias_t[:, u["h"], 256 - w:256], ALU.add)
                        dve.drain()
                        V.tensor_reduce(stats[:, 2, st:st + 1], pr, AX.X, ALU.max)
                        dve.drain()
                        V.tensor_scalar(stats[:, 0, st:st + 1], stats[:, 2, st:st + 1],
                                        sinks[:, u["h"]:u["h"] + 1], -1.0, ALU.max, ALU.mult
                                        ).then_inc(max_ready, 1)
                        return
                    if u["br"] == "cmp":
                        V.tensor_tensor(ps[:, 0:31], ps[:, 0:31], cst("cmp_mask", lo=i * 31, hi=i * 31 + 31), ALU.add)
                    else:
                        V.tensor_tensor(ps[:, i * P:w], ps[:, i * P:w], cst("causal"), ALU.add)
                    dve.drain()
                    V.tensor_reduce(stats[:, 0, st:st + 1], ps[:, 0:w], AX.X, ALU.max, negate=True
                                    ).then_inc(max_ready, 1)

                def normalize(n):
                    u = info(n)
                    w, st = u["w"], n % 4
                    dve.wait_ge(exp_ready, at(l, per, u0 + n + 1))
                    if sink:
                        V.tensor_tensor(stats[:, 1, st:st + 1], stats[:, 1, st:st + 1], stats[:, 3, st:st + 1], ALU.add)
                        dve.drain()
                    V.reciprocal(stats[:, 2, st:st + 1], stats[:, 1, st:st + 1])
                    dve.drain()
                    pr = probs[:, n % 3, 0:w]
                    if u["br"] in ("cmp", "sel", "win"):
                        g = u["h"] * 3 + ("cmp", "sel", "win").index(u["br"])
                        V.tensor_scalar(pr, pr, stats[:, 2, st:st + 1], gates[:, u["i"], g:g + 1],
                                        ALU.mult, ALU.mult).then_inc(p_ready, 1)
                    else:
                        V.tensor_scalar(pr, pr, stats[:, 2, st:st + 1], None, ALU.mult).then_inc(p_ready, 1)

                maxima(0)
                for n in range(n_units):
                    if n + 1 < n_units:
                        maxima(n + 1)
                    normalize(n)

            def gelu_pre_ops(x, t):
                dve.drain()
                V.tensor_tensor(t, x, x, ALU.mult)
                dve.drain()
                V.tensor_scalar(t, t, 0.044715, 1.0, ALU.mult, ALU.add)
                dve.drain()
                V.tensor_tensor(t, t, x, ALU.mult)
                dve.drain()
                V.tensor_scalar(t, t, -54.0, None, ALU.max).then_inc(gelu_pre, 1)

            def mix(l):
                for n, (name, i, ld, who) in enumerate(MIX):
                    ps = acc[n % 2]
                    if who == "dve":
                        dve.drain()
                        dve.wait_ge(acc_full, mix_full(l, n + 1))
                    if name == "gate":
                        V.tensor_tensor(gates[:, :, :], ps[:, 0:72].rearrange("p (b g) -> p b g", g=18),
                                        gbias[:, bass.ds(l, 1), :].broadcast_to([P, TB, 18]), ALU.add
                                        ).then_inc(acc_free[n % 2], 1)
                        dve.wait_ge(gate_exp, l + 1)
                        V.tensor_scalar(gates_e[:, :, :], gates_e[:, :, :], 1.0, None, ALU.add)
                        dve.drain()
                        V.reciprocal(gates[:, :, :], gates_e[:, :, :])
                        dve.drain()
                        g3 = gates.rearrange("p b (h r) -> p b h r", r=3)[:, :, :, 0]
                        V.tensor_tensor(g3, g3, cst("cmp_valid").unsqueeze(2).broadcast_to([P, TB, 6]), ALU.mult)
                        dve.wait_ge(lrstd_ready, l + 1)
                        for c in range(3):
                            m = V.scalar_tensor_tensor(lora[:, c, :], lora[:, c, :],
                                                       lgains[:, bass.ds(l, 1), c:c + 1][:, 0, :],
                                                       et[:, c // 2, :], ALU.mult, ALU.mult)
                        m.then_inc(lora_ready, 1)
                    elif name == "rope":
                        t, kind, _ = ROPES[i]
                        r = t.shape[0]
                        V.tensor_tensor(rt[0:r, :], ps[0:r, :], cst("sin_" + kind, rows=r), ALU.mult
                                        ).then_inc(acc_free[n % 2], 1)
                        V.tensor_tensor(t, t, cst("cos_" + kind, rows=r), ALU.mult)
                        dve.drain()
                        if i == 6:
                            V.tensor_tensor(k6[HD:96, :, :], t[HD:96, :].unsqueeze(1).broadcast_to([32, 6, S]),
                                            rt[HD:96, :].unsqueeze(1).broadcast_to([32, 6, S]), ALU.add
                                            ).then_inc(rope_ready, 1)
                        else:
                            V.tensor_tensor(t, t, rt[0:r, :], ALU.add).then_inc(rope_ready, 1)
                    elif name in ("hid_k", "hid_v"):
                        kv = 0 if name == "hid_k" else 1
                        V.tensor_copy(bias_c[:, kv:kv + 1], ps[:, 62:63])
                        dve.drain()
                        V.tensor_scalar(cmp_t[:, 0, :], ps[:, 0:62], bias_c[:, kv:kv + 1], None, ALU.add
                                        ).then_inc(acc_free[n % 2], 1)
                        dve.drain()
                        gelu_pre_ops(cmp_t[:, 0, :], cmp_t[:, 1, :])
                        dve.wait_ge(gelu_exp, at(l, 2, kv + 1))
                        V.tensor_scalar(cmp_t[:, 2, :], cmp_t[:, 2, :], 1.0, None, ALU.add)
                        dve.drain()
                        V.reciprocal(cmp_t[:, 3, :], cmp_t[:, 2, :])
                        dve.drain()
                        V.tensor_tensor(hid_cmp[:, kv, :], cmp_t[:, 0, :], cmp_t[:, 3, :], ALU.mult
                                        ).then_inc(hidc_ready, 1)
                attend(l, NU, 0, NU, unit_info, False)
                def strictly(m_op):
                    m_op(lambda t: t[:, 0:3, 0:P], cst("strict").unsqueeze(1).broadcast_to([P, 3, P]))
                    return m_op(lambda t: t[:, 1, P:2 * P], cst("strict"))

                def softplus(h):
                    dve.drain()
                    dve.wait_ge(log_ready, at(l, SB_HEADS, h + 1))
                    if h >= 1:
                        dve.wait_ge(suffix_full, at(l, SB_HEADS, h))
                    for b, n in SB_BANKS:
                        V.scalar_tensor_tensor(hid[:, b, 0:n], sb_bank[h % 2][b][:, 0:n], 0.0, sb_e[:, b, 0:n],
                                               ALU.max, ALU.add)
                    dve.drain()
                    strictly(lambda f, mask: V.tensor_tensor(f(hid), f(hid), mask, ALU.mult)).then_inc(sp_ready, 1)

                def mask_shares(h):
                    dve.wait_ge(a_exp, at(l, SB_HEADS, h + 1))
                    t = sb_a[h % 2]
                    strictly(lambda f, mask: V.scalar_tensor_tensor(f(t), f(t), 1.0, mask, ALU.min, ALU.mult)
                             ).then_inc(a_ready, 1)

                softplus(0)
                for h in range(SB_HEADS):
                    if h + 1 < SB_HEADS:
                        softplus(h + 1)
                    mask_shares(h)
                for c in range(KC):
                    dve.wait_ge(acc_full, mix_full(l, T_HEAD + c + 1))
                    V.tensor_tensor(x_T[:, c, :], acc[(T_HEAD + c) % 2][:, :], x_T[:, c, :], ALU.add
                                    ).then_inc(acc_free[(T_HEAD + c) % 2], 1)
                    dve.drain().then_inc(x_final, 1)
                    square_sum(l * 3 + 2, c - 1)

            def first_max(x, top, hit, desc, n, best, out_):
                V.tensor_reduce(rx[:, 12, :, top:top + 1], x, AX.X, ALU.max)
                dve.drain()
                V.tensor_tensor(hit, x, rx[:, 12, :, top:top + 1].broadcast_to([P, TB, n]), ALU.is_equal)
                dve.drain()
                V.tensor_tensor(hit, hit, cst(desc).unsqueeze(1).broadcast_to([P, TB, n]), ALU.mult)
                dve.drain()
                V.tensor_reduce(rx[:, 12, :, best:best + 1], hit, AX.X, ALU.max)
                dve.drain()
                V.tensor_tensor(out_, hit, rx[:, 12, :, best:best + 1].broadcast_to([P, TB, n]), ALU.is_equal)
                dve.drain()

            def route(n, ps):
                V.tensor_tensor(lg[:, :, :], ps[:, 0:80].rearrange("p (b g) -> p b g", g=20),
                                rb[:, :].unsqueeze(1).broadcast_to([P, TB, 20]), ALU.add
                                ).then_inc(acc_free[n % 2], 1)
                dve.drain()
                gl = lg[:, :, 0:4]
                first_max(gl, 0, rx[:, 2, :, 0:4], "desc4", 4, 1, rx[:, 3, :, 0:4])
                V.tensor_tensor(rx[:, 0, :, 0:4], gl, rx[:, 12, :, 0:1].broadcast_to([P, TB, 4]), ALU.subtract
                                ).then_inc(route_pre, 1)
                V.tensor_scalar(rx[:, 4, :, 0:4], rx[:, 3, :, 0:4], -NEG, NEG, ALU.mult, ALU.add)
                dve.drain()
                V.tensor_tensor(rx[:, 5, :, :].rearrange("p b (g e) -> p b g e", e=4),
                                lg[:, :, 4:20].rearrange("p b (g e) -> p b g e", e=4),
                                rx[:, 4, :, 0:4].unsqueeze(3).broadcast_to([P, TB, 4, 4]), ALU.add)
                dve.drain()
                first_max(rx[:, 5, :, :], 2, rx[:, 6, :, :], "desc16", 16, 3, rx[:, 7, :, :])
                V.tensor_scalar(rx[:, 8, :, :], rx[:, 7, :, :], NEG, None, ALU.mult)
                dve.drain()
                V.tensor_tensor(rx[:, 8, :, :], rx[:, 8, :, :], rx[:, 5, :, :], ALU.add)
                dve.drain()
                first_max(rx[:, 8, :, :], 4, rx[:, 6, :, :], "desc16", 16, 5, rx[:, 9, :, :])
                V.tensor_tensor(member[:, :, :], rx[:, 7, :, :], rx[:, 9, :, :], ALU.add).then_inc(member_ready, 1)
                V.tensor_tensor(rx[:, 10, :, 0:1], rx[:, 12, :, 4:5], rx[:, 12, :, 2:3], ALU.subtract
                                ).then_inc(route_pre, 1)
                dve.wait_ge(route_exp, 1)
                V.tensor_reduce(rx[:, 12, :, 6:7], rx[:, 1, :, 0:4], AX.X, ALU.add)
                dve.wait_ge(route_exp, 2)
                V.tensor_scalar(rx[:, 12, :, 7:8], rx[:, 11, :, 0:1], 1.0, None, ALU.add)
                dve.drain()
                V.tensor_tensor(rx[:, 12, :, 7:8], rx[:, 12, :, 7:8], rx[:, 12, :, 6:7], ALU.mult)
                dve.drain()
                V.reciprocal(rx[:, 12, :, 8:9], rx[:, 12, :, 7:8])
                dve.drain()
                V.tensor_tensor(rx[:, 12, :, 9:10], rx[:, 12, :, 8:9], rx[:, 11, :, 0:1], ALU.mult)
                dve.drain()
                V.tensor_tensor(rx[:, 6, :, :], rx[:, 7, :, :], rx[:, 12, :, 8:9].broadcast_to([P, TB, 16]), ALU.mult)
                V.tensor_tensor(rx[:, 8, :, :], rx[:, 9, :, :], rx[:, 12, :, 9:10].broadcast_to([P, TB, 16]), ALU.mult)
                dve.drain()
                V.tensor_tensor(comb[:, :, :], rx[:, 6, :, :], rx[:, 8, :, :], ALU.add).then_inc(comb_done, 1)

            V.memset(eps[:, :], EPS).then_inc(eps_ready, 1)
            dve.wait_ge(params_loaded, N_PARAMS)
            for c in range(KC):
                dve.wait_ge(xt_full, c + 1)
                V.tensor_copy(x_T[:, c, :], turn[c % 2][:, :]).then_inc(x_final, 1)
                dve.drain()
                square_sum(0, c - 1)
            with dve.Fori(0, DEPTH) as l:
                norm(l * 3)
                slices(l, F1, 0, NSL, 0.5, l * 3 + 1)
                norm(l * 3 + 1)
                mix(l)
                norm(l * 3 + 2)
                slices(l, F2, 2 * NSL, NSL, 0.5, l * 3 + 3)

            norm(3 * L, x_T)
            norm(3 * L + 1)
            dve.wait_ge(rel_full, 1)
            V.tensor_tensor(rrow, turn[0][0:8, 0:384], cst("window_row", rows=8), ALU.add).then_inc(relrow_ready, 1)
            taken(dve, L, 0, T2["v", 3])
            taken(dve, L, 0, T2["v", 2])
            gx = [u_T[:, c, :] for c in range(4)] + [vtok[:, b, :] for b in range(TB)]
            gelu_pre_ops(gx[0], probs[:, 0, :])
            for j in range(8):
                t = probs[:, j % 2, :]
                if j + 1 < 8:
                    gelu_pre_ops(gx[j + 1], probs[:, (j + 1) % 2, :])
                dve.wait_ge(gelu_exp, 2 * L + j + 1)
                V.tensor_scalar(t, t, 1.0, None, ALU.add)
                dve.drain()
                V.reciprocal(t, t)
                dve.drain()
                V.tensor_tensor(gx[j], gx[j], t, ALU.mult)
            dve.drain()
            for b in range(TB):
                V.tensor_reduce(lnst[:, 0, b:b + 1], vtok[:, b, :], AX.X, ALU.add)
            dve.drain()
            V.tensor_scalar(lnst[:, 0, :], lnst[:, 0, :], 1.0 / 512, None, ALU.mult)
            dve.drain()
            for b in range(TB):
                V.tensor_scalar(vtok[:, b, :], vtok[:, b, :], lnst[:, 0, b:b + 1], None, ALU.subtract)
            dve.drain()
            for b in range(TB):
                dve.drain()
                V.tensor_tensor(probs[:, 0, :], vtok[:, b, :], vtok[:, b, :], ALU.mult)
                dve.drain()
                m = V.tensor_reduce(lnst[:, 1, b:b + 1], probs[:, 0, :], AX.X, ALU.add)
            m.then_inc(ln_pre, 1)
            dve.wait_ge(ln_rstd, 1)
            dve.wait_ge(ws_loaded, 32)
            for b in range(TB):
                m = V.scalar_tensor_tensor(vtok[:, b, :], vtok[:, b, :], lnst[:, 3, b:b + 1], gv, ALU.mult, ALU.mult)
            m.then_inc(vn_ready, 1)
            for n, (name, i, ld) in enumerate(SEC_T):
                ps = acc[n % 2]
                if name in ("wst", "sv", "pa", "pb", "wo", "route", "rank", "combt", "rankt"):
                    dve.wait_ge(acc_full, full_at(L, 0, full2(n + 1)))
                if name == "gate":
                    taken(dve, L, 0, n)
                    t = (sig_a if i < 8 else sig_b)[:, i % 8, :]
                    V.tensor_scalar(t, t, 1.0, None, ALU.add)
                    dve.drain()
                    V.reciprocal(t, t)
                elif name == "wst":
                    V.tensor_tensor(ws_T[:, 4 * i:4 * i + 4, :], ps[:, :].rearrange("p (g t) -> p g t", t=P),
                                    cst("tril").unsqueeze(1).broadcast_to([P, 4, P]), ALU.mult
                                    ).then_inc(acc_free[n % 2], 1)
                elif name == "sv":
                    V.tensor_tensor(ab_T[:, i, :], ps[:, :], u_T[:, i, :], ALU.mult).then_inc(acc_free[n % 2], 1)
                elif (name, i) == ("swa", 0):
                    dve.wait_ge(bias_loaded, 16)
                    attend(L, NU, 0, NSW, swa_info, True)
                elif name == "pa":
                    V.tensor_tensor(sig_a[:, i, :], ps[:, :], sig_a[:, i, :], ALU.mult).then_inc(acc_free[n % 2], 1)
                elif name == "pb":
                    dve.drain()
                    V.tensor_tensor(rt[:, :], ps[:, :], sig_b[:, i, :], ALU.mult).then_inc(acc_free[n % 2], 1)
                    dve.drain()
                    V.tensor_tensor(sig_a[:, i, :], sig_a[:, i, :], rt[:, :], ALU.add).then_inc(merged_ready, 1)
                elif name == "wo":
                    V.tensor_tensor(x_T[:, i, :], ps[:, :], x_T[:, i, :], ALU.add).then_inc(acc_free[n % 2], 1)
                    dve.drain().then_inc(x_final, 1)
                    square_sum(3 * L + 2, i - 1)
                    if i == KC - 1:
                        norm(3 * L + 2)
                elif name == "route":
                    route(n, ps)
                elif name == "rank":
                    V.tensor_scalar(rank[:, :, :], member[:, :, :], -4.0 * S, 4.0 * S, ALU.mult, ALU.add)
                    V.tensor_reduce(passes[:, 0:1], ps[:, 64:80], AX.X, ALU.max)
                    dve.drain()
                    V.tensor_tensor(rank[:, :, :], rank[:, :, :], ps[:, 0:64].rearrange("p (b e) -> p b e", e=16),
                                    ALU.add).then_inc(acc_free[n % 2], 1)
                    dve.drain().then_inc(rank_ready, 1)
                    V.tensor_scalar(passes[:, 1:2], passes[:, 0:1], float(P), 1.0, ALU.is_gt, ALU.add)
                    for j in range(2, TB):
                        dve.drain()
                        V.scalar_tensor_tensor(passes[:, 1:2], passes[:, 0:1], float(j * P), passes[:, 1:2],
                                               ALU.is_gt, ALU.add)
                    dve.drain()
                    V.tensor_copy(n_passes[:, :], passes[:, 1:2]).then_inc(passes_ready, 1)
                elif name in ("combt", "rankt"):
                    V.tensor_copy(rows_T[:, 0 if name == "combt" else 1, :], ps[0:16, :]).then_inc(acc_free[n % 2], 1)

            def choose(e, p_, q):
                V.tensor_tensor(pick[q], cst("iota").rearrange("p (a t) -> p a t", t=P)[:, bass.ds(p_, 1), :]
                                .broadcast_to([P, TB, P]),
                                rank[:, :, bass.ds(e, 1)].broadcast_to([P, TB, P]), ALU.is_equal
                                ).then_inc(pick_ready, 1)

            def take(pair, q):
                for c in range(KC):
                    dve.wait_ge(scattered, pair * 16 + 8 * q + c + 1)
                    V.tensor_tensor(x_T[:, c, :], acc[c % 2][:, :], x_T[:, c, :], ALU.add
                                    ).then_inc(scatter_taken, 1)

            def step(pair, q, e, p_, first=False, last=False):
                if not last:
                    choose(e + 1, p_, 1 - q)
                dve.wait_ge(xsig_ready, pair * 2 + q + 1)
                V.tensor_scalar(et[:, 0, :], et[:, 0, :], 1.0, None, ALU.add)
                dve.drain()
                V.reciprocal(rt[:, :], et[:, 0, :])
                dve.drain()
                V.tensor_tensor(rt[:, :], rt[:, :], score[0][:, :], ALU.mult)
                dve.drain()
                V.tensor_tensor(xhid, rt[:, :], score[1][:, :], ALU.mult).then_inc(xhid_ready, 1)
                dve.wait_ge(rows_loaded[q], pair * 16 + 16)
                V.scalar_tensor_tensor(place[q], rows[q][:, 1, :], cst("slot_number")[:, bass.ds(p_, 1)],
                                       rows[q][:, 0, :], ALU.is_equal, ALU.mult).then_inc(place_ready, 1)
                if not first:
                    take(pair - 1 + q, 1 - q)

            dve.drain()
            n_p = dve.value_load(n_passes[0:1, 0:1], min_val=1, max_val=TB)
            with dve.Fori(0, n_p) as ps_:
                pair0 = dve.snap(ps_ * (NX // 2))
                choose(0, ps_, 0)
                step(pair0, 0, 0, ps_, first=True)
                with dve.Fori(0, NX // 2 - 1) as i:
                    pair = dve.snap(pair0 + i)
                    step(pair, 1, i * 2 + 1, ps_)
                    step(pair + 1, 0, i * 2 + 2, ps_)
                step(pair0 + (NX // 2 - 1), 1, NX - 1, ps_, last=True)
                take(pair0 + (NX // 2 - 1), 1)
            dve.drain().then_inc(x_final, KC)
            for c in range(KC):
                dve.drain()
                square_sum(3 * L + 3, c)
            norm(3 * L + 3)



def kernel(**inputs):
    import concourse.bacc as bacc
    from concourse.bass_utils import run_bass_kernel_spmd as run

    nc = bacc.Bacc("TRN2", target_bir_lowering=False, num_devices=1)
    arrays, args = {}, {}
    tensors = {**inputs, "const": constant_table()}
    for name, value in tensors.items():
        v = np.ascontiguousarray(value)
        arrays[f"in_{name}"] = v
        args[name] = nc.dram_tensor(f"in_{name}", v.shape, mybir.dt.from_np(v.dtype), kind="ExternalInput").ap()
    out = nc.dram_tensor("out", (1, S, D), F32, kind="ExternalOutput").ap()
    build(nc, args, out)
    r = run(nc, [arrays], core_ids=[0])
    return r.results[0]["out"]
```

```python
from contextlib import ExitStack

import numpy as np

import concourse.bass as bass
from concourse import mybir

ALU = mybir.AluOpType
ACT = mybir.ActivationFunctionType
AX = mybir.AxisListType
F32 = mybir.dt.float32
F32R = mybir.dt.float32r

P = 128
S = 512
D = 1024
KC = D // P
TB = S // P
EPS = 1e-6
NEG = -1e30
DEPTH = 2
D_FF = 2816
FS = 256
GC = 0.7978845608028654
HD = 64

C_CQ, C_CKV, C_KR, C_NQ, C_KC, C_VC, C_KS, C_VS, C_KW, C_VW, C_G, C_SQ, C_SK, C_SV, C_END = (
    int(v) for v in np.cumsum([0, 256, 128, 32, 384, 128, 128, 128, 128, 128, 128, 18, 256, 256, 256]))

_CONST = {}
_CN = 0
for _name, _n in (("ident", 128), ("ones", 128), ("negones", 128), ("negtri", 128), ("causal", 128),
                  ("strict", 128), ("tril", 128), ("r_mla", 96), ("r_nsa", 128), ("cos_mla", 512),
                  ("sin_mla", 512), ("cos_nsa", 512), ("sin_nsa", 512), ("cmp_mask", 4 * 31),
                  ("cmp_valid", 4), ("desc4", 4), ("desc16", 16), ("group_rows", 4 * 128),
                  ("bucket_rows", 384), ("window_row", 384), ("iota", 512), ("slot_number", 4)):
    _CONST[_name] = (_CN, _CN + _n)
    _CN += _n


def constant_table():
    t = np.zeros((P, _CN), np.float32)

    def put(name, a):
        a = np.asarray(a, np.float32)
        t[:a.shape[0], _CONST[name][0]:_CONST[name][0] + a.shape[1]] = a

    r = np.arange(P)
    put("ident", np.eye(P))
    put("ones", np.ones((P, P)))
    put("negones", -np.ones((P, P)))
    put("negtri", -1.0 * (r[:, None] >= r[None, :]))
    put("causal", np.where(r[None, :] <= r[:, None], 0.0, NEG))
    put("strict", r[:, None] < r[None, :])
    put("tril", r[:, None] <= r[None, :])
    pos = np.arange(S, dtype=np.float32)

    def rope(rows, start, half):
        freq = np.float32(500000.0) ** (-np.arange(half, dtype=np.float32) / np.float32(half))
        ang = (pos[:, None] * freq[None, :].astype(np.float32)).astype(np.float32).T
        rot = np.zeros((rows, rows), np.float32)
        c, s = np.ones((rows, S), np.float32), np.zeros((rows, S), np.float32)
        for b in start:
            for i in range(half):
                rot[b + half + i, b + i] = -1.0
                rot[b + i, b + half + i] = 1.0
            c[b:b + 2 * half] = np.concatenate([np.cos(ang), np.cos(ang)])
            s[b:b + 2 * half] = np.concatenate([np.sin(ang), np.sin(ang)])
        return rot, c, s

    for name, args in (("mla", (96, (64,), 16)), ("nsa", (128, (0, 64), 8))):
        rot, c, s = rope(*args)
        put("r_" + name, rot)
        put("cos_" + name, c)
        put("sin_" + name, s)
    q = (np.arange(TB)[None, :, None] * P + r[:, None, None])
    put("cmp_mask", np.where(np.arange(31)[None, None, :] * 16 + 31 <= q, 0.0, NEG).reshape(P, -1))
    put("cmp_valid", (q[:, :, 0] >= 31))
    put("desc4", np.tile(4.0 - np.arange(4), (P, 1)))
    put("desc16", np.tile(16.0 - np.arange(16), (P, 1)))
    g = np.zeros((8, 4, 128), np.float32)
    for i in range(8):
        g[i, i // 2, (i % 2) * 64:(i % 2) * 64 + 64] = 1.0
    put("group_rows", g.reshape(8, -1))
    dist = 255 - np.arange(384)
    ok = (dist >= 0) & (dist < 128)
    nf = np.maximum(dist, 1).astype(np.float32)
    large = 16 + (np.log(nf / np.float32(16)) / np.float32(np.log(8.0)) * np.float32(16)).astype(np.int32)
    bucket = np.where(dist < 16, dist, np.minimum(large, 31))
    rows = np.zeros((32, 384), np.float32)
    for j in range(384):
        if ok[j]:
            rows[bucket[j], j] = 1.0
    put("bucket_rows", rows)
    put("iota", np.tile(np.arange(S), (P, 1)))
    put("slot_number", r[:, None] + P * np.arange(S // P)[None, :])
    put("window_row", np.tile(np.where(ok, 0.0, NEG), (8, 1)))
    return t


MIX = (
    [("cq", 0, 0, "act"), ("cq", 1, 0, "act"), ("ckv", 0, 1, "act"), ("kr", 0, 1, "act")]
    + [("nq", 0, 2, "act"), ("nq", 1, 2, "act"), ("nq", 2, 3, "act"), ("kc", 0, 3, "act")]
    + [("vc", 0, 4, "act"), ("ks", 0, 4, "act"), ("vsw", 0, 5, "act"), ("vsw", 1, 5, "act")]
    + [("kw", 0, 6, "act"), ("gate", 0, 6, "dve")]
    + [("sq", 0, 7, "act"), ("sq", 1, 7, "act"), ("sk", 0, 8, "act"), ("sk", 1, 8, "act")]
    + [("sv", 0, 9, "act"), ("sv", 1, 9, "act")]
    + [("uq", h, 10, "act") for h in range(6)]
    + [("kn", h, 11, "act") for h in range(6)]
    + [("mv", b, 11, "act") for b in range(TB)]
    + [("xs_v", g, None, "act") for g in range(2)]
    + [("rope", i, None, "dve") for i in (10, 0, 1, 2, 3)]
    + [("xs_k", g, None, "act") for g in range(2)]
    + [("rope", i, None, "dve") for i in (4, 5, 6, 7, 8, 9, 11, 12)]
    + [("cmp", 0, None, "act")]
)
TICKET = {(j[0], j[1]): i for i, j in enumerate(MIX)}
HEADS = [("mla", h) for h in range(6)] + [("nsa", h) for h in range(6)]
SB_HEADS = 4
T_LIN = len(MIX)
T_HEAD = T_LIN + len(HEADS) + SB_HEADS
T_MIX = T_HEAD + KC
NSL = D_FF // FS
T_FF = NSL * KC
TL = 2 * T_FF + T_MIX
assert T_MIX % 2 == 0 and T_FF % 2 == 0
NHD = len(HEADS)
TLF = TL - NHD
N_SPLIT = 10
LAST_TICKET = {}
for _i, _j in enumerate(MIX):
    if _j[2] is not None:
        LAST_TICKET[_j[2]] = _i

MIX_DMAS = [1, 1, 4, 3, 1, 2, 2, 1, 1, 1, 1, 1, 2, 2, 1, 1, 1, 1]
W_OUT0 = 14
NLM = len(MIX_DMAS)
LAST_TICKET[12] = LAST_TICKET[13] = TICKET["cmp", 0]
N_ROPE = 13
V_ROPES, K_ROPES = (1, 8), (8, 13)
W_DONE = {n % 3: T_HEAD + 2 * (n - W_OUT0) + 2 for n in range(W_OUT0, NLM)}
SLOT_DMAS = [2 * NSL + sum(MIX_DMAS[s::3]) for s in range(3)]

SB_PLACE = {0: (0, 0), 1: (1, P), 2: (2, 0), 3: (1, 0)}
UNITS = []
for _kind, _h in HEADS:
    for _i in range(TB):
        br = ["mla"] if _kind == "mla" else ["cmp", "sel", "win"]
        for _b in br:
            UNITS.append((_kind, _h, _i, _b, _b == br[0], _b == br[-1]))
NU = len(UNITS)
NSA_HALF = lambda h: (h // 3, h % 3)

SWA_UNITS = [(h, i) for h in range(8) for i in range(TB)]
NX = 16
XF = 512


def run_slices(eng, n, up_step, down_step):
    up_step(0, 0)
    with eng.Fori(0, (n - 1) // 2) as i:
        up_step(i * 2 + 1, 1)
        down_step(i * 2, 0, False)
        up_step(i * 2 + 2, 0)
        down_step(i * 2 + 1, 1, False)
    down_step(n - 1, 0, True)


def build(nc, a, out):
    with ExitStack() as ctx:
        def sb(name, shape):
            return ctx.enter_context(nc.sbuf_tensor(name, shape, F32))

        def sem(name):
            return ctx.enter_context(nc.semaphore(name))

        const = sb("const", [P, _CN])

        def cst(name, rows=P, lo=0, hi=None):
            c0, c1 = _CONST[name]
            return const[0:rows, c0 + lo:(c1 if hi is None else c0 + hi)]

        ident = cst("ident")
        x_T = sb("x_T", [P, KC, S])
        place_of = {"h_T": nc.sbuf_base}
        h_T = sb("h_T", [P, KC, S])
        place_of["o_T"] = nc.sbuf_base
        o_T = sb("o_T", [P, KC, S])
        slot = [sb(f"weights{s}", [P, 2048]) for s in range(3)]
        place_of["hid"] = nc.sbuf_base
        hid = sb("hid", [P, 4, S])
        et = sb("exp_tile", [P, 2, S])
        rt = sb("recip_tile", [P, S])
        place_of["lora"] = nc.sbuf_base
        lora = sb("lora", [P, 4, S])
        rstd = sb("rstd", [P, S])
        place_of["arena"] = nc.sbuf_base
        arena = sb("arena", [P, 18000])
        probs = sb("probs", [P, 3, S])
        probs_T = sb("probs_T", [P, 2, S])
        gains = sb("gains", [P, 3 * DEPTH + 4, KC])
        lgains = sb("lora_gains", [P, DEPTH, 3])
        gbias = sb("gate_bias", [P, DEPTH, 18])
        cmp_w2 = sb("cmp_w2", [P, 2, HD])
        cmp_pos = sb("cmp_pos", [P, 2, 16])
        hid_cmp = sb("hid_cmp", [P, 2, 62])
        cmp_t = sb("cmp_t", [P, 4, 62])
        bias_c = sb("bias_c", [P, 2])
        stats = sb("stats", [P, 4, 4])
        gates = sb("gates", [P, TB, 18])
        gates_e = sb("gates_e", [P, TB, 18])
        vcmp = sb("vcmp", [31, 2, HD])
        kcmp_T = sb("kcmp_T", [P, 31])
        lnst = sb("lnst", [P, 4, TB])
        sinks = sb("sinks", [P, 8])
        rel = sb("rel", [32, 8])
        bs = sb("bs", [8, P])
        rw = sb("rw", [P, KC, 20])
        rb = sb("rb", [P, 20])
        lg = sb("lg", [P, TB, 20])
        rx = sb("rx", [P, 14, TB, 16])
        comb = sb("comb", [P, TB, 16])
        member = sb("member", [P, TB, 16])
        rank = sb("rank", [P, TB, 16])
        passes = sb("passes", [P, 2])
        n_passes = ctx.enter_context(nc.sbuf_tensor("n_passes", [P, 1], mybir.dt.int32))
        eps = sb("eps", [P, 1])

        off = [0]

        def view(*dims):
            n = int(np.prod(dims))
            v = arena[:, off[0]:off[0] + n]
            off[0] += n
            if len(dims) == 2:
                v = v.rearrange("p (a b) -> p a b", b=dims[1])
            return v

        q6 = view(6, S)
        k6 = view(6, S)
        mv = view(TB, 384)
        nq = view(3, S)
        nk = view(4, S)
        vsw = view(2 * TB, P)
        vs, vw = (vsw.rearrange("p (b t) d -> p b t d", t=2)[:, :, t, :] for t in range(2))
        sq_T = view(2, S)
        sk_T = view(2, S)
        sv = view(TB, 256)
        pairs = [view(2, S), view(2, S)]
        assert off[0] <= 18000, off[0]
        off[0] = 0
        u_T = view(4, S)
        vtok = view(TB, S)
        q2 = view(4, S)
        k2 = view(S)
        v2 = view(TB, P)
        sig_a = view(KC, S)
        sig_b = o_T
        bias_t = view(8, 256)
        gv = view(S)
        ab_T = view(8, S)
        assert off[0] <= 18000, off[0]
        ws_T = lora[:, 0:2, :].rearrange("p a (b c) -> p (a b) c", c=P)
        ws_n = lora[:, 2:4, :].rearrange("p a (b c) -> p (a b) c", c=P)
        rrow = rt[0:8, 0:384]
        big = [arena[:, k * 4096:(k + 1) * 4096].rearrange("p (c f) -> p c f", f=XF) for k in range(4)]
        xg_w, xu_w = [big[0], big[2]], [big[1], big[3]]
        xd = ([t[:, :].rearrange("p (c d) -> p c d", d=D) for t in slot]
              + [h_T[:, 0:4, :].rearrange("p a b -> p (a b)").rearrange("p (c d) -> p c d", d=D)])
        xd_w = [xd[0:2], xd[2:4]]
        h_tok = o_T[:, :, :].rearrange("p a b -> p (a b)").rearrange("p (b d) -> p b d", d=D)
        mine_T = [h_T[:, 4 + 2 * q:6 + 2 * q, :].rearrange("p a (c t) -> p (a c) t", t=P) for q in range(2)]
        pick = [lora[:, q, :].rearrange("p (b t) -> p b t", t=P) for q in range(2)]
        place = [lora[:, 2 + q, :] for q in range(2)]
        rows = [probs_T[:, :, :], arena[:, 16384:16384 + 2 * S].rearrange("p (a t) -> p a t", t=S)]
        rows_T = hid[0:16, 2:4, :]
        xhid, xhid_T, y_slot = hid[:, 0, :], hid[:, 1, :], hid[:, 2:4, :]

        def split_at(name, shape, region, first=0):
            return nc.alloc_sbuf_tensor_at(name, shape, F32R, offset=place_of[region] + 4 * first)

        h_hi = split_at("h_hi", [P, KC, S], "arena")
        h_lo = split_at("h_lo", [P, KC, S], "arena", 4096)
        w_hi = [split_at("gate_hi", [P, 2048], "arena", 8192), split_at("up_hi", [P, 2048], "arena", 10240),
                split_at("down_hi", [P, 2048], "o_T")]
        w_lo = [split_at("gate_lo", [P, 2048], "arena", 12288), split_at("up_lo", [P, 2048], "arena", 14336),
                split_at("down_lo", [P, 2048], "o_T", 2048)]
        hid_hi = split_at("hid_hi", [P, 4, S], "hid")
        hid_lo = split_at("hid_lo", [P, 4, S], "lora")

        mix_h = [split_at("mix_h_hi", [P, KC, S], "o_T"), split_at("mix_h_lo", [P, KC, S], "h_T")]
        mix_w = [[split_at("mix_w_hi0", [P, 2048], "arena"), split_at("mix_w_lo0", [P, 2048], "arena", 2048)],
                 [split_at("mix_w_hi1", [P, 2048], "arena", 4096), split_at("mix_w_lo1", [P, 2048], "hid")]]
        LOAD_COLS = [KC * w for w in (256, 160, 256, 256, 256, 256, 146, 256, 256, 256)]

        acc = [ctx.enter_context(nc.psum_tensor(f"acc{i}", [P, S], F32)) for i in range(2)]
        score = [ctx.enter_context(nc.psum_tensor(f"score{i}", [P, S], F32)) for i in range(4)]
        turn = [ctx.enter_context(nc.psum_tensor(f"turn{i}", [P, S], F32)) for i in range(2)]

        sb_bank = [score[0:3], [score[3], turn[0], turn[1]]]
        sb_a = [lora, probs]
        sb_e = q6

        def sb_cols(t, j, lo, hi):
            b, o = SB_PLACE[j]
            return t[:, b, o + lo:o + hi]

        SB_BANKS = ((0, S), (1, S), (2, 2 * P))

        rel_dram = nc.dram_tensor("rel_scratch", [8, P, 384], F32, kind="Internal").ap()
        rows_dram = nc.dram_tensor("rows_scratch", [16, 2, S], F32, kind="Internal").ap()

        params_loaded = sem("params_loaded")
        x_loaded = sem("x_loaded")
        w_loaded = [sem(f"w_loaded{s}") for s in range(3)]
        small_loaded = sem("small_loaded")
        acc_full = sem("acc_full")
        acc_free = [sem(f"acc_free{i}") for i in range(2)]
        x_final = sem("x_final")
        squared = sem("squared")
        summed = sem("summed")
        ssq_full = sem("ssq_full")
        rstd_ready = sem("rstd_ready")
        h_ready = sem("h_ready")
        gu_full = sem("gu_full")
        gate_taken = sem("gate_taken")
        w_hi_ready = [sem(f"w_hi_ready{s}") for s in range(3)]
        w_split = [sem(f"w_split{s}") for s in range(3)]
        mix_w_hi_ready = sem("mix_w_hi_ready")
        mix_w_split = sem("mix_w_split")
        h_hi_ready = sem("h_hi_ready")
        h_split = sem("h_split")
        sig_ready = sem("sig_ready")
        hid_done = sem("hid_done")
        lsq_ready = sem("lsq_ready")
        lssq_full = sem("lssq_full")
        lrstd_ready = sem("lrstd_ready")
        lora_ready = sem("lora_ready")
        rope_ready = sem("rope_ready")
        gate_exp = sem("gate_exp")
        gelu_pre = sem("gelu_pre")
        gelu_exp = sem("gelu_exp")
        hidc_full = sem("hidc_full")
        hidc_ready = sem("hidc_ready")
        s_full = sem("s_full")
        max_ready = sem("max_ready")
        exp_ready = sem("exp_ready")
        p_ready = sem("p_ready")
        t_full = sem("t_full")
        pt_ready = sem("pt_ready")
        pv_done = sem("pv_done")
        z_full = sem("z_full")
        log_ready = sem("log_ready")
        sp_ready = sem("sp_ready")
        suffix_full = sem("suffix_full")
        a_exp = sem("a_exp")
        a_ready = sem("a_ready")
        eps_ready = sem("eps_ready")
        rel_full = sem("rel_full")
        comb_done = sem("comb_done")
        yt_full = sem("yt_full")
        xt_full = sem("xt_full")
        turned = sem("turned")
        g2_pre = sem("g2_pre")
        g2_exp = sem("g2_exp")
        ln_pre = sem("ln_pre")
        ln_rstd = sem("ln_rstd")
        vn_ready = sem("vn_ready")
        ws_loaded = sem("ws_loaded")
        ws_ready = sem("ws_ready")
        relrow_ready = sem("relrow_ready")
        rel_stored = sem("rel_stored")
        bias_loaded = sem("bias_loaded")
        merged_ready = sem("merged_ready")
        route_pre = sem("route_pre")
        route_exp = sem("route_exp")
        rows_stored = sem("rows_stored")
        member_ready = sem("member_ready")
        rank_ready = sem("rank_ready")
        passes_ready = sem("passes_ready")
        htok_full = sem("htok_full")
        htok_ready = sem("htok_ready")
        xgate_loaded = [sem(f"xgate_loaded{i}") for i in range(2)]
        xup_loaded = [sem(f"xup_loaded{i}") for i in range(2)]
        xdown_loaded = [sem(f"xdown_loaded{i}") for i in range(2)]
        rows_loaded = [sem(f"rows_loaded{i}") for i in range(2)]
        pick_ready = sem("pick_ready")
        gathered = sem("gathered")
        mine_ready = sem("mine_ready")
        xgu_full = sem("xgu_full")
        xsig_ready = sem("xsig_ready")
        xhid_ready = sem("xhid_ready")
        xhid_turned = sem("xhid_turned")
        xhidt_ready = sem("xhidt_ready")
        xdown_full = sem("xdown_full")
        yslot_ready = sem("yslot_ready")
        place_ready = sem("place_ready")
        scattered = sem("scattered")
        scatter_taken = sem("scatter_taken")
        y_ready = sem("y_ready")
        y_stored = sem("y_stored")

        def at(l, per_layer, n):
            return l * per_layer + n

        B1, BM, B2 = 0, T_FF, T_FF + T_MIX
        F1, FM, F2 = 0, T_FF, T_FF + T_MIX - NHD
        TG = 4 * NSL
        def full_at(l, base, n):
            return at(l, TLF, base + n + 1)

        def mix_full(l, n):
            return full_at(l, FM, n if n <= T_LIN else n - NHD)

        def free_at(l, base, n):
            return at(l, TL // 2, base // 2 + n // 2 + 1)

        def gu_at(l, base, n):
            return at(l, TG, base + n + 1)

        def slices_at(l, ph, n):
            return at(l, 2 * NSL, ph * NSL + n + 1)

        def dmajor(name, p=P):
            return a[name].rearrange("l (c p) f -> l p c f", p=p)

        w_gate = [dmajor("ffn1_w_gate"), dmajor("ffn2_w_gate")]
        w_up = [dmajor("ffn1_w_up"), dmajor("ffn2_w_up")]
        w_down = [dmajor("ffn1_w_down"), dmajor("ffn2_w_down")]
        w_in, w_out = dmajor("w_in"), dmajor("w_out")
        w_uq, w_ukv = dmajor("mla_w_uq"), dmajor("mla_w_ukv")
        x_tok = a["x"].rearrange("a (b p) d -> p (a b) d", p=P)
        y_tok = out.rearrange("a (b p) d -> p (a b) d", p=P)
        x_in = arena[:, 0:4096].rearrange("p (b d) -> p b d", d=D)
        y_out = x_in
        w_in2, w_out2 = dmajor("w_in_2")[0], dmajor("w_out_2")[0]
        w_pa, w_pb = dmajor("w_proj_a_2")[0], dmajor("w_proj_b_2")[0]
        x_gate = a["expert_w_gate_2"].rearrange("a e (c p) f -> (a e) p c f", p=P)
        x_up = a["expert_w_up_2"].rearrange("a e (c p) f -> (a e) p c f", p=P)
        x_down = a["expert_w_down_2"].rearrange("a e (c p) f -> (a e) p c f", p=P)

        def s3(s, c, n):
            return slot[s][:, 0:c * n].rearrange("p (c n) -> p c n", n=n)

        SECOND = ([("u", 0), ("u", 256), ("v", 0), ("v", 256), ("q", 0), ("q", 256), ("kv", 0)]
                  + [("gate", c) for c in range(0, 2048, 256)]
                  + [("pa", 0), ("pa", 512), ("pb", 0), ("pb", 512)]
                  + [("wo", c) for c in range(0, 1024, 256)])
        SEC_DMAS = [4 if n == "q" else 1 for n, _ in SECOND]
        NSEC = len(SECOND)

        SEC_T = ([("u", c, c // 2) for c in range(4)]
                 + [("v", b, 2 + b // 2) for b in range(4)]
                 + [("q", c, 4 + c // 2) for c in range(4)] + [("k", 0, 6), ("vtok", 0, 6)]
                 + [("gate", c, 7 + c // 2) for c in range(16)]
                 + [("wst", b, None) for b in range(2)]
                 + [("sv", c, None) for c in range(4)]
                 + [("swa", h, None) for h in range(8)]
                 + [("pa", c, 15 + c // 4) for c in range(8)]
                 + [("pb", c, 17 + c // 4) for c in range(8)]
                 + [("wo", c, 19 + c // 2) for c in range(8)]
                 + [("route", 0, None), ("rank", 0, None), ("combt", 0, None), ("rankt", 0, None)])
        NT2 = len(SEC_T)
        assert NT2 % 2 == 0 and NSEC % 3 == 2
        T2 = {(n, i): j for j, (n, i, _) in enumerate(SEC_T)}
        LAST2 = {ld: j for j, (_, _, ld) in enumerate(SEC_T) if ld is not None}
        SWA0 = T2["swa", 0]

        def full2(n):
            return n - max(0, min(n - SWA0, 8))

        block = ctx.enter_context(nc.Block())

        @block.sync
        def _(sp):
            sp.dma_start(x_in, x_tok).then_inc(x_loaded, 16)
            sp.dma_start(const[:, :], a["const"]).then_inc(x_loaded, 16)
            with nc.allow_non_contiguous_dma(reason="small parameter vectors, once"):
                for i, name in enumerate(("ffn1_norm", "mix_norm", "ffn2_norm")):
                    for l in range(DEPTH):
                        sp.dma_start(gains[:, 3 * l + i, :],
                                     a[name][l].rearrange("(c p) -> p c", p=P)).then_inc(params_loaded, 16)
                for i, name in enumerate(("attn_norm_g_2", "ffn_norm_g_2")):
                    sp.dma_start(gains[:, 3 * DEPTH + 1 + i, :],
                                 a[name][0].rearrange("(c p) -> p c", p=P)).then_inc(params_loaded, 16)
                for i, name in ((0, "final_norm"), (3, "final_norm_g_2")):
                    sp.dma_start(gains[:, 3 * DEPTH + i, :],
                                 a[name].rearrange("(c p) -> p c", p=P)).then_inc(params_loaded, 16)
                for l in range(DEPTH):
                    sp.dma_start(lgains[:, l, 0:2],
                                 a["mla_q_norm"][l].rearrange("(c p) -> p c", p=P)).then_inc(params_loaded, 16)
                    sp.dma_start(lgains[:, l, 2:3],
                                 a["mla_kv_norm"][l].rearrange("(c p) -> p c", p=P)).then_inc(params_loaded, 16)
                sp.dma_start(gbias[:, :, :],
                             a["nsa_gate_bias"].partition_broadcast(P)).then_inc(params_loaded, 16)
                sp.dma_start(sinks[:, :],
                             a["attn_sinks_2"][0].partition_broadcast(P)).then_inc(params_loaded, 16)
                sp.dma_start(rel[:, :], a["rel_bias_2"]).then_inc(params_loaded, 16)
                sp.dma_start(bs[:, :], a["gm_b_spatial_2"][0]).then_inc(params_loaded, 16)
                sp.dma_start(rb[:, 0:4], a["router_group_b_2"][0].partition_broadcast(P)).then_inc(params_loaded, 16)
                sp.dma_start(rb[:, 4:20], a["router_expert_b_2"][0].rearrange("g e -> (g e)")
                             .partition_broadcast(P)).then_inc(params_loaded, 16)
                sp.dma_start(rw[:, :, 0:4],
                             a["router_group_w_2"][0].rearrange("(c p) g -> p c g", p=P)).then_inc(params_loaded, 16)
                for g in range(4):
                    sp.dma_start(rw[:, :, 4 + 4 * g:8 + 4 * g],
                                 a["router_expert_w_2"][0, g].rearrange("(c p) e -> p c e", p=P)
                                 ).then_inc(params_loaded, 16)

            def ffn(l, ph):
                def load(s, sl, ap):
                    if not isinstance(sl, int) or sl > 0 or ph == 0:
                        sp.wait_ge(w_split[s], slices_at(l, ph, sl))
                    else:
                        sp.wait_ge(acc_full, mix_full(l, W_DONE[s]))
                    sp.dma_start(s3(s, KC, FS) if s < 2 else s3(2, 2, D), ap).then_inc(w_loaded[s], 16)

                def up(sl, par):
                    load(0, sl, w_gate[ph][l][:, :, bass.ds(sl * FS, FS)])
                    load(1, sl, w_up[ph][l][:, :, bass.ds(sl * FS, FS)])

                def down(sl, par, last):
                    load(2, sl, w_down[ph][l][:, bass.ds(sl * 2, 2), :])

                run_slices(sp, NSL, up, down)

            def mix_loads(l):
                wi = w_in[l]

                def cols(s, c0, n, at_=0, w=256):
                    sp.dma_start(s3(s, KC, w)[:, :, at_:at_ + n], wi[:, :, c0:c0 + n]).then_inc(w_loaded[s], 16)

                for n in range(NLM):
                    s = n % 3
                    if n < 3:
                        sp.wait_ge(w_split[s], slices_at(l, 1, 0))
                    else:
                        o = n - 3
                        sp.wait_ge(acc_full, mix_full(l, (LAST_TICKET[o] if o < W_OUT0 else
                                                          T_HEAD + 2 * (o - W_OUT0) + 1) + 1))
                    if n == 0:
                        cols(s, C_CQ, 256)
                    elif n == 1:
                        cols(s, C_CKV, 160, w=160)
                    elif n == 2:
                        for c in range(2):
                            for g in range(2):
                                cols(s, C_NQ + HD * (3 * g + c), HD, at_=128 * c + 64 * g)
                    elif n == 3:
                        for g in range(2):
                            cols(s, C_NQ + HD * (3 * g + 2), HD, at_=64 * g)
                        cols(s, C_KC, 128, at_=128)
                        with nc.allow_non_contiguous_dma(reason="small parameters"):
                            sp.dma_start(cmp_w2[:, 0, :], a["nsa_cmp_w2_k"][l]).then_inc(small_loaded, 16)
                            sp.dma_start(cmp_w2[:, 1, :], a["nsa_cmp_w2_v"][l]).then_inc(small_loaded, 16)
                            sp.dma_start(cmp_pos[:, 0, :], a["nsa_cmp_pos_k"][l].rearrange("(c q) d -> (q d) c", q=2)
                                         ).then_inc(small_loaded, 16)
                            sp.dma_start(cmp_pos[:, 1, :], a["nsa_cmp_pos_v"][l].rearrange("(c q) d -> (q d) c", q=2)
                                         ).then_inc(small_loaded, 16)
                    elif n == 4:
                        cols(s, C_VC, 256)
                    elif n == 5:
                        cols(s, C_VS, 128)
                        cols(s, C_VW, 128, at_=128)
                    elif n == 6:
                        cols(s, C_KW, 128, w=146)
                        cols(s, C_G, 18, at_=128, w=146)
                    elif n == 7:
                        cols(s, C_SQ, 256)
                    elif n == 8:
                        cols(s, C_SK, 256)
                    elif n == 9:
                        cols(s, C_SV, 256)
                    elif n == 10:
                        sp.dma_start(s3(s, 2, 576), w_uq[l]).then_inc(w_loaded[s], 16)
                    elif n == 11:
                        sp.dma_start(s3(s, 1, 768), w_ukv[l]).then_inc(w_loaded[s], 16)
                    elif n < W_OUT0:
                        w1 = a["nsa_cmp_w1_k" if n == 12 else "nsa_cmp_w1_v"][l].rearrange("(c q d) j -> q d c j", q=2, d=HD)
                        for q in range(2):
                            sp.dma_start(s3(s, 16, P)[q * HD:(q + 1) * HD], w1[q]).then_inc(w_loaded[s], 16)
                    else:
                        sp.dma_start(s3(s, KC, 256), w_out[l][:, :, (n - W_OUT0) * 256:(n - W_OUT0 + 1) * 256]
                                     ).then_inc(w_loaded[s], 16)

            with sp.Fori(0, DEPTH) as l:
                ffn(l, 0)
                mix_loads(l)
                ffn(l, 1)

            L = DEPTH
            sp.wait_ge(x_final, KC * (3 * DEPTH + 1))
            sp.dma_start(ws_n, a["gm_w_spatial_2"][0].rearrange("g t s -> t g s")).then_inc(ws_loaded, 16)
            sp.dma_start(gv, a["gm_v_norm_g_2"][0].partition_broadcast(P)).then_inc(ws_loaded, 16)
            for n, (name, c0) in enumerate(SECOND):
                s = n % 3
                if n < 3:
                    sp.wait_ge(w_split[s], slices_at(L, 0, 0))
                else:
                    sp.wait_ge(acc_full, full_at(L, 0, full2(LAST2[n - 3] + 1)))
                if name == "q":
                    for c in range(2):
                        for g in range(2):
                            h = c0 // 128 + c + 4 * g
                            sp.dma_start(s3(s, KC, 256)[:, :, 128 * c + 64 * g:128 * c + 64 * g + 64],
                                         w_in2[:, :, 1024 + HD * h:1024 + HD * h + HD]).then_inc(w_loaded[s], 16)
                elif name in ("pa", "pb"):
                    sp.dma_start(s3(s, 4, 512), (w_pa if name == "pa" else w_pb)[:, :, c0:c0 + 512]
                                 ).then_inc(w_loaded[s], 16)
                elif name == "wo":
                    sp.dma_start(s3(s, KC, 256), w_out2[:, :, c0:c0 + 256]).then_inc(w_loaded[s], 16)
                else:
                    first = {"u": 0, "v": 512, "kv": 1536, "gate": 1792}[name]
                    sp.dma_start(s3(s, KC, 256), w_in2[:, :, first + c0:first + c0 + 256]
                                 ).then_inc(w_loaded[s], 16)
                if n == 6:
                    sp.wait_ge(relrow_ready, 1)
                    sp.dma_start(rel_dram, rrow.unsqueeze(1).broadcast_to([8, P, 384])).then_inc(rel_stored, 16)
                    sp.wait_ge(rel_stored, 16)
                    sp.dma_start(bias_t, bass.AP(rel_dram.tensor, 127, [[383, P], [384 * P, 8], [1, 256]])
                                 ).then_inc(bias_loaded, 16)
            sp.wait_ge(acc_full, full_at(L, 0, full2(T2["wo", KC - 1] + 1)))

            def x_weights(e, n, q):
                sp.wait_ge(xgu_full, n + 1)
                sp.dma_start(xg_w[q], x_gate[e]).then_inc(xgate_loaded[q], 16)
                sp.dma_start(xu_w[q], x_up[e]).then_inc(xup_loaded[q], 16)

            def x_rest(e, n, q):
                sp.wait_ge(xdown_full, n + 1)
                for t in range(2):
                    sp.dma_start(xd_w[q][t], x_down[e][:, 2 * t:2 * t + 2, :]).then_inc(xdown_loaded[q], 16)
                sp.wait_ge(place_ready, n + 1)
                sp.dma_start(rows[q],
                             rows_dram[bass.ds(e, 1)][0].partition_broadcast(P)).then_inc(rows_loaded[q], 16)

            x_weights(0, 0, 0)
            for q in range(2):
                n = T2["combt" if q == 0 else "rankt", 0]
                sp.wait_ge(acc_free[n % 2], free_at(L, 0, n + 2))
            sp.dma_start(rows_dram, rows_T).then_inc(rows_stored, 16)
            sp.wait_ge(rows_stored, 16)
            sp.wait_ge(htok_ready, 2 * TB)
            sp.wait_ge(passes_ready, 1)
            n_p = sp.value_load(n_passes[0:1, 0:1], min_val=1, max_val=TB)
            x_rest(0, 0, 0)
            x_weights(1, 1, 1)
            x_rest(1, 1, 1)
            with sp.Fori(2, NX // 2 + 1) as i:
                for q in range(2):
                    x_weights(i * 2 + (q - 2), i * 2 + (q - 2), q)
                    x_rest(i * 2 + (q - 2), i * 2 + (q - 2), q)
            with sp.If(n_p > 1):
                with sp.Fori(1, n_p) as ps_:
                    with sp.Fori(1, NX // 2 + 1) as i:
                        n = sp.snap(ps_ * NX + i * 2)
                        for q in range(2):
                            x_weights(i * 2 + (q - 2), n + (q - 2), q)
                            x_rest(i * 2 + (q - 2), n + (q - 2), q)

            for b in range(TB):
                sp.wait_ge(y_ready, 2 * b + 2)
                sp.dma_start(y_tok[:, b, :], y_out[:, b, :]).then_inc(y_stored, 16)
            sp.wait_ge(y_stored, 16 * TB)

        N_PARAMS = 16 * (3 * DEPTH + 4 + 2 * DEPTH + 11)
        L = DEPTH
        OUT_HEADS = [("mla", h) for h in range(6)] + [("nsa", h) for h in range(6)]
        ROPES = ([(q6[0:96, h, :], "mla", ("uq", h)) for h in range(6)]
                 + [(lora[0:96, 3, :], "mla", ("kr", 0))]
                 + [(nq[:, c, :], "nsa", ("nq", c)) for c in range(3)]
                 + [(nk[:, i, :], "nsa", (n, 0)) for i, n in enumerate(("kc", "ks", "kw"))])
        EVAC = {("cq", 0): (lora[:, 0, :], 1.0), ("cq", 1): (lora[:, 1, :], 1.0), ("ckv", 0): (lora[:, 2, :], 1.0),
                ("kr", 0): (lora[0:96, 3, :], 1.0), ("kc", 0): (nk[:, 0, :], 1.0), ("ks", 0): (nk[:, 1, :], 1.0),
                ("kw", 0): (nk[:, 2, :], 1.0), ("vc", 0): (nk[:, 3, :], 1.0)}
        for i in range(3):
            EVAC["nq", i] = (nq[:, i, :], HD ** -0.5)
        for i in range(2):
            EVAC["sq", i] = (sq_T[:, i, :], HD ** -0.5)
            EVAC["sk", i] = (sk_T[:, i, :], 1.0)
            EVAC["sv", i] = (sv[:, 2 * i:2 * i + 2, :].rearrange("p a b -> p (a b)"), 1.0)
            EVAC["vsw", i] = (vsw[:, 4 * i:4 * i + 4, :].rearrange("p a b -> p (a b)"), 1.0)
            EVAC["xs_k", i] = (pairs[0][:, i, :], 1.0)
            EVAC["xs_v", i] = (pairs[1][:, i, :], 1.0)
        for i in range(6):
            EVAC["uq", i] = (q6[0:96, i, :], 96.0 ** -0.5)
            EVAC["kn", i] = (k6[0:HD, i, :], 1.0)
        for i in range(TB):
            EVAC["mv", i] = (mv[:, i, :], 1.0)

        def taken(eng, l, base, n):
            eng.wait_ge(acc_free[n % 2], free_at(l, base, n + 2))

        def unit_info(n):
            kind, h, i, br, first, last = UNITS[n]
            blk = slice(i * P, (i + 1) * P)
            w = (i + 1) * P
            if kind == "mla":
                q, k = q6[0:96, h, blk], k6[0:96, h, 0:w]
                v = [mv[:, j, h * HD:(h + 1) * HD] for j in range(i + 1)]
            else:
                g, c = NSA_HALF(h)
                r = slice(g * HD, (g + 1) * HD)
                q = nq[r, c, blk]
                if br == "cmp":
                    w = 31
                    k, v = kcmp_T[r, :], [vcmp[:, g, :]]
                else:
                    k = nk[r, 1 if br == "sel" else 2, 0:w]
                    vt = vs if br == "sel" else vw
                    v = [vt[:, j, g * HD:(g + 1) * HD] for j in range(i + 1)]
            return dict(q=q, k=k, v=v, w=w, i=i, h=h, br=br, first=first, last=last,
                        out=slice((h % 2) * HD, (h % 2) * HD + HD), blk=blk,
                        head=(0 if kind == "mla" else 6) + h,
                        end=last and i == TB - 1, begin=first and i == 0)

        def swa_info(n):
            h, i = SWA_UNITS[n]
            g, c = h // 4, h % 4
            lo = max(0, i - 1)
            r = slice(g * HD, (g + 1) * HD)
            return dict(q=q2[r, c, i * P:(i + 1) * P], k=k2[r, lo * P:(i + 1) * P],
                        v=[v2[:, j, g * HD:(g + 1) * HD] for j in range(lo, i + 1)],
                        w=(i + 1 - lo) * P, i=i, h=h, first=True, last=True, br="swa",
                        out=slice((h % 2) * HD, (h % 2) * HD + HD), blk=slice(i * P, (i + 1) * P),
                        head=h, end=i == TB - 1, begin=i == 0)

        NSW = len(SWA_UNITS)
        U2 = DEPTH * NU

        @block.tensor
        def _(pe):
            mm = nc.tensor.matmul

            def acc_wait(l, base, n):
                pe.wait_ge(acc_free[n % 2], free_at(l, base, n))
                return acc[n % 2]

            def slot_wait(s, l, n_dmas):
                pe.wait_ge(w_loaded[s], at(l, 16 * SLOT_DMAS[s], 16 * n_dmas))

            def norm(k):
                pe.wait_ge(summed, k + 1)
                mm(turn[0][:, :], cst("ones"), h_T[:, 0, :], start=True, stop=False)
                pe.wait_ge(squared, k * KC + KC)
                mm(turn[0][:, :], cst("ones"), h_T[:, KC - 1, :], start=False, stop=True).then_inc(ssq_full, 1)

            def slices(l, ph):
                base, gub = (B1, B2)[ph], ph * 2 * NSL

                def half(sl, w):
                    pe.wait_ge(w_split[w], slices_at(l, ph, sl + 1))
                    if w == 0:
                        pe.wait_ge(gate_taken, slices_at(l, ph, sl))
                    else:
                        pe.wait_ge(hid_done, at(l, TG, gub + sl * 2 + 2))
                    first = isinstance(sl, int) and sl + w == 0
                    hi, lo = [t[:, :].rearrange("p (c n) -> p c n", n=FS) for t in (w_hi[w], w_lo[w])]

                    def chunk(c, kc):
                        cols = slice(c * P, (c + 1) * P)
                        ps = score[2 * w + c][:, :]
                        mm(ps, hi[:, kc, cols], h_hi[:, kc, :], start=kc == 0, stop=False, skip_group_check=True)
                        mm(ps, hi[:, kc, cols], h_lo[:, kc, :], start=False, stop=False, skip_group_check=True)
                        return mm(ps, lo[:, kc, cols], h_hi[:, kc, :], start=False, stop=kc == KC - 1,
                                  skip_group_check=True)

                    if first:
                        for kc in range(KC):
                            pe.wait_ge(h_split, at(l, 3 * KC, 2 * ph * KC + kc + 1))
                            for c in range(2):
                                m = chunk(c, kc)
                    else:
                        for c in range(2):
                            for kc in range(KC):
                                m = chunk(c, kc)
                    m.then_inc(gu_full, 1)

                def up(sl, par):
                    half(sl, 0)
                    half(sl, 1)

                def down(sl, par, last):
                    pe.wait_ge(w_split[2], slices_at(l, ph, sl + 1))
                    pe.wait_ge(hid_done, at(l, TG, gub + sl * 2 + 4))
                    tile = 0 if last else 2
                    hi, lo = [t[:, :].rearrange("p (c n) -> p c n", n=D) for t in (w_hi[tile], w_lo[tile])]
                    for c in range(KC):
                        pe.wait_ge(acc_free[c % 2], at(l, TL // 2, base // 2 + sl * (KC // 2) + c // 2 + 1))
                        cols = slice(c * P, (c + 1) * P)
                        for j in range(2):
                            mm(acc[c % 2][:, :], hi[:, j, cols], hid_hi[:, 2 * par + j, :], start=j == 0, stop=False)
                            mm(acc[c % 2][:, :], hi[:, j, cols], hid_lo[:, 2 * par + j, :], start=False, stop=False)
                            m = mm(acc[c % 2][:, :], lo[:, j, cols], hid_hi[:, 2 * par + j, :],
                                   start=False, stop=j == 1)
                        m.then_inc(acc_full, 1)

                run_slices(pe, NSL, up, down)

            def linear(ps, s, width, col, m_cols, rhs, n_k, ready=None, chunk_ready=h_ready):
                for kc in range(n_k):
                    if ready is not None:
                        pe.wait_ge(chunk_ready, ready + kc + 1)
                    m = mm(ps[0:m_cols, :], s3(s, n_k, width)[:, kc, col:col + m_cols], rhs[:, kc, :],
                           start=kc == 0, stop=kc == n_k - 1)
                return m

            def parts(first, last, ps, w_sl, h_sl, n, tokens=False):
                for j, (x, y) in enumerate(((0, 0), (0, 1), (1, 0))):
                    w, h = mix_w[n % 2][x][:, w_sl], mix_h[y][:, h_sl[0], h_sl[1]]
                    m = mm(ps, *((h, w) if tokens else (w, h)), start=first and j == 0, stop=last and j == 2)
                return m

            def linear_split(ps, n, width, col, m_cols, ready=None):
                for kc in range(KC):
                    if ready is not None:
                        pe.wait_ge(h_split, ready + kc + 1)
                    m = parts(kc == 0, kc == KC - 1, ps[0:m_cols, :],
                              slice(kc * width + col, kc * width + col + m_cols), (kc, slice(0, S)), n)
                return m

            def by_token_split(ps, ld, width, col, n, blocks):
                for j, b in enumerate(blocks):
                    for kc in range(KC):
                        m = parts(kc == 0, kc == KC - 1, ps[:, j * n:(j + 1) * n],
                                  slice(kc * width + col, kc * width + col + n),
                                  (kc, slice(b * P, (b + 1) * P)), ld, tokens=True)
                return m

            def by_token(ps, s, width, col, n, blocks, n_k=KC, src=h_T):
                for j, b in enumerate(blocks):
                    for kc in range(n_k):
                        m = mm(ps[:, j * n:(j + 1) * n], src[:, kc, b * P:(b + 1) * P],
                               s3(s, n_k, width)[:, kc, col:col + n], start=kc == 0, stop=kc == n_k - 1)
                return m

            def attend(l, per, u0, n_units, info, s_done, fr, fbase, head0):
                def scores(n):
                    u = info(n)
                    if n >= 4:
                        pe.wait_ge(s_done, at(l, per, u0 + n - 3))
                    mm(score[n % 4][:, 0:u["w"]], u["q"], u["k"], start=True, stop=True).then_inc(s_full, 1)

                def turns(n):
                    u = info(n)
                    pe.wait_ge(p_ready, at(l, per, u0 + n + 1))
                    if n >= 2:
                        pe.wait_ge(pt_ready, at(l, per, u0 + n - 1))
                    w = min(u["w"], P)
                    for j in range(len(u["v"])):
                        m = nc.tensor.transpose(turn[n % 2][0:w, j * P:(j + 1) * P],
                                                probs[:, n % 3, j * P:j * P + w], ident)
                    m.then_inc(t_full, 1)

                def values(n):
                    u = info(n)
                    w = min(u["w"], P)
                    t = head0 + u["head"]
                    if u["begin"]:
                        acc_wait(fr, fbase, t)
                    pe.wait_ge(pt_ready, at(l, per, u0 + n + 1))
                    for j, v in enumerate(u["v"]):
                        m = mm(acc[t % 2][u["out"], u["blk"]], v[0:w, :], probs_T[0:w, n % 2, j * P:(j + 1) * P],
                               start=u["first"] and j == 0, stop=u["last"] and j == len(u["v"]) - 1,
                               skip_group_check=True)
                    m.then_inc(pv_done, 1)

                AHEAD = 3
                for n in range(min(AHEAD, n_units)):
                    scores(n)
                for n in range(n_units + 1):
                    if n + AHEAD < n_units:
                        scores(n + AHEAD)
                    if n < n_units:
                        turns(n)
                    if n >= 1:
                        values(n - 1)

            def mix(l):
                def compress(kv, r, spread):
                    name, ld = (("xs_k", 12), ("xs_v", 13))[kv]
                    if r == spread[0]:
                        slot_wait(ld % 3, l, NSL + sum(MIX_DMAS[ld % 3:ld + 1:3]))
                        pe.wait_ge(small_loaded, at(l, 64, 64))
                        for g in range(2):
                            taken(pe, l, BM, TICKET[name, g])
                    w1, per = s3(ld % 3, 16, P), -(-32 // (spread[1] - spread[0]))
                    for j in range(per * (r - spread[0]), min(32, per * (r - spread[0] + 1))):
                        c = j % 16
                        if j < 16:
                            mm(turn[kv][:, 0:62].rearrange("p (g w) -> p g w", g=2), w1[:, c, :],
                               pairs[kv][:, :, 2 * c:2 * c + 481:16], start=c == 0, stop=c == 15)
                        else:
                            m = mm(turn[kv][:, 62:63], w1[:, c, :], cmp_pos[:, kv, c:c + 1],
                                   start=c == 0, stop=c == 15)
                    if r == spread[1] - 1:
                        m.then_inc(hidc_full, 1)

                n_rope = 0
                for n, (name, i, ld, who) in enumerate(MIX):
                    if ld is not None and ld < N_SPLIT:
                        pe.wait_ge(mix_w_split, at(l, N_SPLIT, ld + 1))
                    elif ld is not None:
                        s = ld % 3
                        slot_wait(s, l, NSL + sum(MIX_DMAS[s:ld + 1:3]))
                    if (name, i) == ("kc", 0):
                        pe.wait_ge(lsq_ready, l + 1)
                        for j in range(2):
                            mm(turn[0][:, :], cst("ones"), probs[:, j, :], start=j == 0, stop=j == 1)
                        mm(turn[1][:, :], cst("ones"), probs[:, 2, :], start=True, stop=True).then_inc(lssq_full, 1)
                    if name == "uq" and i == 0:
                        pe.wait_ge(lora_ready, l + 1)
                    if name == "rope":
                        taken(pe, l, BM, TICKET[ROPES[i][2]])
                    if name == "xs_k":
                        pe.wait_ge(rope_ready, at(l, len(ROPES), 1))
                    if name == "xs_v":
                        taken(pe, l, BM, TICKET["vc", 0])
                    if name == "cmp":
                        pe.wait_ge(rope_ready, at(l, N_ROPE, N_ROPE))
                        pe.wait_ge(hidc_ready, at(l, 2, 2))
                    ps = acc_wait(l, BM, n)
                    if name in ("cq", "sq", "sk") or (name == "nq" and i < 2):
                        m = linear_split(ps, ld, 256, 128 * i, 128, at(l, 3 * KC, KC) if n == 0 else None)
                    elif name == "nq" or name in ("ckv", "vc"):
                        m = linear_split(ps, ld, 160 if name == "ckv" else 256, 0, 128)
                    elif name == "kr":
                        m = linear_split(ps, ld, 160, 64, 96)
                    elif name in ("kc", "ks"):
                        m = linear_split(ps, ld, 256, 128, 128)
                    elif name == "kw":
                        m = linear_split(ps, ld, 146, 0, 128)
                    elif name == "vsw":
                        m = by_token_split(ps, ld, 256, 0, 256, (2 * i, 2 * i + 1))
                    elif name == "gate":
                        m = by_token_split(ps, ld, 146, P, 18, range(TB))
                    elif name == "sv":
                        m = by_token_split(ps, ld, 256, 0, 256, (2 * i, 2 * i + 1))
                    elif name == "uq":
                        m = linear(ps, s, 576, 96 * i, 96, lora, 2)
                    elif name == "kn":
                        m = mm(ps[0:HD, :], s3(s, 1, 768)[:, 0, 128 * i:128 * i + HD], lora[:, 2, :],
                               start=True, stop=True)
                    elif name == "mv":
                        wv = slot[s][:, 0:768].rearrange("p (h t d) -> p h t d", t=2, d=HD)[:, :, 1, :]
                        m = mm(ps[:, 0:384], lora[:, 2, i * P:(i + 1) * P], wv, start=True, stop=True)
                    elif name == "rope":
                        t, kind, _ = ROPES[i]
                        r = 96 if kind == "mla" else P
                        m = mm(ps[0:r, :], cst("r_" + kind, rows=r), t, start=True, stop=True)
                    elif name in ("xs_k", "xs_v"):
                        src = nk[:, 0 if name == "xs_k" else 3, :]
                        pick = cst("ident", lo=i * HD, hi=(i + 1) * HD)
                        mm(ps[0:HD, :], pick, src, start=True, stop=True)
                        mm(ps[HD:P, 0:S - 1], pick, src[:, 1:S], start=True, stop=True)
                        m = mm(ps[HD:P, S - 1:S], pick, src[:, 0:1], start=True, stop=True)
                    elif name == "cmp":
                        for g in range(2):
                            mm(ps[g * HD:(g + 1) * HD, 0:31], cmp_w2[:, 0, :], hid_cmp[:, 0, g * 31:g * 31 + 31],
                               start=True, stop=True)
                        for g in range(2):
                            m = mm(ps[0:31, 64 + g * HD:128 + g * HD], hid_cmp[:, 1, g * 31:g * 31 + 31],
                                   cmp_w2[:, 1, :], start=True, stop=True)
                    m.then_inc(acc_full, 1)
                    if name == "rope":
                        if V_ROPES[0] <= n_rope < V_ROPES[1]:
                            compress(1, n_rope, V_ROPES)
                        if K_ROPES[0] <= n_rope < K_ROPES[1]:
                            compress(0, n_rope, K_ROPES)
                        n_rope += 1
                taken(pe, l, BM, TICKET["cmp", 0])
                attend(l, NU, 0, NU, unit_info, exp_ready, l, BM, T_LIN)
                pe.wait_ge(exp_ready, at(l, NU, NU))
                def remaining(h):
                    r, c = slice((h % 2) * HD, (h % 2) * HD + HD), h // 2
                    if h >= 2:
                        pe.wait_ge(a_exp, at(l, SB_HEADS, h - 1))
                    for j in range(TB):
                        b, o = SB_PLACE[j]
                        m = mm(sb_bank[h % 2][b][:, o:o + S - j * P], sk_T[r, c, j * P:(j + 1) * P],
                               sq_T[r, c, j * P:S], start=j != 3, stop=True, skip_group_check=True)
                    m.then_inc(z_full, 1)

                def suffixes(h):
                    pe.wait_ge(sp_ready, at(l, SB_HEADS, h + 1))
                    for j in range(TB):
                        b, o = SB_PLACE[j]
                        ps = sb_bank[h % 2][b]
                        m = mm(ps[:, o:o + S - j * P], cst("negtri"), sb_cols(hid, j, 0, S - j * P),
                               start=False, stop=j == TB - 1, skip_group_check=True)
                        for jj in range(j + 1, TB):
                            m = mm(ps[:, o + (jj - j) * P:o + S - j * P], cst("negones"),
                                   sb_cols(hid, jj, 0, S - jj * P),
                                   start=False, stop=jj == TB - 1, skip_group_check=True)
                    m.then_inc(suffix_full, 1)

                def sb_values(h):
                    r = slice((h % 2) * HD, (h % 2) * HD + HD)
                    ps = acc_wait(l, BM, T_LIN + NHD + h)
                    pe.wait_ge(a_ready, at(l, SB_HEADS, h + 1))
                    for j in range(TB):
                        m = mm(ps[r, j * P:S], sv[:, j, h * HD:(h + 1) * HD], sb_cols(sb_a[h % 2], j, 0, S - j * P),
                               start=j == 0, stop=j == TB - 1, skip_group_check=True)
                    m.then_inc(acc_full, 1)

                remaining(0)
                for h in range(SB_HEADS):
                    if h + 1 < SB_HEADS:
                        remaining(h + 1)
                    suffixes(h)
                    if h >= 1:
                        sb_values(h - 1)
                sb_values(SB_HEADS - 1)
                taken(pe, l, BM, T_LIN + NHD + SB_HEADS - 2)
                taken(pe, l, BM, T_LIN + NHD + SB_HEADS - 1)
                for c in range(KC):
                    ld = W_OUT0 + c // 2
                    slot_wait(ld % 3, l, NSL + sum(MIX_DMAS[ld % 3:ld + 1:3]))
                    ps = acc_wait(l, BM, T_HEAD + c)
                    linear(ps, ld % 3, 256, (c % 2) * P, P, o_T, KC).then_inc(acc_full, 1)

            pe.sem_inc(acc_free[0], 1)
            pe.sem_inc(acc_free[1], 1)
            pe.sem_inc(acc_full, 1)
            pe.sem_inc(gu_full, 1)
            pe.sem_inc(gate_taken, 1)
            for s in range(3):
                pe.sem_inc(w_split[s], 1)
            pe.sem_inc(hid_done, 2)
            pe.sem_inc(mine_ready, 1)
            pe.sem_inc(xgu_full, 2)
            pe.sem_inc(xdown_full, 2)
            pe.sem_inc(place_ready, 2)
            pe.sem_inc(scatter_taken, 2)
            pe.wait_ge(x_loaded, 32)
            for c in range(KC):
                if c >= 2:
                    pe.wait_ge(x_final, c - 1)
                for b in range(TB):
                    m = nc.tensor.transpose(turn[c % 2][:, b * P:(b + 1) * P], x_in[:, b, c * P:(c + 1) * P], ident)
                m.then_inc(xt_full, 1)
            pe.wait_ge(x_final, KC)
            with pe.Fori(0, DEPTH) as l:
                norm(l * 3)
                slices(l, 0)
                norm(l * 3 + 1)
                mix(l)
                norm(l * 3 + 2)
                slices(l, 1)

            pe.wait_ge(params_loaded, N_PARAMS)
            norm(3 * L)
            norm(3 * L + 1)
            pe.wait_ge(h_ready, KC * (3 * L + 1) + 1)
            mm(turn[0][0:8, 0:384], rel[:, :], cst("bucket_rows", rows=32), start=True, stop=True
               ).then_inc(rel_full, 1)
            for n, (name, i, ld) in enumerate(SEC_T):
                if ld is not None:
                    s = ld % 3
                    slot_wait(s, L, sum(SEC_DMAS[s:ld + 1:3]))
                if (name, i) == ("wst", 0):
                    pe.wait_ge(ws_loaded, 32)
                if (name, i) == ("sv", 0):
                    pe.wait_ge(vn_ready, 1)
                    taken(pe, L, 0, T2["wst", 0])
                    taken(pe, L, 0, T2["wst", 1])
                if name == "swa":
                    if i == 0:
                        taken(pe, L, 0, T2["sv", 3])
                        taken(pe, L, 0, T2["k", 0])
                        attend(L, NU, 0, NSW, swa_info, max_ready, L, 0, SWA0)
                    continue
                if (name, i) == ("pa", 0):
                    taken(pe, L, 0, T2["swa", 6])
                    taken(pe, L, 0, T2["swa", 7])
                if name == "route":
                    norm(3 * L + 2)
                    pe.wait_ge(h_ready, KC * (3 * L + 3))
                if name == "rank":
                    for j in range(2 * TB):
                        b, hf = j // 2, j % 2
                        if j >= 2:
                            pe.wait_ge(htok_ready, j - 1)
                        for c in range(4):
                            m = nc.tensor.transpose(turn[j % 2][:, c * P:(c + 1) * P],
                                                    h_T[:, 4 * hf + c, b * P:(b + 1) * P], ident)
                        m.then_inc(htok_full, 1)
                    pe.wait_ge(member_ready, 1)
                if name == "combt":
                    pe.wait_ge(comb_done, 1)
                if name == "rankt":
                    pe.wait_ge(rank_ready, 1)
                ps = acc_wait(L, 0, n)
                if name in ("u", "q", "gate"):
                    m = linear(ps, s, 256, (i % 2) * P, P, h_T, KC, KC * (3 * L + 1) if n == 0 else None)
                elif name == "v":
                    m = by_token(ps, s, 256, 0, 256, (2 * (i % 2), 2 * (i % 2) + 1))
                elif name == "k":
                    m = linear(ps, s, 256, 0, P, h_T, KC)
                elif name == "vtok":
                    m = by_token(ps, s, 256, P, P, range(TB))
                elif name == "wst":
                    for g in range(4):
                        m = nc.tensor.transpose(ps[:, g * P:(g + 1) * P], ws_n[:, 4 * i + g, :], ident)
                elif name == "sv":
                    for b in range(TB):
                        for g in range(2):
                            mm(ps[g * HD:(g + 1) * HD, b * P:(b + 1) * P],
                               vtok[:, b, (2 * i + g) * HD:(2 * i + g + 1) * HD], ws_T[:, 2 * i + g, :],
                               start=True, stop=False, skip_group_check=True)
                        m = mm(ps[:, b * P:(b + 1) * P], cst("group_rows", 8, i * P, (i + 1) * P), bs[:, :],
                               start=False, stop=True, skip_group_check=True)
                elif name in ("pa", "pb"):
                    m = linear(ps, s, 512, (i % 4) * P, P, ab_T if name == "pa" else ab_T[:, 4:8, :], 4)
                elif name == "wo":
                    m = linear(ps, s, 256, (i % 2) * P, P, sig_a, KC, 0 if i == 0 else None, merged_ready)
                elif name == "route":
                    for b in range(TB):
                        for kc in range(KC):
                            m = mm(ps[:, b * 20:(b + 1) * 20], h_T[:, kc, b * P:(b + 1) * P], rw[:, kc, :],
                                   start=kc == 0, stop=kc == KC - 1)
                elif name == "rank":
                    for b in range(TB):
                        for j in range(b + 1):
                            mm(ps[:, b * 16:(b + 1) * 16], cst("strict" if j == b else "ones"), member[:, j, :],
                               start=j == 0, stop=j == b)
                    for b in range(TB):
                        m = mm(ps[:, 64:80], cst("ones"), member[:, b, :], start=b == 0, stop=b == TB - 1)
                elif name in ("combt", "rankt"):
                    for b in range(TB):
                        m = nc.tensor.transpose(ps[0:16, b * P:(b + 1) * P],
                                                (comb if name == "combt" else rank)[:, b, :], ident)
                m.then_inc(acc_full, 1)

            def gather(pair, q):
                pe.wait_ge(pick_ready, pair * 2 + q + 1)
                pe.wait_ge(mine_ready, pair * 2 + q + 1)
                for c in range(KC):
                    for b in range(TB):
                        m = mm(turn[c // 4][:, (c % 4) * P:(c % 4 + 1) * P], h_tok[:, b, c * P:(c + 1) * P],
                               pick[q][:, b, :], start=b == 0, stop=b == TB - 1)
                m.then_inc(gathered, 1)

            def gate_up(pair, q):
                pe.wait_ge(mine_ready, pair * 2 + q + 2)
                for w, (wt, sem_) in enumerate(((xg_w, xgate_loaded), (xu_w, xup_loaded))):
                    pe.wait_ge(sem_[q], pair * 16 + 16)
                    for c in range(KC):
                        m = mm(score[w][:, :], mine_T[q][:, c, :], wt[q][:, c, :], start=c == 0, stop=c == KC - 1)
                m.then_inc(xgu_full, 1)

            def turn_hidden(pair, q):
                pe.wait_ge(xhid_ready, pair * 2 + q + 1)
                for c in range(4):
                    m = nc.tensor.transpose(score[0][:, c * P:(c + 1) * P], xhid[:, c * P:(c + 1) * P], ident)
                m.then_inc(xhid_turned, 1)

            def down_x(pair, q):
                pe.wait_ge(xhidt_ready, pair * 2 + q + 1)
                pe.wait_ge(xdown_loaded[q], pair * 32 + 32)
                for hf in range(2):
                    for c in range(4):
                        m = mm(score[2 + hf][:, :], xhid_T[:, c * P:(c + 1) * P],
                               xd_w[q][c // 2][:, c % 2, hf * S:(hf + 1) * S], start=c == 0, stop=c == 3)
                m.then_inc(xdown_full, 1)

            def scatter(pair, q):
                pe.wait_ge(yslot_ready, pair * 2 + q + 1)
                pe.wait_ge(place_ready, pair * 2 + q + 3)
                for c in range(KC):
                    pe.wait_ge(scatter_taken, pair * 16 + 8 * q + c + 1)
                    mm(acc[c % 2][:, :], y_slot[:, c // 4, (c % 4) * P:(c % 4 + 1) * P], place[q],
                       start=True, stop=True).then_inc(scattered, 1)

            def step(pair, q, first=False, last=False):
                gate_up(pair, q)
                if not last:
                    gather(pair + q, 1 - q)
                turn_hidden(pair, q)
                if not first:
                    scatter(pair - 1 + q, 1 - q)
                down_x(pair, q)

            acc_wait(L, 0, NT2)
            acc_wait(L, 0, NT2 + 1)
            pe.wait_ge(htok_ready, 2 * TB)
            pe.wait_ge(passes_ready, 1)
            n_p = pe.value_load(n_passes[0:1, 0:1], min_val=1, max_val=TB)
            with pe.Fori(0, n_p) as ps_:
                pair0 = pe.snap(ps_ * (NX // 2))
                gather(pair0, 0)
                step(pair0, 0, first=True)
                with pe.Fori(0, NX // 2 - 1) as i:
                    pair = pe.snap(pair0 + i)
                    step(pair, 1)
                    step(pair + 1, 0)
                step(pair0 + (NX // 2 - 1), 1, last=True)
                scatter(pair0 + (NX // 2 - 1), 1)
            norm(3 * L + 3)
            pe.wait_ge(h_ready, KC * (3 * L + 4))
            for n in range(2 * TB):
                if n >= 2:
                    pe.wait_ge(y_ready, n - 1)
                for c in range(4):
                    m = nc.tensor.transpose(turn[n % 2][:, c * P:(c + 1) * P],
                                            h_T[:, 4 * (n % 2) + c, (n // 2) * P:(n // 2 + 1) * P], ident)
                m.then_inc(yt_full, 1)

        @block.scalar
        def _(act):
            fn = nc.scalar.activation

            def split_weights(l, ph, w, sl, tile=None):
                tile = w if tile is None else tile
                dmas = ph * (NSL + sum(MIX_DMAS[w::3]))
                act.wait_ge(w_loaded[w], at(l, 16 * SLOT_DMAS[w], 16 * dmas + sl * 16 + 16))
                fn(w_hi[tile][:, :], slot[w][:, :], ACT.Copy).then_inc(w_hi_ready[w], 1)

            def split_mix(l, n):
                dmas = NSL + sum(MIX_DMAS[n % 3:n + 1:3])
                act.wait_ge(w_loaded[n % 3], at(l, 16 * SLOT_DMAS[n % 3], 16 * dmas))
                if n >= 2:
                    act.wait_ge(acc_full, mix_full(l, LAST_TICKET[n - 2] + 1))
                w = LOAD_COLS[n]
                fn(mix_w[n % 2][0][:, 0:w], slot[n % 3][:, 0:w], ACT.Copy).then_inc(mix_w_hi_ready, 1)

            def norm(k, split=None, mix=None):
                for c in range(KC):
                    act.wait_ge(x_final, k * KC + c + 1)
                    fn(h_T[:, c, :], x_T[:, c, :], ACT.Square).then_inc(squared, 1)
                if split:
                    split_weights(*split, 0, 0)
                if mix is not None:
                    split_mix(mix, 0)
                act.wait_ge(ssq_full, k + 1)
                fn(rstd[:, :], turn[0][:, :], ACT.Ln, scale=1.0 / D, bias=eps[:, :])
                act.drain()
                fn(rstd[:, :], rstd[:, :], ACT.Exp, scale=-0.5).then_inc(rstd_ready, 1)
                if split:
                    for c in range(KC):
                        act.wait_ge(h_ready, k * KC + c + 1)
                        fn(h_hi[:, c, :], h_T[:, c, :], ACT.Copy).then_inc(h_hi_ready, 1)
                if mix is not None:
                    for c in range(KC):
                        act.wait_ge(h_ready, k * KC + c + 1)
                        fn(mix_h[0][:, c, :], h_T[:, c, :], ACT.Copy).then_inc(h_hi_ready, 1)
                    split_mix(mix, 1)

            def slices(l, ph):
                gub, fb = ph * 2 * NSL, (F1, F2)[ph]

                def step(sl):
                    later = not isinstance(sl, int) or sl >= 1
                    if later:
                        split_weights(l, ph, 0, sl)
                        act.wait_ge(gu_full, gu_at(l, gub, sl * 2))
                    split_weights(l, ph, 1, sl)
                    if later:
                        if not isinstance(sl, int) or sl >= 2:
                            act.wait_ge(acc_full, full_at(l, fb, (sl - 1) * KC))
                        split_weights(l, ph, 2, sl - 1)
                    act.wait_ge(hid_done, at(l, TG, gub + sl * 2 + 2))
                    act.wait_ge(gu_full, gu_at(l, gub, sl * 2 + 1))
                    for c in range(2):
                        fn(et[:, c, :], score[c][:, :], ACT.Exp, scale=-1.0).then_inc(sig_ready, 1)

                step(0)
                with act.Fori(0, (NSL - 1) // 2) as i:
                    step(i * 2 + 1)
                    step(i * 2 + 2)
                split_weights(l, ph, 2, NSL - 1, tile=0)

            def attend(l, per, u0, n_units, info, fr, fbase, head0, dest, sink):
                def exps(n):
                    u = info(n)
                    w, st = u["w"], n % 4
                    act.wait_ge(max_ready, at(l, per, u0 + n + 1))
                    if n >= 3 and not sink:
                        act.wait_ge(t_full, at(l, per, u0 + n - 2))
                    src = probs[:, n % 3, 0:w] if sink else score[st][:, 0:w]
                    m = fn(probs[:, n % 3, 0:w], src, ACT.Exp, bias=stats[:, 0, st:st + 1],
                           accum_out=stats[:, 1, st:st + 1])
                    if sink:
                        m = fn(stats[:, 3, st:st + 1], sinks[:, u["h"]:u["h"] + 1], ACT.Exp,
                               bias=stats[:, 0, st:st + 1])
                    m.then_inc(exp_ready, 1)

                def evac_turn(n):
                    u = info(n)
                    r, w = min(u["w"], P), len(u["v"]) * P
                    act.wait_ge(t_full, at(l, per, u0 + n + 1))
                    if n >= 2:
                        act.wait_ge(pv_done, at(l, per, u0 + n - 1))
                    fn(probs_T[0:r, n % 2, 0:w], turn[n % 2][0:r, 0:w], ACT.Copy).then_inc(pt_ready, 1)

                def head_out(n):
                    u = info(n)
                    if u["end"]:
                        t = head0 + u["head"]
                        act.wait_ge(pv_done, at(l, per, u0 + n + 1))
                        fn(dest[u["out"], u["head"] // 2, :], acc[t % 2][u["out"], :], ACT.Copy
                           ).then_inc(acc_free[t % 2], 1)

                exps(0)
                for n in range(n_units + 1):
                    if n + 1 < n_units:
                        exps(n + 1)
                    if n < n_units:
                        evac_turn(n)
                    if n >= 1:
                        head_out(n - 1)

            def mix(l):
                for n, (name, i, ld, who) in enumerate(MIX):
                    if name == "cmp":
                        for k in range(2):
                            act.wait_ge(gelu_pre, at(l, 2, k + 1))
                            fn(cmp_t[:, 2, :], cmp_t[:, 1, :], ACT.Exp, scale=-2 * GC).then_inc(gelu_exp, 1)
                    if who == "act":
                        act.wait_ge(acc_full, mix_full(l, n + 1))
                        if name == "cmp":
                            fn(kcmp_T[:, :], acc[n % 2][:, 0:31], ACT.Copy)
                            m = fn(vcmp.rearrange("p a b -> p (a b)"), acc[n % 2][0:31, 64:192], ACT.Copy)
                        else:
                            t, sc = EVAC[name, i]
                            m = fn(t, acc[n % 2][0:t.shape[0], 0:t.shape[1]], ACT.Copy, scale=sc)
                        m.then_inc(acc_free[n % 2], 1)
                    if ld is not None and ld + 2 < N_SPLIT and LAST_TICKET[ld] == n:
                        split_mix(l, ld + 2)
                    if (name, i) == ("ckv", 0):
                        act.drain()
                        fn(probs[:, :, :], lora[:, 0:3, :], ACT.Square).then_inc(lsq_ready, 1)
                    if (name, i) == ("ks", 0):
                        act.wait_ge(lssq_full, l + 1)
                        fn(et[:, 0, :], turn[0][:, :], ACT.Ln, scale=1.0 / 256, bias=eps[:, :])
                        fn(et[:, 1, :], turn[1][:, :], ACT.Ln, scale=1.0 / 128, bias=eps[:, :])
                        act.drain()
                        fn(et[:, :, :], et[:, :, :], ACT.Exp, scale=-0.5).then_inc(lrstd_ready, 1)
                    if name == "gate":
                        taken(act, l, BM, n)
                        fn(gates_e[:, :, :], gates[:, :, :], ACT.Exp, scale=-1.0).then_inc(gate_exp, 1)
                attend(l, NU, 0, NU, unit_info, l, BM, T_LIN, o_T, False)
                def logs(h):
                    act.drain()
                    act.wait_ge(z_full, at(l, SB_HEADS, h + 1))
                    if h >= 1:
                        act.wait_ge(sp_ready, at(l, SB_HEADS, h))
                    for b, n in SB_BANKS:
                        fn(sb_e[:, b, 0:n], sb_bank[h % 2][b][:, 0:n], ACT.Abs)
                    e = arena[:, 0:2 * S + 2 * P]
                    act.drain()
                    fn(e, e, ACT.Exp, scale=-1.0)
                    act.drain()
                    fn(e, e, ACT.Ln, bias=1.0).then_inc(log_ready, 1)

                def shares(h):
                    act.wait_ge(suffix_full, at(l, SB_HEADS, h + 1))
                    if h >= 2:
                        act.wait_ge(acc_full, mix_full(l, T_LIN + NHD + h - 1))
                    for b, n in SB_BANKS:
                        m = fn(sb_a[h % 2][:, b, 0:n], sb_bank[h % 2][b][:, 0:n], ACT.Exp)
                    m.then_inc(a_exp, 1)

                def sb_out(h):
                    t = T_LIN + NHD + h
                    act.wait_ge(acc_full, mix_full(l, t + 1))
                    r = slice((h % 2) * HD, (h % 2) * HD + HD)
                    fn(o_T[r, 6 + h // 2, :], acc[t % 2][r, :], ACT.Copy).then_inc(acc_free[t % 2], 1)

                logs(0)
                for h in range(SB_HEADS):
                    if h + 1 < SB_HEADS:
                        logs(h + 1)
                    shares(h)
                    if h >= 1:
                        sb_out(h - 1)
                sb_out(SB_HEADS - 1)

            act.wait_ge(eps_ready, 1)
            with act.Fori(0, DEPTH) as l:
                norm(l * 3, (l, 0))
                slices(l, 0)
                norm(l * 3 + 1, mix=l)
                mix(l)
                norm(l * 3 + 2, (l, 1))
                slices(l, 1)

            act.wait_ge(params_loaded, N_PARAMS)
            norm(3 * L)
            norm(3 * L + 1)
            for n, (name, i, ld) in enumerate(SEC_T):
                if name in ("u", "v", "q", "k", "vtok", "gate"):
                    act.wait_ge(acc_full, full_at(L, 0, full2(n + 1)))
                    ps = acc[n % 2][:, :]
                    if name == "u":
                        m = fn(u_T[:, i, :], ps, ACT.Copy)
                    elif name == "v":
                        b, hf = i % 2, i // 2
                        m = fn(vtok[:, 2 * b:2 * b + 2, hf * 256:(hf + 1) * 256],
                               ps.rearrange("p (a b) -> p a b", b=256), ACT.Copy)
                    elif name == "q":
                        m = fn(q2[:, i, :], ps, ACT.Copy, scale=HD ** -0.5)
                    elif name == "k":
                        m = fn(k2, ps, ACT.Copy)
                    elif name == "vtok":
                        m = fn(v2.rearrange("p a b -> p (a b)"), ps, ACT.Copy)
                    else:
                        m = fn((sig_a if i < 8 else sig_b)[:, i % 8, :], ps, ACT.Exp, scale=-1.0)
                    m.then_inc(acc_free[n % 2], 1)
                if name == "gate":
                    t = (sig_a if i < 8 else sig_b)[:, i % 8, :]
                    act.drain()
                    fn(t, t, ACT.Ln, bias=1.0)
                    act.drain()
                    fn(t, t, ACT.Exp, scale=-1.0)
                if name == "gate" and i < 8:
                    act.wait_ge(gelu_pre, 2 * L + i + 1)
                    fn(probs[:, i % 2, :], probs[:, i % 2, :], ACT.Exp, scale=-2 * GC).then_inc(gelu_exp, 1)
                if name == "gate" and i == 10:
                    act.wait_ge(ln_pre, 1)
                    fn(lnst[:, 2, :], lnst[:, 1, :], ACT.Ln, scale=1.0 / 512, bias=eps[:, :])
                    act.drain()
                    fn(lnst[:, 3, :], lnst[:, 2, :], ACT.Exp, scale=-0.5).then_inc(ln_rstd, 1)
                if (name, i) == ("swa", 0):
                    attend(L, NU, 0, NSW, swa_info, L, 0, SWA0, ab_T[:, 4:8, :], True)
                if name == "route":
                    norm(3 * L + 2)
                    for j in range(2 * TB):
                        act.wait_ge(htok_full, j + 1)
                        fn(h_tok[:, j // 2, (j % 2) * S:(j % 2 + 1) * S], turn[j % 2][:, :], ACT.Copy
                           ).then_inc(htok_ready, 1)
                    act.wait_ge(route_pre, 1)
                    fn(rx[:, 1, :, 0:4], rx[:, 0, :, 0:4], ACT.Exp).then_inc(route_exp, 1)
                    act.wait_ge(route_pre, 2)
                    fn(rx[:, 11, :, 0:1], rx[:, 10, :, 0:1], ACT.Exp).then_inc(route_exp, 1)

            def mine_out(pair, q):
                act.wait_ge(gathered, pair * 2 + q + 1)
                for t in range(2):
                    m = fn(mine_T[q][:, 4 * t:4 * t + 4, :], turn[t][:, :].rearrange("p (c t) -> p c t", t=P), ACT.Copy)
                m.then_inc(mine_ready, 1)

            def step(pair, q, last=False):
                act.wait_ge(xgu_full, pair * 2 + q + 3)
                fn(et[:, 0, :], score[0][:, :], ACT.Exp, scale=-1.0).then_inc(xsig_ready, 1)
                if not last:
                    mine_out(pair + q, 1 - q)
                act.wait_ge(xhid_turned, pair * 2 + q + 1)
                fn(xhid_T, score[0][:, :], ACT.Copy).then_inc(xhidt_ready, 1)
                act.wait_ge(xdown_full, pair * 2 + q + 3)
                for t in range(2):
                    m = fn(y_slot[:, t, :], score[2 + t][:, :], ACT.Copy)
                m.then_inc(yslot_ready, 1)

            act.wait_ge(passes_ready, 1)
            n_p = act.value_load(n_passes[0:1, 0:1], min_val=1, max_val=TB)
            with act.Fori(0, n_p) as ps_:
                pair0 = act.snap(ps_ * (NX // 2))
                mine_out(pair0, 0)
                step(pair0, 0)
                with act.Fori(0, NX // 2 - 1) as i:
                    pair = act.snap(pair0 + i)
                    step(pair, 1)
                    step(pair + 1, 0)
                step(pair0 + (NX // 2 - 1), 1, last=True)
            norm(3 * L + 3)
            for n in range(2 * TB):
                act.wait_ge(yt_full, n + 1)
                fn(y_out[:, n // 2, (n % 2) * S:(n % 2 + 1) * S], turn[n % 2][:, :], ACT.Copy).then_inc(y_ready, 1)

        @block.vector
        def _(dve):
            V = nc.vector

            def norm(k, dest=h_T):
                dve.wait_ge(rstd_ready, k + 1)
                for c in range(KC):
                    V.scalar_tensor_tensor(dest[:, c, :], x_T[:, c, :], gains[:, bass.ds(k, 1), c:c + 1][:, 0, :],
                                           rstd[:, :], ALU.mult, ALU.mult).then_inc(h_ready, 1)
                    if dest is x_T:
                        dve.drain().then_inc(x_final, 1)
                        square_sum(k + 1, c - 1)

            def square_sum(k, c):
                if 1 <= c < KC - 1:
                    dve.wait_ge(squared, k * KC + c + 1)
                    m = V.tensor_tensor(h_T[:, 0, :], h_T[:, 0, :], h_T[:, c, :], ALU.add)
                    if c == KC - 2:
                        m.then_inc(summed, 1)

            def split_weights(l, ph, w, sl, tile=None):
                tile = w if tile is None else tile
                dve.wait_ge(w_hi_ready[w], at(l, 2 * NSL, ph * NSL + sl + 1))
                V.tensor_tensor(w_lo[tile][:, :], slot[w][:, :], w_hi[tile][:, :], ALU.subtract).then_inc(w_split[w], 1)

            def split_mix(l, n):
                dve.wait_ge(mix_w_hi_ready, at(l, N_SPLIT, n + 1))
                w = LOAD_COLS[n]
                V.tensor_tensor(mix_w[n % 2][1][:, 0:w], slot[n % 3][:, 0:w], mix_w[n % 2][0][:, 0:w],
                                ALU.subtract).then_inc(mix_w_split, 1)

            def norm_split(l, ph, k):
                nth = 1 if ph is None else 2 * ph
                hi, lo = mix_h if ph is None else (h_hi, h_lo)

                def low(c):
                    dve.drain()
                    dve.wait_ge(h_hi_ready, at(l, 3 * KC, nth * KC + c + 1))
                    V.tensor_tensor(lo[:, c, :], h_T[:, c, :], hi[:, c, :], ALU.subtract).then_inc(h_split, 1)

                if ph is None:
                    split_mix(l, 0)
                else:
                    split_weights(l, ph, 0, 0)
                dve.wait_ge(rstd_ready, k + 1)
                for c in range(KC):
                    V.scalar_tensor_tensor(h_T[:, c, :], x_T[:, c, :], gains[:, bass.ds(k, 1), c:c + 1][:, 0, :],
                                           rstd[:, :], ALU.mult, ALU.mult).then_inc(h_ready, 1)
                    if c >= 1:
                        low(c - 1)
                low(KC - 1)
                if ph is None:
                    split_mix(l, 1)

            def slices(l, ph, k):
                base, gub = (F1, F2)[ph], ph * 2 * NSL

                def gate(sl):
                    for c in range(2):
                        dve.wait_ge(sig_ready, at(l, TG, gub + sl * 2 + c + 1))
                        V.tensor_scalar(et[:, c, :], et[:, c, :], 1.0, None, ALU.add)
                        dve.drain()
                        V.reciprocal(rt[:, :], et[:, c, :])
                        dve.drain()
                        m = V.tensor_tensor(et[:, c, :], rt[:, :], score[c][:, :], ALU.mult)
                    m.then_inc(gate_taken, 1)

                def hidden(sl, par):
                    dve.drain()
                    dve.wait_ge(gu_full, gu_at(l, gub, sl * 2 + 2))
                    for c in range(2):
                        V.tensor_tensor(et[:, c, :], et[:, c, :], score[2 + c][:, :], ALU.mult)
                    dve.drain()
                    V.tensor_copy(hid_hi[:, 2 * par:2 * par + 2, :], et[:, :, :])
                    dve.drain()
                    V.tensor_tensor(hid_lo[:, 2 * par:2 * par + 2, :], et[:, :, :],
                                    hid_hi[:, 2 * par:2 * par + 2, :], ALU.subtract).then_inc(hid_done, 2)

                def down(sl, last=False, chunks=range(KC)):
                    for c in chunks:
                        dve.wait_ge(acc_full, full_at(l, base, sl * KC + c + 1))
                        V.scalar_tensor_tensor(x_T[:, c, :], acc[c % 2][:, :], 0.5, x_T[:, c, :],
                                               ALU.mult, ALU.add).then_inc(acc_free[c % 2], 1)
                        if last:
                            dve.drain().then_inc(x_final, 1)
                            square_sum(k, c - 1)

                def step(sl, par):
                    split_weights(l, ph, 0, sl)
                    if not isinstance(sl, int) or sl >= 2:
                        down(sl - 2)
                    hidden(sl - 1, 1 - par)
                    split_weights(l, ph, 1, sl)
                    split_weights(l, ph, 2, sl - 1)
                    gate(sl)

                split_weights(l, ph, 1, 0)
                gate(0)
                step(1, 1)
                with dve.Fori(0, (NSL - 3) // 2) as i:
                    step(i * 2 + 2, 0)
                    step(i * 2 + 3, 1)
                step(NSL - 1, 0)
                split_weights(l, ph, 2, NSL - 1, tile=0)
                down(NSL - 2, chunks=range(KC // 2))
                hidden(NSL - 1, 0)
                down(NSL - 2, chunks=range(KC // 2, KC))
                down(NSL - 1, True)

            def attend(l, per, u0, n_units, info, sink):
                def maxima(n):
                    u = info(n)
                    w, st, i = u["w"], n % 4, u["i"]
                    ps = score[st]
                    dve.wait_ge(s_full, at(l, per, u0 + n + 1))
                    if sink:
                        if n >= 3:
                            dve.wait_ge(t_full, at(l, per, u0 + n - 2))
                        pr = probs[:, n % 3, 0:w]
                        V.tensor_tensor(pr, ps[:, 0:w], bias_t[:, u["h"], 256 - w:256], ALU.add)
                        dve.drain()
                        V.tensor_reduce(stats[:, 2, st:st + 1], pr, AX.X, ALU.max)
                        dve.drain()
                        V.tensor_scalar(stats[:, 0, st:st + 1], stats[:, 2, st:st + 1],
                                        sinks[:, u["h"]:u["h"] + 1], -1.0, ALU.max, ALU.mult
                                        ).then_inc(max_ready, 1)
                        return
                    if u["br"] == "cmp":
                        V.tensor_tensor(ps[:, 0:31], ps[:, 0:31], cst("cmp_mask", lo=i * 31, hi=i * 31 + 31), ALU.add)
                    else:
                        V.tensor_tensor(ps[:, i * P:w], ps[:, i * P:w], cst("causal"), ALU.add)
                    dve.drain()
                    V.tensor_reduce(stats[:, 0, st:st + 1], ps[:, 0:w], AX.X, ALU.max, negate=True
                                    ).then_inc(max_ready, 1)

                def normalize(n):
                    u = info(n)
                    w, st = u["w"], n % 4
                    dve.wait_ge(exp_ready, at(l, per, u0 + n + 1))
                    if sink:
                        V.tensor_tensor(stats[:, 1, st:st + 1], stats[:, 1, st:st + 1], stats[:, 3, st:st + 1], ALU.add)
                        dve.drain()
                    V.reciprocal(stats[:, 2, st:st + 1], stats[:, 1, st:st + 1])
                    dve.drain()
                    pr = probs[:, n % 3, 0:w]
                    if u["br"] in ("cmp", "sel", "win"):
                        g = u["h"] * 3 + ("cmp", "sel", "win").index(u["br"])
                        V.tensor_scalar(pr, pr, stats[:, 2, st:st + 1], gates[:, u["i"], g:g + 1],
                                        ALU.mult, ALU.mult).then_inc(p_ready, 1)
                    else:
                        V.tensor_scalar(pr, pr, stats[:, 2, st:st + 1], None, ALU.mult).then_inc(p_ready, 1)

                maxima(0)
                for n in range(n_units):
                    if n + 1 < n_units:
                        maxima(n + 1)
                    normalize(n)

            def gelu_pre_ops(x, t):
                dve.drain()
                V.tensor_tensor(t, x, x, ALU.mult)
                dve.drain()
                V.tensor_scalar(t, t, 0.044715, 1.0, ALU.mult, ALU.add)
                dve.drain()
                V.tensor_tensor(t, t, x, ALU.mult)
                dve.drain()
                V.tensor_scalar(t, t, -54.0, None, ALU.max).then_inc(gelu_pre, 1)

            def mix(l):
                def compressed(kv, nth):
                    ps = turn[kv]
                    dve.drain()
                    dve.wait_ge(hidc_full, at(l, 2, nth))
                    V.tensor_copy(bias_c[:, kv:kv + 1], ps[:, 62:63])
                    dve.drain()
                    V.tensor_scalar(cmp_t[:, 0, :], ps[:, 0:62], bias_c[:, kv:kv + 1], None, ALU.add)
                    dve.drain()
                    gelu_pre_ops(cmp_t[:, 0, :], cmp_t[:, 1, :])
                    dve.wait_ge(gelu_exp, at(l, 2, nth))
                    V.tensor_scalar(cmp_t[:, 2, :], cmp_t[:, 2, :], 1.0, None, ALU.add)
                    dve.drain()
                    V.reciprocal(cmp_t[:, 3, :], cmp_t[:, 2, :])
                    dve.drain()
                    V.tensor_tensor(hid_cmp[:, kv, :], cmp_t[:, 0, :], cmp_t[:, 3, :], ALU.mult
                                    ).then_inc(hidc_ready, 1)

                n_rope = 0
                for n, (name, i, ld, who) in enumerate(MIX):
                    ps = acc[n % 2]
                    if who == "dve":
                        dve.drain()
                        dve.wait_ge(acc_full, mix_full(l, n + 1))
                    if name == "gate":
                        V.tensor_tensor(gates[:, :, :], ps[:, 0:72].rearrange("p (b g) -> p b g", g=18),
                                        gbias[:, bass.ds(l, 1), :].broadcast_to([P, TB, 18]), ALU.add
                                        ).then_inc(acc_free[n % 2], 1)
                        dve.wait_ge(gate_exp, l + 1)
                        V.tensor_scalar(gates_e[:, :, :], gates_e[:, :, :], 1.0, None, ALU.add)
                        dve.drain()
                        V.reciprocal(gates[:, :, :], gates_e[:, :, :])
                        dve.drain()
                        g3 = gates.rearrange("p b (h r) -> p b h r", r=3)[:, :, :, 0]
                        V.tensor_tensor(g3, g3, cst("cmp_valid").unsqueeze(2).broadcast_to([P, TB, 6]), ALU.mult)
                        dve.wait_ge(lrstd_ready, l + 1)
                        for c in range(3):
                            m = V.scalar_tensor_tensor(lora[:, c, :], lora[:, c, :],
                                                       lgains[:, bass.ds(l, 1), c:c + 1][:, 0, :],
                                                       et[:, c // 2, :], ALU.mult, ALU.mult)
                        m.then_inc(lora_ready, 1)
                    elif name == "rope":
                        t, kind, _ = ROPES[i]
                        r = t.shape[0]
                        V.tensor_tensor(rt[0:r, :], ps[0:r, :], cst("sin_" + kind, rows=r), ALU.mult
                                        ).then_inc(acc_free[n % 2], 1)
                        V.tensor_tensor(t, t, cst("cos_" + kind, rows=r), ALU.mult)
                        dve.drain()
                        if i == 6:
                            V.tensor_tensor(k6[HD:96, :, :], t[HD:96, :].unsqueeze(1).broadcast_to([32, 6, S]),
                                            rt[HD:96, :].unsqueeze(1).broadcast_to([32, 6, S]), ALU.add
                                            ).then_inc(rope_ready, 1)
                        else:
                            V.tensor_tensor(t, t, rt[0:r, :], ALU.add).then_inc(rope_ready, 1)
                        n_rope += 1
                        if n_rope == V_ROPES[1] + 1:
                            compressed(1, 1)
                        if n_rope == N_ROPE:
                            compressed(0, 2)
                    if ld is not None and ld + 2 < N_SPLIT and LAST_TICKET[ld] == n:
                        split_mix(l, ld + 2)
                attend(l, NU, 0, NU, unit_info, False)
                def strictly(m_op):
                    m_op(lambda t: t[:, 0:3, 0:P], cst("strict").unsqueeze(1).broadcast_to([P, 3, P]))
                    return m_op(lambda t: t[:, 1, P:2 * P], cst("strict"))

                def softplus(h):
                    dve.drain()
                    dve.wait_ge(log_ready, at(l, SB_HEADS, h + 1))
                    if h >= 1:
                        dve.wait_ge(suffix_full, at(l, SB_HEADS, h))
                    for b, n in SB_BANKS:
                        V.scalar_tensor_tensor(hid[:, b, 0:n], sb_bank[h % 2][b][:, 0:n], 0.0, sb_e[:, b, 0:n],
                                               ALU.max, ALU.add)
                    dve.drain()
                    strictly(lambda f, mask: V.tensor_tensor(f(hid), f(hid), mask, ALU.mult)).then_inc(sp_ready, 1)

                def mask_shares(h):
                    dve.wait_ge(a_exp, at(l, SB_HEADS, h + 1))
                    t = sb_a[h % 2]
                    strictly(lambda f, mask: V.scalar_tensor_tensor(f(t), f(t), 1.0, mask, ALU.min, ALU.mult)
                             ).then_inc(a_ready, 1)

                softplus(0)
                for h in range(SB_HEADS):
                    if h + 1 < SB_HEADS:
                        softplus(h + 1)
                    mask_shares(h)
                for c in range(KC):
                    dve.wait_ge(acc_full, mix_full(l, T_HEAD + c + 1))
                    V.tensor_tensor(x_T[:, c, :], acc[(T_HEAD + c) % 2][:, :], x_T[:, c, :], ALU.add
                                    ).then_inc(acc_free[(T_HEAD + c) % 2], 1)
                    dve.drain().then_inc(x_final, 1)
                    square_sum(l * 3 + 2, c - 1)

            def first_max(x, top, hit, desc, n, best, out_):
                V.tensor_reduce(rx[:, 12, :, top:top + 1], x, AX.X, ALU.max)
                dve.drain()
                V.tensor_tensor(hit, x, rx[:, 12, :, top:top + 1].broadcast_to([P, TB, n]), ALU.is_equal)
                dve.drain()
                V.tensor_tensor(hit, hit, cst(desc).unsqueeze(1).broadcast_to([P, TB, n]), ALU.mult)
                dve.drain()
                V.tensor_reduce(rx[:, 12, :, best:best + 1], hit, AX.X, ALU.max)
                dve.drain()
                V.tensor_tensor(out_, hit, rx[:, 12, :, best:best + 1].broadcast_to([P, TB, n]), ALU.is_equal)
                dve.drain()

            def route(n, ps):
                V.tensor_tensor(lg[:, :, :], ps[:, 0:80].rearrange("p (b g) -> p b g", g=20),
                                rb[:, :].unsqueeze(1).broadcast_to([P, TB, 20]), ALU.add
                                ).then_inc(acc_free[n % 2], 1)
                dve.drain()
                gl = lg[:, :, 0:4]
                first_max(gl, 0, rx[:, 2, :, 0:4], "desc4", 4, 1, rx[:, 3, :, 0:4])
                V.tensor_tensor(rx[:, 0, :, 0:4], gl, rx[:, 12, :, 0:1].broadcast_to([P, TB, 4]), ALU.subtract
                                ).then_inc(route_pre, 1)
                V.tensor_scalar(rx[:, 4, :, 0:4], rx[:, 3, :, 0:4], -NEG, NEG, ALU.mult, ALU.add)
                dve.drain()
                V.tensor_tensor(rx[:, 5, :, :].rearrange("p b (g e) -> p b g e", e=4),
                                lg[:, :, 4:20].rearrange("p b (g e) -> p b g e", e=4),
                                rx[:, 4, :, 0:4].unsqueeze(3).broadcast_to([P, TB, 4, 4]), ALU.add)
                dve.drain()
                first_max(rx[:, 5, :, :], 2, rx[:, 6, :, :], "desc16", 16, 3, rx[:, 7, :, :])
                V.tensor_scalar(rx[:, 8, :, :], rx[:, 7, :, :], NEG, None, ALU.mult)
                dve.drain()
                V.tensor_tensor(rx[:, 8, :, :], rx[:, 8, :, :], rx[:, 5, :, :], ALU.add)
                dve.drain()
                first_max(rx[:, 8, :, :], 4, rx[:, 6, :, :], "desc16", 16, 5, rx[:, 9, :, :])
                V.tensor_tensor(member[:, :, :], rx[:, 7, :, :], rx[:, 9, :, :], ALU.add).then_inc(member_ready, 1)
                V.tensor_tensor(rx[:, 10, :, 0:1], rx[:, 12, :, 4:5], rx[:, 12, :, 2:3], ALU.subtract
                                ).then_inc(route_pre, 1)
                dve.wait_ge(route_exp, 1)
                V.tensor_reduce(rx[:, 12, :, 6:7], rx[:, 1, :, 0:4], AX.X, ALU.add)
                dve.wait_ge(route_exp, 2)
                V.tensor_scalar(rx[:, 12, :, 7:8], rx[:, 11, :, 0:1], 1.0, None, ALU.add)
                dve.drain()
                V.tensor_tensor(rx[:, 12, :, 7:8], rx[:, 12, :, 7:8], rx[:, 12, :, 6:7], ALU.mult)
                dve.drain()
                V.reciprocal(rx[:, 12, :, 8:9], rx[:, 12, :, 7:8])
                dve.drain()
                V.tensor_tensor(rx[:, 12, :, 9:10], rx[:, 12, :, 8:9], rx[:, 11, :, 0:1], ALU.mult)
                dve.drain()
                V.tensor_tensor(rx[:, 6, :, :], rx[:, 7, :, :], rx[:, 12, :, 8:9].broadcast_to([P, TB, 16]), ALU.mult)
                V.tensor_tensor(rx[:, 8, :, :], rx[:, 9, :, :], rx[:, 12, :, 9:10].broadcast_to([P, TB, 16]), ALU.mult)
                dve.drain()
                V.tensor_tensor(comb[:, :, :], rx[:, 6, :, :], rx[:, 8, :, :], ALU.add).then_inc(comb_done, 1)

            V.memset(eps[:, :], EPS).then_inc(eps_ready, 1)
            for c in range(KC):
                dve.wait_ge(xt_full, c + 1)
                V.tensor_copy(x_T[:, c, :], turn[c % 2][:, :]).then_inc(x_final, 1)
                dve.drain()
                square_sum(0, c - 1)
            dve.wait_ge(x_loaded, 32)
            dve.wait_ge(params_loaded, N_PARAMS)
            with dve.Fori(0, DEPTH) as l:
                norm_split(l, 0, l * 3)
                slices(l, 0, l * 3 + 1)
                norm_split(l, None, l * 3 + 1)
                mix(l)
                norm_split(l, 1, l * 3 + 2)
                slices(l, 1, l * 3 + 3)

            norm(3 * L, x_T)
            norm(3 * L + 1)
            dve.wait_ge(rel_full, 1)
            V.tensor_tensor(rrow, turn[0][0:8, 0:384], cst("window_row", rows=8), ALU.add).then_inc(relrow_ready, 1)
            taken(dve, L, 0, T2["v", 3])
            taken(dve, L, 0, T2["v", 2])
            gx = [u_T[:, c, :] for c in range(4)] + [vtok[:, b, :] for b in range(TB)]
            gelu_pre_ops(gx[0], probs[:, 0, :])
            for j in range(8):
                t = probs[:, j % 2, :]
                if j + 1 < 8:
                    gelu_pre_ops(gx[j + 1], probs[:, (j + 1) % 2, :])
                dve.wait_ge(gelu_exp, 2 * L + j + 1)
                V.tensor_scalar(t, t, 1.0, None, ALU.add)
                dve.drain()
                V.reciprocal(t, t)
                dve.drain()
                V.tensor_tensor(gx[j], gx[j], t, ALU.mult)
            dve.drain()
            for b in range(TB):
                V.tensor_reduce(lnst[:, 0, b:b + 1], vtok[:, b, :], AX.X, ALU.add)
            dve.drain()
            V.tensor_scalar(lnst[:, 0, :], lnst[:, 0, :], 1.0 / 512, None, ALU.mult)
            dve.drain()
            for b in range(TB):
                V.tensor_scalar(vtok[:, b, :], vtok[:, b, :], lnst[:, 0, b:b + 1], None, ALU.subtract)
            dve.drain()
            for b in range(TB):
                dve.drain()
                V.tensor_tensor(probs[:, 0, :], vtok[:, b, :], vtok[:, b, :], ALU.mult)
                dve.drain()
                m = V.tensor_reduce(lnst[:, 1, b:b + 1], probs[:, 0, :], AX.X, ALU.add)
            m.then_inc(ln_pre, 1)
            dve.wait_ge(ln_rstd, 1)
            dve.wait_ge(ws_loaded, 32)
            for b in range(TB):
                m = V.scalar_tensor_tensor(vtok[:, b, :], vtok[:, b, :], lnst[:, 3, b:b + 1], gv, ALU.mult, ALU.mult)
            m.then_inc(vn_ready, 1)
            for n, (name, i, ld) in enumerate(SEC_T):
                ps = acc[n % 2]
                if name in ("wst", "sv", "pa", "pb", "wo", "route", "rank", "combt", "rankt"):
                    dve.wait_ge(acc_full, full_at(L, 0, full2(n + 1)))
                if name == "wst":
                    V.tensor_tensor(ws_T[:, 4 * i:4 * i + 4, :], ps[:, :].rearrange("p (g t) -> p g t", t=P),
                                    cst("tril").unsqueeze(1).broadcast_to([P, 4, P]), ALU.mult
                                    ).then_inc(acc_free[n % 2], 1)
                elif name == "sv":
                    V.tensor_tensor(ab_T[:, i, :], ps[:, :], u_T[:, i, :], ALU.mult).then_inc(acc_free[n % 2], 1)
                elif (name, i) == ("swa", 0):
                    dve.wait_ge(bias_loaded, 16)
                    attend(L, NU, 0, NSW, swa_info, True)
                elif name == "pa":
                    V.tensor_tensor(sig_a[:, i, :], ps[:, :], sig_a[:, i, :], ALU.mult).then_inc(acc_free[n % 2], 1)
                elif name == "pb":
                    dve.drain()
                    V.tensor_tensor(rt[:, :], ps[:, :], sig_b[:, i, :], ALU.mult).then_inc(acc_free[n % 2], 1)
                    dve.drain()
                    V.tensor_tensor(sig_a[:, i, :], sig_a[:, i, :], rt[:, :], ALU.add).then_inc(merged_ready, 1)
                elif name == "wo":
                    V.tensor_tensor(x_T[:, i, :], ps[:, :], x_T[:, i, :], ALU.add).then_inc(acc_free[n % 2], 1)
                    dve.drain().then_inc(x_final, 1)
                    square_sum(3 * L + 2, i - 1)
                    if i == KC - 1:
                        norm(3 * L + 2)
                elif name == "route":
                    route(n, ps)
                elif name == "rank":
                    V.tensor_scalar(rank[:, :, :], member[:, :, :], -4.0 * S, 4.0 * S, ALU.mult, ALU.add)
                    V.tensor_reduce(passes[:, 0:1], ps[:, 64:80], AX.X, ALU.max)
                    dve.drain()
                    V.tensor_tensor(rank[:, :, :], rank[:, :, :], ps[:, 0:64].rearrange("p (b e) -> p b e", e=16),
                                    ALU.add).then_inc(acc_free[n % 2], 1)
                    dve.drain().then_inc(rank_ready, 1)
                    V.tensor_scalar(passes[:, 1:2], passes[:, 0:1], float(P), 1.0, ALU.is_gt, ALU.add)
                    for j in range(2, TB):
                        dve.drain()
                        V.scalar_tensor_tensor(passes[:, 1:2], passes[:, 0:1], float(j * P), passes[:, 1:2],
                                               ALU.is_gt, ALU.add)
                    dve.drain()
                    V.tensor_copy(n_passes[:, :], passes[:, 1:2]).then_inc(passes_ready, 1)
                elif name in ("combt", "rankt"):
                    V.tensor_copy(rows_T[:, 0 if name == "combt" else 1, :], ps[0:16, :]).then_inc(acc_free[n % 2], 1)

            def choose(e, p_, q):
                V.tensor_tensor(pick[q], cst("iota").rearrange("p (a t) -> p a t", t=P)[:, bass.ds(p_, 1), :]
                                .broadcast_to([P, TB, P]),
                                rank[:, :, bass.ds(e, 1)].broadcast_to([P, TB, P]), ALU.is_equal
                                ).then_inc(pick_ready, 1)

            def take(pair, q):
                for c in range(KC):
                    dve.wait_ge(scattered, pair * 16 + 8 * q + c + 1)
                    V.tensor_tensor(x_T[:, c, :], acc[c % 2][:, :], x_T[:, c, :], ALU.add
                                    ).then_inc(scatter_taken, 1)

            def step(pair, q, e, p_, first=False, last=False):
                if not last:
                    choose(e + 1, p_, 1 - q)
                dve.wait_ge(xsig_ready, pair * 2 + q + 1)
                V.tensor_scalar(et[:, 0, :], et[:, 0, :], 1.0, None, ALU.add)
                dve.drain()
                V.reciprocal(rt[:, :], et[:, 0, :])
                dve.drain()
                V.tensor_tensor(rt[:, :], rt[:, :], score[0][:, :], ALU.mult)
                dve.drain()
                V.tensor_tensor(xhid, rt[:, :], score[1][:, :], ALU.mult).then_inc(xhid_ready, 1)
                dve.wait_ge(rows_loaded[q], pair * 16 + 16)
                V.scalar_tensor_tensor(place[q], rows[q][:, 1, :], cst("slot_number")[:, bass.ds(p_, 1)],
                                       rows[q][:, 0, :], ALU.is_equal, ALU.mult).then_inc(place_ready, 1)
                if not first:
                    take(pair - 1 + q, 1 - q)

            dve.drain()
            n_p = dve.value_load(n_passes[0:1, 0:1], min_val=1, max_val=TB)
            with dve.Fori(0, n_p) as ps_:
                pair0 = dve.snap(ps_ * (NX // 2))
                choose(0, ps_, 0)
                step(pair0, 0, 0, ps_, first=True)
                with dve.Fori(0, NX // 2 - 1) as i:
                    pair = dve.snap(pair0 + i)
                    step(pair, 1, i * 2 + 1, ps_)
                    step(pair + 1, 0, i * 2 + 2, ps_)
                step(pair0 + (NX // 2 - 1), 1, NX - 1, ps_, last=True)
                take(pair0 + (NX // 2 - 1), 1)
            dve.drain().then_inc(x_final, KC)
            for c in range(KC):
                dve.drain()
                square_sum(3 * L + 3, c)
            norm(3 * L + 3)



def kernel(**inputs):
    import concourse.bacc as bacc
    from concourse.bass_utils import run_bass_kernel_spmd as run

    nc = bacc.Bacc("TRN2", target_bir_lowering=False, num_devices=1)
    arrays, args = {}, {}
    tensors = {**inputs, "const": constant_table()}
    for name, value in tensors.items():
        v = np.ascontiguousarray(value)
        arrays[f"in_{name}"] = v
        args[name] = nc.dram_tensor(f"in_{name}", v.shape, mybir.dt.from_np(v.dtype), kind="ExternalInput").ap()
    out = nc.dram_tensor("out", (1, S, D), F32, kind="ExternalOutput").ap()
    build(nc, args, out)
    r = run(nc, [arrays], core_ids=[0])
    return r.results[0]["out"]
```
